# Optimizing a Trainium2 kernel written in Bass

```python
import jax, jax.numpy as jnp
from jax import lax
import numpy as np

D_MODEL = 1024
BATCH = 1
SEQ = 256
DEPTH = 1

RET_HEADS = 8
RET_HEAD_DIM = 64
RET_WIDTH = RET_HEADS * RET_HEAD_DIM
RET_CHUNK = 128
MLA_HEADS = 8
MLA_NOPE_DIM = 64
MLA_ROPE_DIM = 32
MLA_V_DIM = 64
MLA_Q_RANK = 256
MLA_KV_RANK = 128
MLA_WIDTH = MLA_HEADS * MLA_V_DIM
MIX_WIDTH = RET_WIDTH + MLA_WIDTH
IN_WIDTH = 4 * RET_WIDTH + MLA_Q_RANK + MLA_KV_RANK + MLA_ROPE_DIM
D_FF = 2816
CONV_WIDTH = 3
Q_BLOCK = 128
ROPE_BASE = 10000.0
EPS = 1e-6


def rms_norm(x, w):
    xf = x.astype(jnp.float32)
    y = xf * lax.rsqrt(jnp.mean(xf * xf, axis=-1, keepdims=True) + EPS)
    return (y * w.astype(jnp.float32)).astype(x.dtype)

def rope(x, positions):
    d = x.shape[-1]
    inv_freq = ROPE_BASE ** (-jnp.arange(0, d, 2, dtype=jnp.float32) / d)
    ang = positions.astype(jnp.float32)[..., None] * inv_freq
    if x.ndim == 4:
        ang = ang[:, :, None, :]
    cos, sin = jnp.cos(ang), jnp.sin(ang)
    xf = x.astype(jnp.float32)
    x1, x2 = xf[..., : d // 2], xf[..., d // 2:]
    return jnp.concatenate([x1 * cos - x2 * sin, x1 * sin + x2 * cos], axis=-1).astype(x.dtype)

def retention(q, k, v):
    B, S, H, dk = q.shape
    dv = v.shape[-1]
    C = RET_CHUNK
    N = S // C
    log_gamma = jnp.log1p(-jnp.power(2.0, -5.0 - jnp.arange(H, dtype=jnp.float32)))
    qc = q.astype(jnp.float32).reshape(B, N, C, H, dk)
    kc = k.astype(jnp.float32).reshape(B, N, C, H, dk)
    vc = v.astype(jnp.float32).reshape(B, N, C, H, dv)
    idx = jnp.arange(C, dtype=jnp.float32)
    diff = idx[:, None] - idx[None, :]
    decay_mask = jnp.where(diff >= 0, jnp.exp(log_gamma[:, None, None] * jnp.maximum(diff, 0.0)), 0.0)
    scores = jnp.einsum('bnihd,bnjhd->bnhij', qc, kc) * decay_mask
    o_inner = jnp.einsum('bnhij,bnjhe->bnihe', scores, vc)
    zeta = jnp.exp(log_gamma[:, None] * (C - 1.0 - idx))
    chunk_states = jnp.einsum('bnjhd,hj,bnjhe->nbhde', kc, zeta, vc)
    chunk_decay = jnp.exp(log_gamma * C)[None, :, None, None]

    def step(R, s_n):
        return chunk_decay * R + s_n, R

    _, r_prev = lax.scan(step, jnp.zeros((B, H, dk, dv), jnp.float32), chunk_states)
    r_prev = jnp.moveaxis(r_prev, 0, 1)
    xi = jnp.exp(log_gamma[:, None] * (idx + 1.0))
    o_cross = jnp.einsum('bnihd,bnhde,hi->bnihe', qc, r_prev, xi)
    return (o_inner + o_cross).reshape(B, S, H, dv)

def retention_group(q, k, v, g, positions, gn_w):
    B, S, _ = q.shape
    q = rope(q.reshape(B, S, RET_HEADS, RET_HEAD_DIM), positions)
    k = rope(k.reshape(B, S, RET_HEADS, RET_HEAD_DIM), positions) * (RET_HEAD_DIM ** -0.5)
    v = v.reshape(B, S, RET_HEADS, RET_HEAD_DIM)
    o = retention(q, k, v)
    mu = jnp.mean(o, axis=-1, keepdims=True)
    var = jnp.mean(jnp.square(o - mu), axis=-1, keepdims=True)
    o = ((o - mu) * lax.rsqrt(var + EPS)).reshape(B, S, RET_WIDTH) * gn_w.astype(jnp.float32)
    return (jax.nn.silu(g.astype(jnp.float32)) * o).astype(g.dtype)

def mla_group(c_q, c_kv, k_pe, positions, q_norm_w, w_uq, kv_norm_w, w_ukv):
    B, S, _ = c_q.shape
    H = MLA_HEADS
    q = jnp.einsum('bsr,rf->bsf', rms_norm(c_q, q_norm_w), w_uq).reshape(B, S, H, MLA_NOPE_DIM + MLA_ROPE_DIM)
    q_nope = q[..., :MLA_NOPE_DIM]
    q_pe = rope(q[..., MLA_NOPE_DIM:], positions)
    kv = jnp.einsum('bsr,rf->bsf', rms_norm(c_kv, kv_norm_w), w_ukv).reshape(B, S, H, MLA_NOPE_DIM + MLA_V_DIM)
    k_nope = kv[..., :MLA_NOPE_DIM]
    v = kv[..., MLA_NOPE_DIM:]
    k_pe = rope(k_pe, positions)
    scale = (MLA_NOPE_DIM + MLA_ROPE_DIM) ** -0.5
    N = S // Q_BLOCK
    qn_b = jnp.moveaxis(q_nope.reshape(B, N, Q_BLOCK, H, MLA_NOPE_DIM), 1, 0)
    qp_b = jnp.moveaxis(q_pe.reshape(B, N, Q_BLOCK, H, MLA_ROPE_DIM), 1, 0)
    key_pos = jnp.arange(S)
    neg = jnp.finfo(jnp.float32).min

    def block(args):
        qn, qp, blk = args
        s = (jnp.einsum('bqhd,bkhd->bhqk', qn, k_nope)
             + jnp.einsum('bqhr,bkr->bhqk', qp, k_pe)).astype(jnp.float32) * scale
        q_pos = blk * Q_BLOCK + jnp.arange(Q_BLOCK)
        s = jnp.where(key_pos[None, :] <= q_pos[:, None], s, neg)
        p = jax.nn.softmax(s, axis=-1).astype(v.dtype)
        return jnp.einsum('bhqk,bkhd->bqhd', p, v)

    o = lax.map(block, (qn_b, qp_b, jnp.arange(N)))
    return jnp.moveaxis(o, 0, 1).reshape(B, S, MLA_WIDTH)

def conv_ffn(h, w_up, conv_w, conv_b, w_down):
    S = h.shape[1]
    u = jnp.einsum('bsd,df->bsf', h, w_up)
    up = jnp.pad(u, ((0, 0), (CONV_WIDTH - 1, 0), (0, 0)))
    u = conv_b + sum(conv_w[j] * up[:, j:j + S] for j in range(CONV_WIDTH))
    gate, val = u[..., :D_FF], u[..., D_FF:]
    return jnp.einsum('bsf,fd->bsd', jax.nn.silu(gate) * val, w_down)

def first_inputs(seed: int = 0) -> dict:
    key = jax.random.key(seed)
    ks = jax.random.split(key, 20)
    f32 = jnp.float32

    def nrm(k, shape, fan_in):
        return jax.random.normal(k, shape, f32) * (fan_in ** -0.5)

    def gain(k, shape):
        return 1.0 + 0.02 * jax.random.normal(k, shape, f32)

    x = jax.random.normal(ks[0], (BATCH, SEQ, D_MODEL), f32)
    offset = jax.random.randint(ks[1], (BATCH, 1), 0, 4096, dtype=jnp.int32)
    positions = (offset + jnp.arange(SEQ, dtype=jnp.int32)[None, :]).astype(jnp.int32)
    return {
        "x": x,
        "positions": positions,
        "attn_norm_w": gain(ks[2], (DEPTH, D_MODEL)),
        "w_in": nrm(ks[3], (DEPTH, D_MODEL, IN_WIDTH), D_MODEL),
        "ret_gn_w": gain(ks[4], (DEPTH, RET_WIDTH)),
        "mla_q_norm_w": gain(ks[5], (DEPTH, MLA_Q_RANK)),
        "w_uq": nrm(ks[6], (DEPTH, MLA_Q_RANK, MLA_HEADS * (MLA_NOPE_DIM + MLA_ROPE_DIM)), MLA_Q_RANK),
        "mla_kv_norm_w": gain(ks[7], (DEPTH, MLA_KV_RANK)),
        "w_ukv": nrm(ks[8], (DEPTH, MLA_KV_RANK, MLA_HEADS * (MLA_NOPE_DIM + MLA_V_DIM)), MLA_KV_RANK),
        "w_out": nrm(ks[9], (DEPTH, MIX_WIDTH, D_MODEL), MIX_WIDTH),
        "ffn_norm_w": gain(ks[10], (DEPTH, D_MODEL)),
        "w_up": nrm(ks[11], (DEPTH, D_MODEL, 2 * D_FF), D_MODEL),
        "conv_w": nrm(ks[12], (DEPTH, CONV_WIDTH, 2 * D_FF), CONV_WIDTH),
        "conv_b": 0.01 * jax.random.normal(ks[13], (DEPTH, 2 * D_FF), f32),
        "w_down": nrm(ks[14], (DEPTH, D_FF, D_MODEL), D_FF),
        "final_norm_w": gain(ks[15], (D_MODEL,)),
    }

def first_block(x, positions, attn_norm_w, w_in, ret_gn_w, mla_q_norm_w, w_uq, mla_kv_norm_w, w_ukv,
              w_out, ffn_norm_w, w_up, conv_w, conv_b, w_down, final_norm_w):
    splits = np.cumsum([RET_WIDTH, RET_WIDTH, RET_WIDTH, RET_WIDTH, MLA_Q_RANK, MLA_KV_RANK]).tolist()
    for l in range(DEPTH):
        h = rms_norm(x, attn_norm_w[l])
        proj = jnp.einsum('bsd,df->bsf', h, w_in[l])
        r_q, r_k, r_v, r_g, c_q, c_kv, k_pe = jnp.split(proj, splits, axis=-1)
        y_ret = retention_group(r_q, r_k, r_v, r_g, positions, ret_gn_w[l])
        y_mla = mla_group(c_q, c_kv, k_pe, positions, mla_q_norm_w[l], w_uq[l],
                          mla_kv_norm_w[l], w_ukv[l])
        mixed = jnp.concatenate([y_ret, y_mla.astype(y_ret.dtype)], axis=-1)
        x = x + jnp.einsum('bsm,md->bsd', mixed, w_out[l])
        x = x + conv_ffn(rms_norm(x, ffn_norm_w[l]), w_up[l], conv_w[l], conv_b[l], w_down[l])
    return rms_norm(x, final_norm_w)


ATTN_GROUPS = ((128, 1), (512, 4), (2048, 16))
ATTN_HEADS_PER_GROUP = 8
ATTN_HEAD_DIM = 64
ATTN_BLOCK = 128
N_ATTN_HEADS = len(ATTN_GROUPS) * ATTN_HEADS_PER_GROUP
ATTN_QKV_WIDTH = 3 * N_ATTN_HEADS * ATTN_HEAD_DIM
ATTN_OUT = ATTN_HEADS_PER_GROUP * ATTN_HEAD_DIM

GLA_HEADS = 4
GLA_DK = D_MODEL // 2
GLA_DV = D_MODEL
GLA_HK = GLA_DK // GLA_HEADS
GLA_HV = GLA_DV // GLA_HEADS
GLA_GATE_RANK = 16
GLA_TAU = 16.0
GLA_CHUNK = 64

D_FF_2 = 4 * D_MODEL

N_BRANCHES = 2

_IN_SIZES = (ATTN_QKV_WIDTH, GLA_DK, GLA_DK, GLA_DV, GLA_DV, GLA_GATE_RANK, N_BRANCHES * D_MODEL)
D_IN = sum(_IN_SIZES)
_IN_OFFSETS = tuple(int(v) for v in np.cumsum(_IN_SIZES)[:-1])


def rms_norm_2(x, g):
    xf = x.astype(jnp.float32)
    y = xf * lax.rsqrt(jnp.mean(jnp.square(xf), axis=-1, keepdims=True) + EPS)
    return (y * g.astype(jnp.float32)).astype(x.dtype)

def _dilated_group(q, k, v, window, dilation):
    b, s, h, e = q.shape
    n_back = window // dilation
    blk = ATTN_BLOCK
    assert n_back <= blk
    seg = dilation * blk
    s_pad = -(-s // seg) * seg
    L = s_pad // dilation
    nb = L // blk

    def to_blocks(t):
        t = jnp.pad(t, ((0, 0), (0, s_pad - s), (0, 0), (0, 0)))
        t = t.reshape(b, L, dilation, h, e).transpose(0, 2, 3, 1, 4)
        return t.reshape(b, dilation, h, nb, blk, e)

    def with_prev(t):
        prev = jnp.pad(t[:, :, :, :-1], ((0, 0), (0, 0), (0, 0), (1, 0), (0, 0), (0, 0)))
        return jnp.concatenate([prev, t], axis=4)

    qb, kb, vb = to_blocks(q), to_blocks(k), to_blocks(v)
    kw, vw = with_prev(kb), with_prev(vb)
    scores = jnp.einsum('bdhnqe,bdhnke->bdhnqk', qb, kw).astype(jnp.float32) * (e ** -0.5)
    qi = jnp.arange(blk)[:, None]
    ki = jnp.arange(2 * blk)[None, :]
    dist = blk + qi - ki
    first = (jnp.arange(nb) == 0)[:, None, None]
    valid = (dist >= 0) & (dist <= n_back) & ~(first & (ki < blk))
    scores = jnp.where(valid, scores, -jnp.inf)
    mx = jnp.max(scores, axis=-1, keepdims=True)
    p = jnp.exp(scores - mx)
    den = jnp.sum(p, axis=-1, keepdims=True)
    o = jnp.einsum('bdhnqk,bdhnke->bdhnqe', p, vw.astype(jnp.float32)) / den
    lse = (mx + jnp.log(den))[..., 0]
    o = o.reshape(b, dilation, h, L, e).transpose(0, 3, 1, 2, 4).reshape(b, s_pad, h, e)[:, :s]
    lse = lse.reshape(b, dilation, h, L).transpose(0, 3, 1, 2).reshape(b, s_pad, h)[:, :s]
    return o, lse

def dilated_attention(q, k, v, gq, gk):
    b, s = q.shape[:2]
    q = rms_norm_2(q, gq)
    k = rms_norm_2(k, gk)
    outs, lses = [], []
    for gi, (window, dilation) in enumerate(ATTN_GROUPS):
        sl = slice(gi * ATTN_HEADS_PER_GROUP, (gi + 1) * ATTN_HEADS_PER_GROUP)
        o, l = _dilated_group(q[:, :, sl], k[:, :, sl], v[:, :, sl], window, dilation)
        outs.append(o)
        lses.append(l)
    wts = jax.nn.softmax(jnp.stack(lses, axis=0), axis=0)
    o = jnp.sum(wts[..., None] * jnp.stack(outs, axis=0), axis=0)
    return o.reshape(b, s, ATTN_OUT).astype(v.dtype)

def gated_linear_attention(q, k, v, log_a):
    b, s, h, dk = q.shape
    dv = v.shape[-1]
    c = GLA_CHUNK
    n = s // c

    def chunks(t):
        return t.reshape(b, n, c, h, t.shape[-1]).transpose(1, 0, 3, 2, 4).astype(jnp.float32)

    qc = chunks(q) * (dk ** -0.5)
    kc, vc, ac = chunks(k), chunks(v), chunks(log_a)
    causal = jnp.tril(jnp.ones((c, c), dtype=bool))[:, :, None]

    def step(state, inp):
        qt, kt, vt, at = inp
        bcum = jnp.cumsum(at, axis=2)
        o_inter = jnp.einsum('bhtk,bhkv->bhtv', qt * jnp.exp(bcum), state)
        diff = bcum[:, :, :, None, :] - bcum[:, :, None, :, :]
        decay = jnp.exp(jnp.where(causal, diff, -jnp.inf))
        attn = jnp.einsum('bhtk,bhsk,bhtsk->bhts', qt, kt, decay)
        o_intra = jnp.einsum('bhts,bhsv->bhtv', attn, vt)
        blast = bcum[:, :, -1:, :]
        state = (jnp.exp(blast[:, :, 0, :])[..., None] * state
                 + jnp.einsum('bhsk,bhsv->bhkv', kt * jnp.exp(blast - bcum), vt))
        return state, o_inter + o_intra

    state0 = jnp.zeros((b, h, dk, dv), jnp.float32)
    _, o = lax.scan(step, state0, (qc, kc, vc, ac))
    return o.transpose(1, 0, 3, 2, 4).reshape(b, s, h, dv).astype(v.dtype)

def second_inputs(seed: int = 0) -> dict:
    key = jax.random.key(seed)
    ks = jax.random.split(key, 16)
    f32 = jnp.float32

    def dense(k, fan_in, fan_out):
        return jax.random.normal(k, (DEPTH, fan_in, fan_out), f32) * fan_in ** -0.5

    def gain(k, n):
        return 1.0 + 0.02 * jax.random.normal(k, (DEPTH, n), f32)

    return {
        'x': jax.random.normal(ks[0], (BATCH, SEQ, D_MODEL), f32),
        'norm1_g': gain(ks[1], D_MODEL),
        'w_in': dense(ks[2], D_MODEL, D_IN),
        'attn_q_norm_g': gain(ks[3], ATTN_HEAD_DIM),
        'attn_k_norm_g': gain(ks[4], ATTN_HEAD_DIM),
        'gla_gate_up': dense(ks[5], GLA_GATE_RANK, GLA_DK),
        'gla_gate_bias': 0.1 * jax.random.normal(ks[6], (DEPTH, GLA_DK), f32),
        'gla_out_norm_g': gain(ks[7], GLA_HV),
        'branch_gate_bias': 0.1 * jax.random.normal(ks[8], (DEPTH, N_BRANCHES * D_MODEL), f32),
        'w_attn_branch': dense(ks[9], ATTN_OUT, D_MODEL),
        'w_gla_branch': dense(ks[10], GLA_DV, D_MODEL),
        'w_out': dense(ks[11], D_MODEL, D_MODEL),
        'norm2_g': gain(ks[12], D_MODEL),
        'w_ff_up': dense(ks[13], D_MODEL, D_FF_2),
        'w_ff_down': dense(ks[14], D_FF_2, D_MODEL),
    }

def second_block(x, norm1_g, w_in, attn_q_norm_g, attn_k_norm_g, gla_gate_up, gla_gate_bias,
              gla_out_norm_g, branch_gate_bias, w_attn_branch, w_gla_branch, w_out,
              norm2_g, w_ff_up, w_ff_down):
    b, s, _ = x.shape
    for l in range(DEPTH):
        h = rms_norm_2(x, norm1_g[l])
        proj = jnp.einsum('bsd,de->bse', h, w_in[l])
        p_attn, p_q, p_k, p_v, p_r, p_a, p_gate = jnp.split(proj, _IN_OFFSETS, axis=-1)

        qkv = p_attn.reshape(b, s, 3, N_ATTN_HEADS, ATTN_HEAD_DIM)
        o_attn = dilated_attention(qkv[:, :, 0], qkv[:, :, 1], qkv[:, :, 2],
                                   attn_q_norm_g[l], attn_k_norm_g[l])

        gate_logits = (p_a @ gla_gate_up[l] + gla_gate_bias[l]).astype(jnp.float32)
        log_a = jax.nn.log_sigmoid(gate_logits) / GLA_TAU
        o_gla = gated_linear_attention(
            p_q.reshape(b, s, GLA_HEADS, GLA_HK),
            p_k.reshape(b, s, GLA_HEADS, GLA_HK),
            p_v.reshape(b, s, GLA_HEADS, GLA_HV),
            log_a.reshape(b, s, GLA_HEADS, GLA_HK))
        o_gla = rms_norm_2(o_gla, gla_out_norm_g[l]).reshape(b, s, GLA_DV) * jax.nn.silu(p_r)

        gates = jax.nn.sigmoid(p_gate + branch_gate_bias[l]).reshape(b, s, N_BRANCHES, D_MODEL)
        mixed = (gates[:, :, 0] * (o_attn @ w_attn_branch[l])
                 + gates[:, :, 1] * (o_gla @ w_gla_branch[l]))
        x = x + mixed @ w_out[l]

        h2 = rms_norm_2(x, norm2_g[l])
        x = x + jnp.square(jax.nn.relu(h2 @ w_ff_up[l])) @ w_ff_down[l]
    return x


def setup_inputs(seed=0):
    out = dict(first_inputs(seed))
    for name, value in second_inputs(seed + 1).items():
        if name != "x":
            out[name + "_2"] = value
    return out


def reference(
    x, positions, attn_norm_w, w_in, ret_gn_w, mla_q_norm_w, w_uq, mla_kv_norm_w, w_ukv, w_out,
    ffn_norm_w, w_up, conv_w, conv_b, w_down, final_norm_w, norm1_g_2, w_in_2, attn_q_norm_g_2,
    attn_k_norm_g_2, gla_gate_up_2, gla_gate_bias_2, gla_out_norm_g_2, branch_gate_bias_2,
    w_attn_branch_2, w_gla_branch_2, w_out_2, norm2_g_2, w_ff_up_2, w_ff_down_2,
):
    x = first_block(
        x, positions, attn_norm_w, w_in, ret_gn_w, mla_q_norm_w, w_uq, mla_kv_norm_w, w_ukv,
        w_out, ffn_norm_w, w_up, conv_w, conv_b, w_down, final_norm_w,
    )
    return second_block(
        x, norm1_g_2, w_in_2, attn_q_norm_g_2, attn_k_norm_g_2, gla_gate_up_2, gla_gate_bias_2,
        gla_out_norm_g_2, branch_gate_bias_2, w_attn_branch_2, w_gla_branch_2, w_out_2,
        norm2_g_2, w_ff_up_2, w_ff_down_2,
    )


_drawn_inputs = setup_inputs


def setup_inputs(seed=0):
    import zlib

    import numpy as np

    out = dict(_drawn_inputs(seed))
    spreads = {}
    factors = {'ret_gn_w': 5.306,
     'mla_q_norm_w': 8.0,
     'mla_kv_norm_w': 8.0,
     'ffn_norm_w': 3.346,
     'conv_b': 6.606,
     'norm1_g_2': 3.893,
     'attn_q_norm_g_2': 8.0,
     'attn_k_norm_g_2': 8.0,
     'gla_gate_bias_2': 4.11,
     'gla_out_norm_g_2': 8.0,
     'branch_gate_bias_2': 4.026,
     'norm2_g_2': 3.252}
    for name, (base, spread) in spreads.items():
        noise = np.random.default_rng([zlib.crc32(name.encode()), seed]).standard_normal(out[name].shape)
        drawn = base * np.exp(spread * noise) if base else spread * noise
        out[name] = __import__('jax').numpy.asarray(drawn.astype(out[name].dtype))
    for name, factor in factors.items():
        out[name] = (out[name] * factor).astype(out[name].dtype)
    return out
```

```python
from collections import namedtuple
from contextlib import ExitStack

import numpy as np

import concourse.bass as bass
from concourse import mybir

P = 128
F32 = mybir.dt.float32
F32R = mybir.dt.float32r
I32 = mybir.dt.int32
ALU = mybir.AluOpType
ACT = mybir.ActivationFunctionType
AX = mybir.AxisListType

TOKENS, D = 256, 1024
TT = TOKENS // P
KT = D // P
EPS = 1e-6
RAW, RING = 3, 4
HALF = 1024

RH, RD = 8, 64
RW = RH * RD
MH, NOPE, PE_D, MV = 8, 64, 32, 64
QK = NOPE + PE_D
QR, KVR = 256, 128
FF1 = 2816
CH1 = FF1 // 256
AH, AG, AD = 8, 3, 64
DIL = (1, 4, 16)
GH, GK, GV = 4, 128, 256
FF2 = 4096
CH2 = FF2 // 256
AQ0 = 0
AW = AG * AH * AD
GQ0 = 3 * AW
GK0, GV0 = GQ0 + 512, GQ0 + 1024
GR0 = GV0 + 1024
GA0 = GR0 + 1024
GG0 = GA0 + 16

NEG = -1e30
LEVELS = 7

VEC = {}
_r = 0
for _name, _n in (("attn_norm_w", 8), ("ffn_norm_w", 8), ("norm1_g_2", 8), ("norm2_g_2", 8),
                  ("branch_gate_bias_2", 16), ("ret_gn_w", 4), ("mla_q_norm_w", 2), ("mla_kv_norm_w", 1),
                  ("gla_gate_bias_2", 4), ("gla_out_norm_g_2", 2), ("conv_b", 44)):
    VEC[_name] = (_r, _n)
    _r += _n
VROWS = _r
CW0, CW1, CW2 = VROWS, VROWS + 44, VROWS + 88

C_IDENT = 0
C_INVF = C_IDENT + P
C_CAUSAL = C_INVF + 48
C_DECAY = C_CAUSAL + 3 * P
C_DIL = C_DECAY + RH * 3 * P
C_LEVEL = C_DIL + 9 * P
C_END = C_LEVEL + (LEVELS + 1) * P


def constants():
    t = np.zeros((P, C_END), np.float32)
    t[:, C_IDENT:C_IDENT + P] = np.eye(P)
    t[:, C_INVF:C_INVF + 32] = 10000.0 ** (-np.arange(0, 64, 2) / 64)
    t[:, C_INVF + 32:C_INVF + 48] = 10000.0 ** (-np.arange(0, 32, 2) / 32)
    i = np.arange(P)
    late = np.where(i[None, :] <= i[:, None], 0.0, NEG)
    t[:, C_CAUSAL:C_CAUSAL + P] = late
    t[:, C_CAUSAL + 2 * P:C_CAUSAL + 3 * P] = late
    for h in range(RH):
        log_gamma = np.log1p(-(2.0 ** (-5.0 - h)))
        for n, shift in enumerate((0, P, 0)):
            d = shift + i[None, :] - i[:, None]
            at = C_DECAY + (3 * h + n) * P
            t[:, at:at + P] = np.where(d >= 0, np.exp(log_gamma * np.maximum(d, 0)), 0) * RD ** -0.5
    for a in range(TT):
        keys = (a + 1) * P
        d = a * P + i[:, None] - np.arange(keys)[None, :]
        for g, dil in enumerate(DIL):
            ok = (d >= 0) & (d % dil == 0) & (d <= P * dil)
            at = C_DIL + 3 * P * a + g * keys
            t[:, at:at + keys] = np.where(ok, 0.0, NEG)
    for lv in range(LEVELS):
        b = 2 << lv
        ok = (i[:, None] // b == i[None, :] // b) & (i[:, None] % b < b // 2) & (i[None, :] % b >= b // 2)
        t[:, C_LEVEL + lv * P:C_LEVEL + (lv + 1) * P] = ok
    t[:, C_LEVEL + LEVELS * P:C_END] = np.eye(P)
    return t


M_FF1 = 16
M_IN2 = M_FF1 + 3 * CH1
M_ATT = M_IN2 + 9
M_R = M_ATT + 6 * AG
M_GATE = M_R + 4
M_BR = M_GATE + 8
M_OUT2 = M_BR + 6
M_FF2 = M_OUT2 + 4
M_END = M_FF2 + 2 * CH2
C_OUT, C_GLA, C_ATT, C_R = 9, 11, 16, 25
C_GATE, C_BR, C_OUT2 = 27, 31, 35

PARTS = ("x", "positions", "attn_norm_w", "w_in", "ret_gn_w", "mla_q_norm_w", "w_uq", "mla_kv_norm_w", "w_ukv",
         "w_out", "ffn_norm_w", "w_up", "conv_w", "conv_b", "w_down", "final_norm_w", "norm1_g_2", "w_in_2",
         "attn_q_norm_g_2", "attn_k_norm_g_2", "gla_gate_up_2", "gla_gate_bias_2", "gla_out_norm_g_2",
         "branch_gate_bias_2", "w_attn_branch_2", "w_gla_branch_2", "w_out_2", "norm2_g_2", "w_ff_up_2",
         "w_ff_down_2")
Parts = namedtuple("Parts", PARTS)

TWO_PI = (6.28125, 0.0019350051879882812, 3.0199159819e-07)
MAGIC = 1.5 * 2 ** 23


def slab_table(w):
    def rows(x, k0, k1, c0, c1):
        return x[k0 * P:k1 * P, c0:c1].rearrange("(k p) c -> p k c", p=P)

    def chunk(x, c0, c1):
        return [(rows(x, k, k + 4, c0, c1), 2 * (c1 - c0), 0) for k in (0, 4)]

    w_in, w_in_2 = w.w_in[0], w.w_in_2[0]
    one = chunk(w_in, 2048, 2464) + chunk(w_in, 0, 512)
    one += [(rows(w.w_uq[0], 0, 2, 0, 768), 768, 0), (rows(w.w_ukv[0], 0, 1, 0, 1024), 512, 0)]
    for c in (512, 1024, 1536):
        one += chunk(w_in, c, c + 512)
    for c in (0, 512):
        one += chunk(w.w_out[0], c, c + 512)
    assert len(one) == M_FF1

    two = chunk(w_in_2, GQ0, GQ0 + 512) + chunk(w_in_2, GK0, GK0 + 512)
    two += [(rows(w_in_2, 0, KT, GA0, GA0 + 16), 64, 0)]
    two += chunk(w_in_2, GV0, GV0 + 512) + chunk(w_in_2, GV0 + 512, GV0 + 1024)
    for g in range(AG):
        for part in range(3):
            two += chunk(w_in_2, part * AW + g * 512, part * AW + g * 512 + 512)
    for c in (GR0, GR0 + 512):
        two += chunk(w_in_2, c, c + 512)
    for c in range(GG0, GG0 + 2048, 256):
        two += [(rows(w_in_2, 0, KT, c, c + 256), HALF, 256)]
    for c in (0, 512):
        two += [(rows(w.w_attn_branch_2[0], 0, 4, c, c + 512), HALF, 512)]
        two += [(rows(w.w_gla_branch_2[0], 0, KT, q, q + 256), HALF, 256) for q in (c, c + 256)]
    for c in (0, 512):
        two += chunk(w.w_out_2[0], c, c + 512)
    assert len(two) == M_FF2 - M_IN2
    return {**dict(enumerate(one)), **{M_IN2 + n: t for n, t in enumerate(two)}}


def ffn_columns(m):
    if m < M_IN2:
        return 0 if m == M_IN2 - 1 or m >= M_FF1 + 2 and (m - M_FF1 - 2) % 3 == 2 else 256
    return 0 if m == M_END - 1 or (m > M_FF2 and (m - M_FF2) % 2 == 0) else 256


SEMAPHORES = (
    "x_in ident_in pos_in consts_in qkg_in vecs_in fw_in gate_up_in levels_in dil_in out_stored "
    "hi_done lo_done mm_done acc_free0 acc_free1 "
    "act_chain dve_chain "
    "vecs_turned vecs_ready "
    "ssq rms_ms rms_root x_scaled x_turned h_hi_done h_lo_done x_added "
    "trig_arg trig latent_scaled latents_turned latents_hi latents_lo "
    "mla_q_ready mla_k_ready mla_q_turned mla_k_turned mla_qT mla_kT mla_scores mla_masked mla_max mla_exp "
    "mla_turned mla_pt mla_pv mla_o "
    "ret_roped ret_q_turned ret_k_turned ret_qT ret_kT ret_scores ret_masked ret_o_head ret_copied "
    "ret_centred ret_sq ret_y mixed_turned mixed_hi mixed_lo "
    "taps tap1 gate_conv val_conv gate_silu act_ready act_hi_done act_lo_done "
    "gla_turned gla_qT gla_kT pa_turned pa_T gla_logits gla_z  gla_soft gla_diff "
    "gla_e gla_qe gla_level gla_taken gla_o gla_go gla_ssq gla_ms gla_norm gla_ready "
    "go_turned go_hi go_lo "
    "att_squared att_ms att_root att_scaled att_turned att_T "
    "att_scores att_masked att_max att_exp att_turnedp att_pt att_pv att_o oa_turned oa_hi oa_lo "
    "qkg_scaled mix_ready mix_hi mix_lo "
    "up_relu up_square up_hi up_lo"
).split()
Semaphores = namedtuple("Semaphores", SEMAPHORES)


def two_blocks_kernel(nc, w, consts, out):
    with ExitStack() as ctx:
        def sb(name, shape, dt=F32):
            return ctx.enter_context(nc.sbuf_tensor(name, shape, dt))

        bank = ctx.enter_context(nc.psum_tensor("bank", [P, 8, 512], F32))
        raw = sb("raw", [P, RAW, 2 * HALF])
        w_hi = sb("w_hi", [P, RING, HALF], F32R)
        w_lo = sb("w_lo", [P, RING, HALF], F32R)
        h_hi = sb("h_hi", [P, KT, TOKENS], F32R)
        h_lo = sb("h_lo", [P, KT, TOKENS], F32R)
        a_hi = sb("a_hi", [P, 12, TOKENS], F32R)
        a_lo = sb("a_lo", [P, 12, TOKENS], F32R)
        x = sb("x_tok", [P, TT, D])
        ident = sb("ident", [P, P])
        vec = sb("vec", [P, VROWS + 132])
        mix_gain = sb("mix_gain", [P, KT])
        qkg = sb("qkg", [P, 2])
        st = sb("stats", [P, 96])
        arena = sb("arena", [P, 26016])

        s = Semaphores(*[ctx.enter_context(nc.semaphore(n)) for n in SEMAPHORES])
        raw_in = [ctx.enter_context(nc.semaphore(f"raw_in{r}")) for r in range(RAW)]
        acc_free = (s.acc_free0, s.acc_free1)
        table = slab_table(w)

        def area(at, *dims):
            n = 1
            for d in dims:
                n *= d
            v = arena[:, at:at + n]
            if len(dims) == 2:
                return v.rearrange("p (a b) -> p a b", b=dims[1])
            if len(dims) == 3:
                return v.rearrange("p (a b c) -> p a b c", b=dims[1], c=dims[2])
            if len(dims) == 4:
                return v.rearrange("p (a b c d) -> p a b c d", b=dims[1], c=dims[2], d=dims[3])
            return v

        def column(name, k=0):
            r = VEC[name][0] + k
            return vec[:, r:r + 1]

        def flat(v):
            return v.rearrange("p a b -> p (a b)")

        def raw_half(r, half, size, cols):
            if not cols:
                return raw[:, r, half * size:(half + 1) * size]
            c = cols // 2
            return raw[:, r, 0:2 * size].rearrange("p (k c) -> p k c", c=cols)[:, :, half * c:(half + 1) * c]

        def pair(c, width=512):
            return bank[:, 2 * (c % 2):2 * (c % 2) + 2, 0:width]

        xn = area(0, TT, D)
        vec_rows = area(3072, 3, P)
        proj = area(4096, TT, 2464)
        causal = area(9024, 3 * P)
        decay = area(9408, RH, 3 * P)
        q_tok = area(12480, TT, MH, QK)
        k_tok = area(14016, TT, MH, QK)
        kv = area(15552, TT, MH, NOPE + MV)
        mqT = area(17600, MH, TOKENS)
        mkT = area(19648, MH, TOKENS)
        rqT = area(21696, RH // 2, TOKENS)
        rkT = area(22720, RH // 2, TOKENS)
        sT = area(23744, 2, 3 * P)
        pT = area(24512, 2, 3 * P)
        rope_tmp = area(0, 2, RH * RD // 2)
        angle = area(25280, 2, TT, 48)
        turns = area(25472, 2, TT, 48)
        pos_i = area(25664, TT)
        pos_f = area(25666, TT)
        invf = area(25668, 48)
        conv = area(0, 2, 2, 512)
        silu1 = area(2048, 2, 512)
        act1 = area(3072, 2, 512)
        fw = area(24864, D)
        gqk = area(0, 2, TT, 512)
        qe = area(0, GH, TOKENS)
        ke = area(1024, GH, TOKENS)
        soft = area(2048, GH * TOKENS)
        gv = area(3072, TT, GH * GV)
        gqT = area(5120, GH, TOKENS)
        gkT = area(6144, GH, TOKENS)
        run = area(7168, GH * TOKENS)
        z = area(8192, GH * TOKENS)
        g_in = area(9216, GH, TT, P)
        resets = area(9216, GH * TOKENS)
        g_cross = area(10240, GH, P)
        levels = area(10752, LEVELS + 1, P)
        paT = area(11776, TOKENS)
        gate_up = area(12032, GH * GK)
        ga = area(12544, TT, 16)
        a_tok = area(12576, 2, TT, 512)
        aqT = area(14624, 4 * AG, TOKENS)
        akT = area(17696, 4 * AG, TOKENS)
        av = area(20768, TT, AW)
        asq = area(23840, TT, 512)
        dil = area(24864, 9 * P)
        go = area(5120, TT, GH * GV)
        silu_r = area(0, TT, GH * GV)
        gates = (area(3072, KT, TOKENS), area(7168, KT, TOKENS))
        p = area(9216, 2, 6 * P)
        ppT = area(10752, 2, 6 * P)
        oa = area(23840, TT, 512)
        mix = area(12576, 2, 2, 512)
        relu2 = area(3072, 3, 512)
        square2 = area(4608, 3, 512)

        def turn(dst, src, rows=P):
            return nc.tensor.transpose(dst, src, ident[0:rows, 0:rows])

        block = ctx.enter_context(nc.Block())

        @block.sync
        def _(sp):
            def load_slab(slot, m, dst, src):
                if not isinstance(m, int) or m >= RAW:
                    sp.wait_ge(s.lo_done, m * 2 - 2 * RAW + 2)
                sp.dma_start(dst, src).then_inc(raw_in[slot], 16)

            def load(m):
                src = table[m][0]
                _, k, c = src.shape
                load_slab(m % RAW, m, raw[:, m % RAW, 0:k * c].rearrange("p (k c) -> p k c", c=c), src)

            def load_ffn(m0, i, src):
                m = m0 if i is None else i * 6 + m0
                k = src.shape[1]
                load_slab(m0 % RAW, m, raw[:, m0 % RAW, :].rearrange("p (k c) -> p k c", k=k), src)

            sp.dma_start(x[:], w.x[0].rearrange("(a p) d -> p a d", p=P)).then_inc(s.x_in, 16)
            sp.dma_start(ident[:], consts[:, C_IDENT:C_IDENT + P]).then_inc(s.ident_in, 16)
            load(0)
            load(1)
            for a in range(TT):
                sp.dma_start(pos_i[:, a:a + 1].bitcast(I32),
                             w.positions[0, a * P:(a + 1) * P].rearrange("(p o) -> p o", o=1)).then_inc(s.pos_in, 16)
            sp.dma_start(invf, consts[:, C_INVF:C_INVF + 48]).then_inc(s.pos_in, 16)
            load(2)
            sp.dma_start(causal, consts[:, C_CAUSAL:C_CAUSAL + 3 * P]).then_inc(s.consts_in, 16)
            sp.dma_start(decay, consts[:, C_DECAY:C_DIL].rearrange("p (h c) -> p h c", h=RH)).then_inc(s.consts_in, 16)
            for g, v in enumerate((w.attn_q_norm_g_2, w.attn_k_norm_g_2)):
                for r in (0, 64):
                    sp.dma_start(qkg[r:r + 64, g:g + 1], v.rearrange("l (d o) -> (l d) o", o=1)).then_inc(s.qkg_in, 16)
            for m in range(3, M_FF1):
                load(m)

            up = w.w_up[0].rearrange("(k p) c -> p k c", p=P)
            down = w.w_down[0].rearrange("(n k p) c -> n p k c", k=2, p=P)
            load_ffn(M_FF1, None, up[:, :, 0:256])
            load_ffn(M_FF1 + 1, None, up[:, :, FF1:FF1 + 256])
            with sp.Fori(0, CH1 // 2) as i:
                for e in range(2):
                    m = M_FF1 + 2 + 3 * e
                    load_ffn(m, i, up[:, :, bass.ds(i * 512 + 256 * (e + 1), 256)])
                    load_ffn(m + 1, i, up[:, :, bass.ds(i * 512 + FF1 + 256 * (e + 1), 256)])
                    load_ffn(m + 2, i, down[bass.ds(i * 2 + e, 1)].rearrange("n p k c -> p (n k) c"))
            load_ffn(M_IN2 - 1, None, down[CH1 - 1])

            load(M_IN2)
            sp.wait_ge(s.mm_done, 2 * M_FF1)
            sp.dma_start(fw, w.final_norm_w.rearrange("(o d) -> o d", o=1).to_broadcast([P, D])).then_inc(s.fw_in, 16)
            sp.dma_start(gate_up[0:16, :], w.gla_gate_up_2[0]).then_inc(s.gate_up_in, 16)
            sp.dma_start(levels, consts[:, C_LEVEL:C_END].rearrange("p (l c) -> p l c", c=P)).then_inc(s.levels_in, 16)
            for m in range(M_IN2 + 1, M_IN2 + 5):
                load(m)
            sp.wait_ge(s.x_added, 2)
            sp.dma_start(dil, consts[:, C_DIL:C_LEVEL]).then_inc(s.dil_in, 16)
            for m in range(M_IN2 + 5, M_FF2):
                load(m)

            up = w.w_ff_up_2[0].rearrange("(k p) c -> p k c", p=P)
            down = w.w_ff_down_2[0].rearrange("(n k p) c -> n p k c", k=2, p=P)
            load_ffn(M_FF2, None, up[:, :, 0:256])
            with sp.Fori(0, CH2 // 3) as i:
                for e in range(3):
                    m = M_FF2 + 1 + 2 * e
                    load_ffn(m, i, up[:, :, bass.ds(i * 768 + 256 * (e + 1), 256)])
                    load_ffn(m + 1, i, down[bass.ds(i * 3 + e, 1)].rearrange("n p k c -> p (n k) c"))
            load_ffn(M_END - 1, None, down[CH2 - 1])

            for a in range(TT):
                sp.wait_ge(s.x_added, 3 + a)
                sp.dma_start(out[0].rearrange("(a p) d -> a p d", p=P)[a], x[:, a, :]).then_inc(s.out_stored, 16)
            sp.wait_ge(s.out_stored, 16 * TT)

        @block.tensor
        def _(pe):
            def passes(dst, l_hi, l_lo, r_hi, r_lo, start, stop):
                nc.tensor.matmul(dst, l_hi, r_hi, start=start, stop=False)
                nc.tensor.matmul(dst, l_hi, r_lo, start=False, stop=False)
                return nc.tensor.matmul(dst, l_lo, r_hi, start=False, stop=stop)

            def half_rows(n, width, k0, kn, lhs, accs, first, last, ready=None, i=None):
                q = n % RING
                pe.wait_ge(s.lo_done, n + 1 if i is None else i * 12 + n + 1)
                for k in range(kn):
                    if ready:
                        ready(k0 + k)
                    for a in range(TT):
                        for acc, c0, c1 in accs[a]:
                            at = k * width
                            ins = passes(acc, lhs[0][:, k0 + k, a * P:(a + 1) * P], lhs[1][:, k0 + k, a * P:(a + 1) * P],
                                         w_hi[:, q, at + c0:at + c1], w_lo[:, q, at + c0:at + c1],
                                         first and k == 0, last and k == kn - 1)
                ins.then_inc(s.mm_done, 1)

            def chunk_rows(n, c, width, lhs, ready=None, halves=(0, 1, 2, 3), kn=2):
                for e in halves:
                    if e == 0:
                        pe.wait_ge(acc_free[c % 2], c // 2)
                    half_rows(n + e, width, kn * e, kn, lhs, [[(pair(c, width)[:, a], 0, width)] for a in range(TT)],
                              e == 0, e == KT // kn - 1, ready)

            def half_columns(n, kn, c, dst, lhs, i=None):
                q = n % RING
                pe.wait_ge(s.lo_done, n + 1 if i is None else i * 12 + n + 1)
                for t in range(c):
                    for k in range(kn):
                        at = (k * c + t) * P
                        wh, wl = w_hi[:, q, at:at + P], w_lo[:, q, at:at + P]
                        ins = passes(dst[:, t * TOKENS:(t + 1) * TOKENS], wh, wl, lhs[0][:, k, :], lhs[1][:, k, :],
                                     k == 0, k == kn - 1)
                ins.then_inc(s.mm_done, 1)

            def turn_tiles(count, src, done, banks=(4, 5, 6, 7), free=None):
                for k in range(count):
                    b = banks[k // 2]
                    if k % 2 == 0 and free:
                        free(k // 2)
                    for a in range(TT):
                        at = k % 2 * TOKENS + a * P
                        ins = turn(bank[:, b, at:at + P], src(a, k))
                    if k % 2 == 1 or k == count - 1:
                        ins.then_inc(done, 1)

            h, al = (h_hi, h_lo), (a_hi, a_lo)

            def normed(norm):
                pe.wait_ge(s.x_scaled, 2 * norm + 2)
                turn_tiles(KT, lambda a, k: xn[:, a, k * P:(k + 1) * P], s.x_turned)
                return lambda k: pe.wait_ge(s.h_lo_done, 4 * norm + k // 2 + 1) if k % 2 == 0 else None

            pe.wait_ge(s.ident_in, 16)
            pe.wait_ge(s.vecs_in, 16 * (len(VEC) + 2))
            turn(bank[:, 3, 0:VROWS], vec_rows[0:VROWS, 0, :], VROWS)
            turn(bank[:, 3, CW0:CW0 + 88], vec_rows[0:88, 1, :], 88)
            turn(bank[:, 3, CW2:CW2 + 44], vec_rows[0:44, 2, :], 44).then_inc(s.vecs_turned, 1)
            ready = normed(0)
            chunk_rows(0, 0, 416, h, ready)
            pe.wait_ge(s.vecs_ready, 1)
            chunk_rows(4, 1, 512, h)
            pe.wait_ge(s.latent_scaled, 1)
            turn_tiles(3, lambda a, k: proj[:, a, 2048 + k * P:2176 + k * P], s.latents_turned)
            for k in range(2):
                if k == 0:
                    pe.wait_ge(s.latents_lo, 1)
                    for a in range(TT):
                        pe.wait_ge(acc_free[a], 1)
                half_rows(8 + k, 768, k, 1, al, [[(bank[:, 2 * a, :], 0, 512), (bank[:, 2 * a + 1, 0:256], 512, 768)]
                                                 for a in range(TT)], k == 0, k == 1)
            pe.wait_ge(s.latents_lo, 2)
            for e in range(2):
                for a in range(TT):
                    pe.wait_ge(acc_free[a], 2)
                half_rows(10 + e, 512, 2, 1, al, [[(bank[:, 2 * a + e, :], 0, 512)] for a in range(TT)], True, True)
            chunk_rows(12, 6, 512, h)
            pe.wait_ge(s.mla_q_ready, 1)
            for hd in range(MH):
                for a in range(TT):
                    at = hd % 2 * TOKENS + a * P
                    ins = turn(bank[0:QK, 4 + hd // 2, at:at + P], q_tok[:, a, hd, :])
                if hd % 2:
                    ins.then_inc(s.mla_q_turned, 1)
            chunk_rows(16, 7, 512, h, halves=(0, 1))
            pe.wait_ge(s.mla_k_ready, 1)
            for hd in range(MH):
                if hd % 2 == 0:
                    pe.wait_ge(s.mla_qT, hd // 2 + 1)
                for a in range(TT):
                    at = hd % 2 * TOKENS + a * P
                    ins = turn(bank[0:QK, 4 + hd // 2, at:at + P], k_tok[:, a, hd, :])
                if hd % 2:
                    ins.then_inc(s.mla_k_turned, 1)
            chunk_rows(16, 7, 512, h, halves=(2, 3))
            pe.wait_ge(s.ret_roped, 1)
            pe.wait_ge(s.mla_kT, 4)
            turn_tiles(4, lambda a, k: proj[:, a, k * P:(k + 1) * P], s.ret_q_turned, (4, 5))
            turn_tiles(4, lambda a, k: proj[:, a, 512 + k * P:640 + k * P], s.ret_k_turned, (6, 7))

            def mla_score(hd):
                if hd >= 2:
                    pe.wait_ge(s.mla_masked, hd - 1)
                b = bank[:, 4 + hd % 2, :]
                nc.tensor.matmul(b[:, 0:P], mqT[0:QK, hd, 0:P], mkT[0:QK, hd, 0:P], start=True, stop=True)
                nc.tensor.matmul(b[:, P:3 * P], mqT[0:QK, hd, P:2 * P], mkT[0:QK, hd, :], start=True,
                                 stop=True).then_inc(s.mla_scores, 1)

            pe.wait_ge(s.ret_qT, 2)
            mla_score(0)
            mla_score(1)
            pe.wait_ge(s.ret_kT, 2)
            for hd in range(MH):
                if hd % 2 == 0:
                    chunk_rows(20, 8, 512, h, halves=(hd // 2,))
                pe.wait_ge(s.mla_exp, hd + 1)
                if hd >= 1:
                    pe.wait_ge(s.mla_pt, hd)
                for n in range(3):
                    ins = turn(bank[:, 6, n * P:(n + 1) * P], sT[:, hd % 2, n * P:(n + 1) * P])
                ins.then_inc(s.mla_turned, 1)
                if hd + 2 < MH:
                    mla_score(hd + 2)
                pe.wait_ge(s.mla_pt, hd + 1)
                if hd == 4:
                    pe.wait_ge(s.mla_o, 1)
                o = bank[:, 7, hd % 4 * 128:hd % 4 * 128 + 128]
                v = [kv[:, a, hd, NOPE:NOPE + MV] for a in range(TT)]
                w_ = pT[:, hd % 2, :]
                nc.tensor.matmul(o[:, 0:64], w_[:, 0:P], v[0], start=True, stop=True)
                nc.tensor.matmul(o[:, 64:128], w_[:, P:2 * P], v[0], start=True, stop=False)
                nc.tensor.matmul(o[:, 64:128], w_[:, 2 * P:3 * P], v[1], start=False, stop=True).then_inc(s.mla_pv, 1)

            def ret_score(hd):
                if hd >= 2:
                    pe.wait_ge(s.ret_masked, hd - 1)
                r = hd % 2 * RD
                q, k = rqT[r:r + RD, hd // 2, :], rkT[r:r + RD, hd // 2, :]
                b = bank[:, 4 + hd % 2, :]
                nc.tensor.matmul(b[:, 0:2 * P], k[:, 0:P], q, start=True, stop=True)
                nc.tensor.matmul(b[:, 2 * P:3 * P], k[:, P:2 * P], q[:, P:2 * P], start=True,
                                 stop=True).then_inc(s.ret_scores, 1)

            pe.wait_ge(s.mla_masked, MH)
            ret_score(0)
            ret_score(1)
            pe.wait_ge(s.mla_pt, MH)
            pe.wait_ge(s.mla_o, 2)
            pe.wait_ge(s.acc_free1, 4)
            for hd in range(RH):
                pe.wait_ge(s.ret_masked, hd + 1)
                v = [proj[:, a, 1024 + hd * RD:1024 + (hd + 1) * RD] for a in range(TT)]
                o = [bank[:, 6 + a, hd * RD:(hd + 1) * RD] for a in range(TT)]
                w_ = sT[:, hd % 2, :]
                nc.tensor.matmul(o[0], w_[:, 0:P], v[0], start=True, stop=True)
                nc.tensor.matmul(o[1], w_[:, P:2 * P], v[0], start=True, stop=False)
                nc.tensor.matmul(o[1], w_[:, 2 * P:3 * P], v[1], start=False, stop=True).then_inc(s.ret_o_head, 1)
                if hd + 2 < RH:
                    ret_score(hd + 2)
            pe.wait_ge(s.ret_masked, RH)
            pe.wait_ge(s.ret_copied, 1)
            pe.wait_ge(s.ret_y, 1)
            turn_tiles(KT, lambda a, k: proj[:, a, k * P:(k + 1) * P], s.mixed_turned)
            for c in range(2):
                chunk_rows(24 + 4 * c, C_OUT + c, 512, al,
                           lambda k: pe.wait_ge(s.mixed_lo, k // 2 + 1) if k % 2 == 0 else None)

            ready = normed(1)

            def ff1_up(n, e, i=None, j0=None):
                for v in range(2):
                    if i is not None or j0 >= 2:
                        pe.wait_ge((s.gate_conv, s.val_conv)[v], j0 - 1 if i is None else i * 2 + j0 - 1)
                    for f in range(2):
                        half_columns(n + 2 * v + f, KT, 1, bank[:, 2 * e + v, f * TOKENS:(f + 1) * TOKENS], h, i)

            def ff_down(n, at, first, last, act, i=None):
                act()
                for k in range(2):
                    half_rows(n + k, 1024, at + k, 1, al,
                              [[(bank[:, 4 + 2 * a + b, :], 512 * b, 512 * b + 512) for b in range(2)] for a in range(TT)],
                              first and k == 0, last and k == 1, None, i)

            n1 = 2 * M_FF1
            for k in range(KT):
                ready(k)
            pe.wait_ge(s.acc_free0, 6)
            ff1_up(n1, 0, None, 0)
            pe.wait_ge(s.acc_free1, 5)
            ff1_up(n1 + 4, 1, None, 1)
            ff_down(n1 + 8, 0, True, False, lambda: pe.wait_ge(s.act_lo_done, 1))
            ff1_up(n1 + 10, 0, None, 2)
            ff_down(n1 + 14, 2, False, False, lambda: pe.wait_ge(s.act_lo_done, 2))
            with pe.Fori(1, CH1 // 2) as i:
                ff1_up(n1 + 4, 1, i, 1)
                ff_down(n1 + 8, 0, False, False, lambda: pe.wait_ge(s.act_lo_done, i * 2 + 1), i)
                ff1_up(n1 + 10, 0, i, 2)
                ff_down(n1 + 14, 2, False, False, lambda: pe.wait_ge(s.act_lo_done, i * 2 + 2), i)
            ff_down(2 * M_IN2 - 2, 0, False, True, lambda: pe.wait_ge(s.act_lo_done, CH1))

            n2 = 2 * M_IN2
            pe.wait_ge(s.x_added, 1)
            pe.wait_ge(s.val_conv, CH1)
            ready = normed(2)
            chunk_rows(n2, C_GLA, 512, h, ready)
            chunk_rows(n2 + 4, C_GLA + 1, 512, h)
            chunk_rows(n2 + 8, C_GLA + 2, 16, h, halves=(0, 1), kn=4)
            chunk_rows(n2 + 10, C_GLA + 3, 512, h)
            pe.wait_ge(s.acc_free1, 6)
            turn_tiles(4, lambda a, k: gqk[:, 0, a, k * P:(k + 1) * P], s.gla_turned, (4, 5))
            pe.wait_ge(s.acc_free0, 7)
            turn_tiles(4, lambda a, k: gqk[:, 1, a, k * P:(k + 1) * P], s.gla_turned, (6, 7))
            chunk_rows(n2 + 14, C_GLA + 4, 512, h, halves=(0, 1))
            pe.wait_ge(s.acc_free1, 7)
            pe.wait_ge(s.gla_qT, 1)
            for a in range(TT):
                ins = turn(bank[0:16, 4, a * P:(a + 1) * P], ga[:, a, :])
            ins.then_inc(s.pa_turned, 1)
            chunk_rows(n2 + 14, C_GLA + 4, 512, h, halves=(2, 3))
            pe.wait_ge(s.pa_T, 1)
            pe.wait_ge(s.gate_up_in, 16)
            pe.wait_ge(s.gla_kT, 1)
            for hd in range(GH):
                ins = nc.tensor.matmul(bank[:, 6 + hd // 2, hd % 2 * TOKENS:(hd % 2 + 1) * TOKENS],
                                       gate_up[0:16, hd * GK:(hd + 1) * GK], paT[0:16, :], start=True, stop=True)
            ins.then_inc(s.gla_logits, 1)

            def turn_heads(t):
                nth = t // 3 * 2 + t % 3
                pe.wait_ge(s.att_scaled, nth + 1)
                if nth == 0:
                    pe.wait_ge(s.gla_z, 1)
                else:
                    pe.wait_ge(s.att_T, nth)
                turn_tiles(4, lambda a, k: a_tok[:, t % 3, a, k * P:(k + 1) * P], s.att_turned, (6, 7))

            for t in range(3 * AG):
                chunk_rows(n2 + 18 + 4 * t, C_ATT + t, 512, h)
                if t >= 1 and (t - 1) % 3 < 2:
                    turn_heads(t - 1)
                q_, k_ = (gqT, gkT) if t == 8 else (qe, ke)
                pe.wait_ge(s.gla_qe, min(t + 1, 8))
                if t >= 1:
                    pe.wait_ge(s.gla_taken, t)
                for hd in range(GH):
                    if t == 0:
                        ins = nc.tensor.matmul(bank[:, 4, hd * P:(hd + 1) * P], k_[:, hd, 0:P], q_[:, hd, P:2 * P],
                                               start=True, stop=True)
                    else:
                        for a in range(TT):
                            at = (hd % 2 * 2 + a) * P
                            ins = nc.tensor.matmul(bank[:, 4 + hd // 2, at:at + P], k_[:, hd, a * P:(a + 1) * P],
                                                   q_[:, hd, a * P:(a + 1) * P], start=True, stop=True)
                ins.then_inc(s.gla_level, 1)
            pe.wait_ge(s.gla_taken, 9)
            pe.wait_ge(s.att_T, 2 * AG)
            for a in range(TT):
                for hd in range(GH):
                    o = bank[:, 4 + 2 * a + hd // 2, hd % 2 * GV:(hd % 2 + 1) * GV]
                    v = [gv[:, t, hd * GV:(hd + 1) * GV] for t in range(TT)]
                    if a == 1:
                        nc.tensor.matmul(o, g_cross[:, hd, :], v[0], start=True, stop=False)
                    ins = nc.tensor.matmul(o, g_in[:, hd, a, :], v[a], start=a == 0, stop=True)
                ins.then_inc(s.gla_o, 1)

            def fill(f):
                if f < 8:
                    chunk_rows(2 * M_R + f // 4 * 4, C_R + f // 4, 512, h, halves=(f % 4,))
                    return
                c = C_GATE + (f - 8) // 4
                if f % 4 == 0:
                    pe.wait_ge(acc_free[c % 2], c // 2)
                t = f % 4
                half_columns(2 * M_R + f, KT, 1, bank[:, 2 * (c % 2) + t // 2, t % 2 * TOKENS:(t % 2 + 1) * TOKENS], h)

            def att_score(u):
                a, i = u // AH, u % AH
                keys = (a + 1) * P
                r = i % 2 * AD
                if u >= 1:
                    pe.wait_ge(s.att_masked, u)
                for g in range(AG):
                    k = g * 4 + i // 2
                    at = (4 + u % 2) * 512 + g * keys if a == 0 else 4 * 512 + g * keys
                    ins = nc.tensor.matmul(bank[:, at // 512, at % 512:at % 512 + keys],
                                           aqT[r:r + AD, k, a * P:(a + 1) * P], akT[r:r + AD, k, 0:keys],
                                           start=True, stop=True)
                ins.then_inc(s.att_scores, 1)

            def att_turn(u, part):
                done = u if u < AH else AH + 2 * (u - AH)
                if part == 0:
                    pe.wait_ge(s.att_exp, u + 1)
                if done + part >= 1:
                    pe.wait_ge(s.att_pt, done + part)
                for b in range(3):
                    at = (3 * part + b) * P
                    ins = turn(bank[:, 6, b * P:(b + 1) * P], p[:, u % 2, at:at + P])
                ins.then_inc(s.att_turnedp, 1)

            def att_value(u):
                a, i = u // AH, u % AH
                pe.wait_ge(s.att_pt, u + 1 if a == 0 else AH + 2 * (u - AH) + 2)
                if u == AH:
                    pe.wait_ge(s.att_o, 1)
                o = bank[:, 7, i * AD:(i + 1) * AD]
                n = AG * (a + 1)
                for b in range(n):
                    g, t = b // (a + 1), b % (a + 1)
                    ins = nc.tensor.matmul(o, ppT[:, u % 2, b * P:(b + 1) * P],
                                           av[:, t, g * 512 + i * AD:g * 512 + (i + 1) * AD], start=b == 0, stop=b == n - 1)
                ins.then_inc(s.att_pv, 1)

            fill(0)
            pe.wait_ge(s.gla_go, 2)
            att_score(0)
            f = 1
            for u in range(2 * AH):
                if u > 0:
                    fill(f)
                    f += 1
                    att_value(u - 1)
                att_turn(u, 0)
                if u + 1 < 2 * AH:
                    att_score(u + 1)
                if u >= AH:
                    fill(f)
                    f += 1
                    att_turn(u, 1)
            assert f == 24
            att_value(2 * AH - 1)

            pe.wait_ge(s.gla_ready, 1)
            pe.wait_ge(s.att_masked, 2 * AH)
            turn_tiles(4, lambda a, k: go[:, a, k * P:(k + 1) * P], s.go_turned, (4, 5))
            pe.wait_ge(s.att_o, 2)
            turn_tiles(4, lambda a, k: oa[:, a, k * P:(k + 1) * P], s.oa_turned, (6, 7))
            turn_tiles(4, lambda a, k: go[:, a, 512 + k * P:640 + k * P], s.go_turned, (4, 5),
                       lambda b: pe.wait_ge(s.go_lo, b + 1))
            b0 = 2 * M_BR
            for e in range(2):
                if e == 0:
                    pe.wait_ge(s.oa_lo, 2)
                for t in range(2):
                    c = C_BR + 2 * e + t
                    pe.wait_ge(acc_free[c % 2], c // 2)
                    half_columns(b0 + 6 * e + t, 4, 2, bank[:, 2 * (c % 2), :], (a_hi, a_lo))
                if e == 0:
                    pe.wait_ge(s.go_lo, 4)
                for t in range(2):
                    c = C_BR + 2 * e + t
                    for f in range(2):
                        half_columns(b0 + 6 * e + 2 + 2 * t + f, KT, 1,
                                     bank[:, 2 * (c % 2) + 1, f * TOKENS:(f + 1) * TOKENS],
                                     (a_hi[:, 4:12, :], a_lo[:, 4:12, :]))
            for c in range(2):
                chunk_rows(2 * M_OUT2 + 4 * c, C_OUT2 + c, 512, h,
                           lambda k: pe.wait_ge(s.mix_lo, k // 2 + 1) if k % 2 == 0 else None)

            pe.wait_ge(s.acc_free0, 19)
            pe.wait_ge(s.acc_free1, 18)
            ready = normed(3)
            for k in range(KT):
                ready(k)

            def ff2_up(n, b, j0, i=None):
                if i is not None or j0 >= 3:
                    pe.wait_ge(s.up_relu, j0 - 2 if i is None else i * 3 + j0 - 2)
                for f in range(2):
                    half_columns(n + f, KT, 1, bank[:, b, f * TOKENS:(f + 1) * TOKENS], h, i)

            n3 = 2 * M_FF2

            def ff2_step(i, first):
                for e in range(3):
                    ff2_up(n3 + 2 + 4 * e, (e + 1) % 3, e + 1, i)
                    ff_down(n3 + 4 + 4 * e, 2 * e, first and e == 0, False,
                            lambda: pe.wait_ge(s.up_lo, e + 1 if i is None else i * 3 + e + 1), i)

            ff2_up(n3, 0, 0)
            ff2_step(None, True)
            with pe.Fori(1, CH2 // 3) as i:
                ff2_step(i, False)
            ff_down(2 * M_END - 2, 0, False, True, lambda: pe.wait_ge(s.up_lo, CH2))

        @block.scalar
        def _(act):
            chain = [0]

            def link(ins):
                chain[0] += 1
                ins.then_inc(s.act_chain, 1)
                act.wait_ge(s.act_chain, chain[0])

            def split_hi(n, size, cols, i=None):
                m, half = n // 2, n % 2
                if half == 0:
                    landed = 16 * (m // RAW + 1)
                    act.wait_ge(raw_in[m % RAW], landed if i is None else i * 32 + landed)
                if i is not None or n >= RING:
                    act.wait_ge(s.mm_done, n - RING + 1 if i is None else i * 12 + n - RING + 1)
                dst = w_hi[:, n % RING, 0:size]
                if cols:
                    dst = dst.rearrange("p (k c) -> p k c", c=cols // 2)
                nc.scalar.copy(dst, raw_half(m % RAW, half, size, cols)).then_inc(s.hi_done, 1)

            def hi(*ns, i=None):
                for n in ns:
                    _, size, cols = table[n // 2] if n // 2 in table else (None, HALF, ffn_columns(n // 2))
                    split_hi(n, size, cols, i)

            def evacuate(dst, src, c, mm, func=ACT.Copy):
                act.wait_ge(s.mm_done, mm)
                nc.scalar.activation(dst, src, func).then_inc(acc_free[c % 2], 1)

            def sum_squares():
                for a in range(TT):
                    ins = nc.scalar.activation(xn[:, a, :], x[:, a, :], ACT.Square, accum_out=st[:, a:a + 1])
                ins.then_inc(s.ssq, 1)

            def root(nth, v):
                act.wait_ge(s.rms_ms, nth)
                nc.scalar.activation(v, v, ACT.Sqrt).then_inc(s.rms_root, 1)

            def turned_hi(dst, at, count, turned, before, gain, done, first=4):
                for k in range(count):
                    if k % 2 == 0:
                        act.wait_ge(turned, before + k // 2 + 1)
                    ins = nc.scalar.activation(dst[:, at + k, :], bank[:, first + k // 2, k % 2 * 256:k % 2 * 256 + 256],
                                               ACT.Copy, scale=gain(k))
                    if k % 2 == 1 or k == count - 1:
                        ins.then_inc(done, 1)

            for name, (r, n) in VEC.items():
                nc.scalar.dma_start(vec_rows[r:r + n, 0, :],
                                    w[PARTS.index(name)].rearrange("l (r c) -> (l r) c", c=P)).then_inc(s.vecs_in, 16)
            nc.scalar.dma_start(vec_rows[0:88, 1, :], w.conv_w[0, 0:2].rearrange("j (r c) -> (j r) c", c=P)).then_inc(
                s.vecs_in, 16)
            nc.scalar.dma_start(vec_rows[0:44, 2, :], w.conv_w[0, 2:3].rearrange("j (r c) -> (j r) c", c=P)).then_inc(
                s.vecs_in, 16)

            act.wait_ge(s.x_in, 16)
            sum_squares()
            root(1, st[:, 2:4])
            hi(0, 1, 2, 3)
            act.wait_ge(s.vecs_ready, 1)
            turned_hi(h_hi, 0, KT, s.x_turned, 0, lambda k: column("attn_norm_w", k), s.h_hi_done)
            hi(4, 5, 6, 7)
            evacuate(proj[:, :, 2048:2464], pair(0, 416), 0, 4)
            act.wait_ge(s.acc_free0, 1)
            for a in range(TT):
                nc.scalar.activation(xn[:, a, 0:QR], proj[:, a, 2048:2304], ACT.Square, accum_out=st[:, 4 + a:5 + a])
            for a in range(TT):
                ins = nc.scalar.activation(xn[:, a, QR:QR + KVR], proj[:, a, 2304:2432], ACT.Square,
                                           accum_out=st[:, 6 + a:7 + a])
            ins.then_inc(s.ssq, 1)
            root(2, st[:, 4:8])
            act.wait_ge(s.trig_arg, 1)
            nc.scalar.activation(angle, angle, ACT.Sin).then_inc(s.trig, 1)
            hi(8, 9, 10, 11)
            turned_hi(a_hi, 0, 3, s.latents_turned, 0,
                      lambda k: column("mla_q_norm_w", k) if k < 2 else column("mla_kv_norm_w"), s.latents_hi)
            evacuate(proj[:, :, 0:512], pair(1), 1, 8)
            hi(12, 13)
            for a in range(TT):
                evacuate(q_tok[:, a].rearrange("p h c -> p (h c)"),
                         flat(pair(2 + a))[:, 0:MH * QK], 2 + a, 10)
            hi(14, 15)
            for a in range(TT):
                evacuate(kv[:, a].rearrange("p h c -> p (h c)"), flat(pair(4 + a)), 4 + a, 12)
            hi(16, 17, 18, 19)
            evacuate(proj[:, :, 512:1024], pair(6), 6, 16)
            for r in range(4):
                act.wait_ge(s.mla_q_turned, r + 1)
                nc.scalar.activation(flat(mqT[0:QK, 2 * r:2 * r + 2, :]), bank[0:QK, 4 + r, :], ACT.Copy,
                                     scale=QK ** -0.5).then_inc(s.mla_qT, 1)
            hi(20, 21, 22, 23)
            evacuate(proj[:, :, 1024:1536], pair(7), 7, 20)
            for b in range(2):
                act.wait_ge(s.ret_q_turned, b + 1)
                nc.scalar.copy(flat(rqT[:, 2 * b:2 * b + 2, :]), bank[:, 4 + b, :]).then_inc(s.ret_qT, 1)
            for hd in range(MH + 1):
                if hd < MH:
                    act.wait_ge(s.mla_max, hd + 1)
                    for a in range(TT):
                        row = sT[:, hd % 2, 0:P] if a == 0 else sT[:, hd % 2, P:3 * P]
                        at = 2 * hd + a
                        ins = nc.scalar.activation(row, row, ACT.Exp, bias=st[:, 16 + at:17 + at],
                                                   accum_out=st[:, 32 + at:33 + at])
                    ins.then_inc(s.mla_exp, 1)
                if hd >= 1:
                    act.wait_ge(s.mla_turned, hd)
                    if hd >= 3:
                        act.wait_ge(s.mla_pv, hd - 2)
                    nc.scalar.copy(pT[:, (hd - 1) % 2, :], bank[:, 6, 0:3 * P]).then_inc(s.mla_pt, 1)
                if hd % 2 and hd < MH:
                    hi(24 + hd // 2)
            evacuate(proj[:, :, 1536:2048], pair(8), 8, 24, ACT.Silu)
            act.wait_ge(s.ret_o_head, RH)
            nc.scalar.copy(proj[:, :, 0:512], bank[:, 6:8, :]).then_inc(s.ret_copied, 1)
            act.wait_ge(s.ret_centred, 1)
            nc.scalar.activation(xn[:, :, 0:512], proj[:, :, 0:512], ACT.Square).then_inc(s.ret_sq, 1)
            root(3, st[:, 64:80])
            turned_hi(a_hi, 0, KT, s.mixed_turned, 0, lambda k: mix_gain[:, k:k + 1], s.mixed_hi)
            hi(28, 29, 30, 31, 32, 33, 34, 35)
            act.wait_ge(s.acc_free1, 5)
            act.wait_ge(s.acc_free0, 6)
            sum_squares()
            root(4, st[:, 2:4])
            turned_hi(h_hi, 0, KT, s.x_turned, 4, lambda k: column("ffn_norm_w", k), s.h_hi_done)

            def taps(j, e, v):
                for f in range(2):
                    t = 22 * v + f
                    bias, scale = VEC["conv_b"][0] + t, CW2 + t
                    ins = nc.scalar.activation(
                        conv[:, v, e, f * 256:f * 256 + 256], bank[:, 2 * e + v, f * 256:f * 256 + 256], ACT.Identity,
                        bias=vec[:, bass.ds(j * 2 + bias, 1)] if not isinstance(j, int) else
                        vec[:, 2 * j + bias:2 * j + bias + 1],
                        scale=vec[:, bass.ds(j * 2 + scale, 1)] if not isinstance(j, int) else
                        vec[:, 2 * j + scale:2 * j + scale + 1])
                ins.then_inc(s.taps, 1)

            def ff1_chunk(j, e, mm, split1, split2, split3):
                act.wait_ge(s.mm_done, mm)
                taps(j, e, 0)
                split1()
                act.wait_ge(s.mm_done, mm + 2)
                taps(j, e, 1)
                split2()
                act.wait_ge(s.gate_conv, j + 1)
                nc.scalar.activation(silu1[:, e, :], conv[:, 0, e, :], ACT.Silu).then_inc(s.gate_silu, 1)
                act.wait_ge(s.act_ready, j + 1)
                nc.scalar.copy(flat(a_hi[:, 2 * e:2 * e + 2, :]), act1[:, e, :]).then_inc(s.act_hi_done, 1)
                split3()

            n1 = 2 * M_FF1
            ff1_chunk(0, 0, n1 + 2, lambda: hi(n1 + 4, n1 + 5), lambda: hi(n1 + 6, n1 + 7), lambda: None)
            with act.Fori(0, CH1 // 2 - 1) as i:
                for e in range(2):
                    b = n1 + 6 * e
                    ff1_chunk(i * 2 + 1 + e, 1 - e, i * 12 + b + 6, lambda: hi(b + 8, b + 9, i=i),
                              lambda: hi(b + 10, b + 11, i=i), lambda: hi(b + 12, b + 13, i=i))
            b = n1 + 12 * (CH1 // 2 - 1)
            ff1_chunk(CH1 - 2, 1, b + 6, lambda: hi(b + 8, b + 9), lambda: hi(b + 10, b + 11), lambda: hi(b + 12, b + 13))
            ff1_chunk(CH1 - 1, 0, b + 12, lambda: hi(b + 14, b + 15), lambda: hi(b + 16, b + 17),
                      lambda: hi(b + 18, b + 19))
            n2 = 2 * M_IN2
            hi(n2 + 2, n2 + 3)

            act.wait_ge(s.x_added, 1)
            sum_squares()
            root(5, st[:, 2:4])
            act.wait_ge(s.x_added, 2)
            sum_squares()
            root(6, st[:, 2:4])
            turned_hi(h_hi, 0, KT, s.x_turned, 8, lambda k: column("norm1_g_2", k), s.h_hi_done)
            hi(n2 + 4, n2 + 5, n2 + 6, n2 + 7)
            evacuate(gqk[:, 0], pair(C_GLA), C_GLA, n2 + 4)
            hi(n2 + 8, n2 + 9, n2 + 10, n2 + 11)
            evacuate(gqk[:, 1], pair(C_GLA + 1), C_GLA + 1, n2 + 8)
            hi(n2 + 12, n2 + 13)
            evacuate(ga, pair(C_GLA + 2, 16), C_GLA + 2, n2 + 10)
            hi(n2 + 14, n2 + 15, n2 + 16, n2 + 17)
            evacuate(gv[:, :, 0:512], pair(C_GLA + 3), C_GLA + 3, n2 + 14)
            act.wait_ge(s.gla_turned, 2)
            nc.scalar.activation(gqT.rearrange("p (b h) t -> p b (h t)", b=2), bank[:, 4:6, :], ACT.Copy,
                                 scale=GK ** -0.5).then_inc(s.gla_qT, 1)
            hi(n2 + 18, n2 + 19, n2 + 20, n2 + 21)
            evacuate(gv[:, :, 512:1024], pair(C_GLA + 4), C_GLA + 4, n2 + 18)
            act.wait_ge(s.gla_logits, 1)
            for hd in range(GH):
                ins = nc.scalar.activation(z[:, hd * TOKENS:(hd + 1) * TOKENS],
                                           bank[:, 6 + hd // 2, hd % 2 * TOKENS:(hd % 2 + 1) * TOKENS], ACT.Identity,
                                           bias=column("gla_gate_bias_2", hd))
            ins.then_inc(s.gla_z, 1)
            act.wait_ge(s.gla_z, 1)
            link(nc.scalar.activation(soft, z, ACT.Abs))
            link(nc.scalar.activation(soft, soft, ACT.Exp, scale=-1.0))
            nc.scalar.activation(soft, soft, ACT.Ln, bias=1.0).then_inc(s.gla_soft, 1)

            def level_decay(t):
                act.wait_ge(s.gla_diff, t + 1)
                link(nc.scalar.activation(z, z, ACT.Abs))
                nc.scalar.activation(z, z, ACT.Exp, scale=-1.0 / 16).then_inc(s.gla_e, 1)

            def inverse_root(wait, nth, v, done):
                act.wait_ge(wait, nth)
                link(nc.scalar.activation(v, v, ACT.Ln))
                nc.scalar.activation(v, v, ACT.Exp, scale=-0.5).then_inc(done, 1)

            def heads_out(t):
                nth = t // 3 * 2 + t % 3
                act.wait_ge(s.att_turned, 2 * nth + 2)
                dst = (aqT, akT)[t % 3][:, t // 3 * 4:t // 3 * 4 + 4, :]
                nc.scalar.activation(dst.rearrange("p (b k) t -> p b (k t)", b=2), bank[:, 6:8, :], ACT.Copy,
                                     scale=qkg[:, t % 3:t % 3 + 1]).then_inc(s.att_T, 1)

            level_decay(0)
            act.wait_ge(s.qkg_scaled, 1)
            for t in range(3 * AG):
                n = n2 + 18 + 4 * t
                if t + 1 < LEVELS + 1:
                    level_decay(t + 1)
                hi(n + 4, n + 5, n + 6, n + 7)
                g, part = t // 3, t % 3
                dst = av[:, :, g * 512:g * 512 + 512] if part == 2 else a_tok[:, part]
                evacuate(dst, pair(C_ATT + t), C_ATT + t, n + 4)
                if part < 2:
                    nth = 2 * g + part
                    c = C_ATT + t
                    act.wait_ge(acc_free[c % 2], c // 2 + 1)
                    nc.scalar.activation(asq, a_tok[:, part], ACT.Square).then_inc(s.att_squared, 1)
                    inverse_root(s.att_ms, nth + 1, st[:, 48:64], s.att_root)
                if t >= 1 and (t - 1) % 3 < 2:
                    heads_out(t - 1)
            for a in range(TT):
                act.wait_ge(s.gla_o, a + 1)
                nc.scalar.copy(go[:, a, :], flat(bank[:, 4 + 2 * a:6 + 2 * a, :])).then_inc(s.gla_go, 1)
            hi(2 * M_R + 4)
            act.wait_ge(s.gla_go, 2)
            for a in range(TT):
                for hd in range(GH):
                    at = 16 + GH * a + hd
                    ins = nc.scalar.activation(silu_r[:, a, hd * GV:(hd + 1) * GV], go[:, a, hd * GV:(hd + 1) * GV], ACT.Square,
                                               accum_out=st[:, at:at + 1])
            ins.then_inc(s.gla_ssq, 1)
            inverse_root(s.gla_ms, 1, st[:, 16:24], s.gla_norm)

            def filled(f):
                hi(2 * M_R + 4 + f)
                if f % 4 != 3:
                    return
                mm, c = 2 * M_R + f + 1, C_R + f // 4
                if f < 8:
                    evacuate(silu_r[:, :, f // 4 * 512:f // 4 * 512 + 512], pair(c), c, mm, ACT.Silu)
                    return
                act.wait_ge(s.mm_done, mm)
                for t in range(4):
                    k = (f - 8) // 4 * 4 + t
                    ins = nc.scalar.activation(gates[k // KT][:, k % KT, :], bank[:, 2 * (c % 2) + t // 2,
                                                                                   t % 2 * 256:t % 2 * 256 + 256],
                                               ACT.Sigmoid, bias=column("branch_gate_bias_2", k))
                ins.then_inc(acc_free[c % 2], 1)

            def weights_back(u, part):
                done = (u if u < AH else AH + 2 * (u - AH)) + part
                act.wait_ge(s.att_turnedp, done + 1)
                if u >= 2:
                    act.wait_ge(s.att_pv, u - 1)
                nc.scalar.copy(ppT[:, u % 2, 3 * P * part:3 * P * (part + 1)], bank[:, 6, 0:3 * P]).then_inc(s.att_pt, 1)

            f = 1
            for u in range(2 * AH):
                keys = AG * (u // AH + 1) * P
                act.wait_ge(s.att_max, u + 1)
                nc.scalar.activation(p[:, u % 2, 0:keys], p[:, u % 2, 0:keys], ACT.Exp, bias=st[:, 32 + u:33 + u],
                                     accum_out=st[:, 80 + u:81 + u]).then_inc(s.att_exp, 1)
                if u > 0:
                    filled(f)
                    f += 1
                weights_back(u, 0)
                if u >= AH:
                    filled(f)
                    f += 1
                    weights_back(u, 1)
            turned_hi(a_hi, 4, 4, s.go_turned, 0, lambda k: column("gla_out_norm_g_2", k % 2), s.go_hi)
            turned_hi(a_hi, 0, 4, s.oa_turned, 0, lambda k: 1.0, s.oa_hi, 6)
            turned_hi(a_hi, 8, 4, s.go_turned, 2, lambda k: column("gla_out_norm_g_2", k % 2), s.go_hi)
            n = 2 * M_BR

            def mixed_hi(q):
                act.wait_ge(s.mix_ready, q + 1)
                nc.scalar.copy(flat(h_hi[:, 2 * q:2 * q + 2, :]), mix[:, 0, q % 2, :]).then_inc(s.mix_hi, 1)

            hi(n + 4, n + 5, n + 6, n + 7)
            mixed_hi(0)
            hi(n + 8, n + 9)
            mixed_hi(1)
            hi(n + 10, n + 11, n + 12, n + 13)
            mixed_hi(2)
            hi(n + 14, n + 15)
            mixed_hi(3)
            hi(*range(n + 16, n + 24))
            act.wait_ge(s.acc_free1, 18)
            act.wait_ge(s.acc_free0, 19)
            sum_squares()
            root(7, st[:, 2:4])
            turned_hi(h_hi, 0, KT, s.x_turned, 12, lambda k: column("norm2_g_2", k), s.h_hi_done)

            def ff2_chunk(j, e, mm, split1, split2):
                act.wait_ge(s.mm_done, mm)
                nc.scalar.activation(relu2[:, e, :], bank[:, e, :], ACT.Relu).then_inc(s.up_relu, 1)
                split1()
                act.wait_ge(s.up_square, j + 1)
                nc.scalar.copy(flat(a_hi[:, 2 * e:2 * e + 2, :]), square2[:, e, :]).then_inc(s.up_hi, 1)
                split2()

            n3 = 2 * M_FF2
            ff2_chunk(0, 0, n3 + 2, lambda: hi(n3 + 4, n3 + 5), lambda: None)
            with act.Fori(0, CH2 // 3 - 1) as i:
                for e in range(3):
                    b = n3 + 4 * e
                    ff2_chunk(i * 3 + e + 1, (e + 1) % 3, i * 12 + b + 4, lambda: hi(b + 6, b + 7, i=i),
                              lambda: hi(b + 8, b + 9, i=i))
            for e in range(3):
                b = n3 + 12 * (CH2 // 3 - 1) + 4 * e
                ff2_chunk(CH2 - 3 + e, (e + 1) % 3, b + 4, lambda: hi(b + 6, b + 7),
                          (lambda: hi(b + 8, b + 9)) if e < 2 else (lambda: None))

        @block.vector
        def _(dve):
            chain = [0]

            def link(ins):
                chain[0] += 1
                ins.then_inc(s.dve_chain, 1)
                dve.wait_ge(s.dve_chain, chain[0])

            def lo(*ns, i=None):
                for n in ns:
                    _, size, cols = table[n // 2] if n // 2 in table else (None, HALF, ffn_columns(n // 2))
                    dve.wait_ge(s.hi_done, n + 1 if i is None else i * 12 + n + 1)
                    dst, h = w_lo[:, n % RING, 0:size], w_hi[:, n % RING, 0:size].bitcast(F32)
                    if cols:
                        dst = dst.rearrange("p (k c) -> p k c", c=cols // 2)
                        h = h.rearrange("p (k c) -> p k c", c=cols // 2)
                    nc.vector.tensor_tensor(dst, raw_half(n // 2 % RAW, n % 2, size, cols), h, ALU.subtract).then_inc(
                        s.lo_done, 1)

            def mean_square(dst, src, width):
                return nc.vector.tensor_scalar(dst, src, 1.0 / width, EPS, ALU.mult, ALU.add)

            def inverse_rms(ssq, root):
                dve.wait_ge(s.ssq, ssq)
                mean_square(st[:, 2:4], st[:, 0:2], D).then_inc(s.rms_ms, 1)
                dve.wait_ge(s.rms_root, root)
                link(nc.vector.reciprocal(st[:, 2:4], st[:, 2:4]))

            def scale_x():
                for a in range(TT):
                    nc.vector.tensor_scalar(xn[:, a, :], x[:, a, :], st[:, 2 + a:3 + a], None, ALU.mult).then_inc(
                        s.x_scaled, 1)

            def turned_lo(dst, dst_hi, at, count, hi_done, before, gain, done, first=4):
                for k in range(count):
                    if k % 2 == 0:
                        dve.wait_ge(hi_done, before + k // 2 + 1)
                    ins = nc.vector.scalar_tensor_tensor(
                        dst[:, at + k, :], bank[:, first + k // 2, k % 2 * 256:k % 2 * 256 + 256], gain(k),
                        dst_hi[:, at + k, :].bitcast(F32), ALU.mult, ALU.subtract)
                    if k % 2 == 1 or k == count - 1:
                        ins.then_inc(done, 1)

            def rotate(t, heads, width, lane):
                half = width // 2
                for a in range(TT):
                    x1, x2 = t[:, a, :, 0:half], t[:, a, :, half:width]
                    cos, sin = [angle[:, f, a, lane:lane + half].rearrange("p (o f) -> p o f", o=1).to_broadcast(
                        [P, heads, half]) for f in range(2)]
                    t1, t2 = [rope_tmp[:, f, 0:heads * half].rearrange("p (h f) -> p h f", f=half) for f in range(2)]
                    nc.vector.tensor_tensor(t1, x1, sin, ALU.mult)
                    nc.vector.tensor_tensor(t2, x2, sin, ALU.mult)
                    nc.vector.tensor_tensor(x1, x1, cos, ALU.mult)
                    link(nc.vector.tensor_tensor(x2, x2, cos, ALU.mult))
                    nc.vector.tensor_tensor(x1, x1, t2, ALU.subtract)
                    ins = nc.vector.tensor_tensor(x2, x2, t1, ALU.add)
                    if a == 0:
                        link(ins)
                return ins

            nc.vector.memset(mix_gain[:, 4:8], 1.0)
            inverse_rms(1, 1)
            scale_x()
            dve.wait_ge(s.vecs_turned, 1)
            nc.vector.tensor_copy(vec[:], bank[:, 3, 0:VROWS + 132]).then_inc(s.vecs_ready, 1)
            lo(0, 1, 2, 3)
            dve.wait_ge(s.vecs_ready, 1)
            nc.vector.tensor_copy(mix_gain[:, 0:4], vec[:, VEC["ret_gn_w"][0]:VEC["ret_gn_w"][0] + 4])
            turned_lo(h_lo, h_hi, 0, KT, s.h_hi_done, 0, lambda k: column("attn_norm_w", k), s.h_lo_done)
            dve.wait_ge(s.pos_in, 48)
            link(nc.vector.tensor_copy(pos_f, pos_i.bitcast(I32)))
            for a in range(TT):
                for t in range(2):
                    ins = nc.vector.tensor_scalar(angle[:, t, a, :], invf, pos_f[:, a:a + 1], None, ALU.mult)
            link(ins)
            for t, turn_ in enumerate((0.25, 0.0)):
                ins = nc.vector.tensor_scalar(turns[:, t], angle[:, t], 0.15915494309189535, turn_, ALU.mult, ALU.add)
            link(ins)
            angle_f, turns_f = area(25280, 4 * 48), area(25472, 4 * 48)
            link(nc.vector.tensor_scalar(turns_f, turns_f, MAGIC, None, ALU.add))
            link(nc.vector.tensor_scalar(turns_f, turns_f, MAGIC, None, ALU.subtract))
            for part in TWO_PI:
                link(nc.vector.scalar_tensor_tensor(angle_f, turns_f, -part, angle_f, ALU.mult, ALU.add))
            link(nc.vector.tensor_scalar(angle[:, 0], angle[:, 0], 1.5707963267948966, None, ALU.add))
            nc.vector.tensor_scalar(angle_f, angle_f, 3.1415925, -3.1415925, ALU.min, ALU.max).then_inc(s.trig_arg, 1)
            lo(4, 5, 6, 7)
            dve.wait_ge(s.ssq, 2)
            mean_square(st[:, 4:6], st[:, 4:6], QR)
            mean_square(st[:, 6:8], st[:, 6:8], KVR).then_inc(s.rms_ms, 1)
            dve.wait_ge(s.rms_root, 2)
            link(nc.vector.reciprocal(st[:, 4:8], st[:, 4:8]))
            for a in range(TT):
                nc.vector.tensor_scalar(proj[:, a, 2048:2304], proj[:, a, 2048:2304], st[:, 4 + a:5 + a], None, ALU.mult)
                ins = nc.vector.tensor_scalar(proj[:, a, 2304:2432], proj[:, a, 2304:2432], st[:, 6 + a:7 + a], None,
                                              ALU.mult)
            ins.then_inc(s.latent_scaled, 1)
            lo(8, 9, 10, 11)
            turned_lo(a_lo, a_hi, 0, 3, s.latents_hi, 0,
                      lambda k: column("mla_q_norm_w", k) if k < 2 else column("mla_kv_norm_w"), s.latents_lo)
            dve.wait_ge(s.trig, 1)
            link(rotate(proj[:, :, 2432:2464].rearrange("p a (h c) -> p a h c", h=1), 1, PE_D, 32))
            for a in range(TT):
                nc.vector.tensor_copy(k_tok[:, a, :, NOPE:QK], proj[:, a, 2432:2464].rearrange(
                    "p (o c) -> p o c", o=1).to_broadcast([P, MH, PE_D]))
            lo(12, 13)
            dve.wait_ge(s.acc_free0, 2)
            dve.wait_ge(s.acc_free1, 2)
            rotate(q_tok[:, :, :, NOPE:QK], MH, PE_D, 32).then_inc(s.mla_q_ready, 1)
            lo(14, 15)
            for a in range(TT):
                dve.wait_ge(acc_free[a], 3)
                ins = nc.vector.tensor_copy(k_tok[:, a, :, 0:NOPE], kv[:, a, :, 0:NOPE])
            ins.then_inc(s.mla_k_ready, 1)
            lo(16, 17)
            dve.wait_ge(s.mla_q_ready, 1)
            link(rotate(proj[:, :, 0:512].rearrange("p a (h c) -> p a h c", c=RD), RH, RD, 0))
            lo(18, 19)
            for r in range(4):
                dve.wait_ge(s.mla_k_turned, r + 1)
                nc.vector.tensor_copy(flat(mkT[0:QK, 2 * r:2 * r + 2, :]), bank[0:QK, 4 + r, :]).then_inc(s.mla_kT, 1)
            dve.wait_ge(s.acc_free0, 4)
            rotate(proj[:, :, 512:1024].rearrange("p a (h c) -> p a h c", c=RD), RH, RD, 0).then_inc(s.ret_roped, 1)
            lo(20, 21, 22, 23)
            for b in range(2):
                dve.wait_ge(s.ret_k_turned, b + 1)
                nc.vector.tensor_copy(flat(rkT[:, 2 * b:2 * b + 2, :]), bank[:, 6 + b, :]).then_inc(s.ret_kT, 1)

            def mla_out(r):
                dve.wait_ge(s.mla_pv, 4 * r + 4)
                at = 32 + 8 * r
                link(nc.vector.reciprocal(st[:, at:at + 8], st[:, at:at + 8]))
                o = bank[:, 7, :].rearrange("p (h a c) -> p a h c", h=4, a=2)
                inv = st[:, at:at + 8].rearrange("p (h a o) -> p a h o", a=2, o=1)
                for a in range(TT):
                    ins = nc.vector.tensor_tensor(
                        proj[:, a, 512 + 256 * r:768 + 256 * r].rearrange("p (h c) -> p h c", c=MV),
                        o[:, a], inv[:, a].to_broadcast([P, 4, MV]), ALU.mult)
                ins.then_inc(s.mla_o, 1)

            dve.wait_ge(s.consts_in, 32)
            for hd in range(MH):
                dve.wait_ge(s.mla_scores, hd + 1)
                if hd >= 2:
                    dve.wait_ge(s.mla_turned, hd - 1)
                nc.vector.tensor_tensor(sT[:, hd % 2, :], bank[:, 4 + hd % 2, 0:3 * P], causal, ALU.add).then_inc(
                    s.mla_masked, 1)
                dve.wait_ge(s.mla_masked, hd + 1)
                at = 16 + 2 * hd
                nc.vector.tensor_reduce(st[:, at:at + 1], sT[:, hd % 2, 0:P], AX.X, ALU.max, negate=True)
                nc.vector.tensor_reduce(st[:, at + 1:at + 2], sT[:, hd % 2, P:3 * P], AX.X, ALU.max,
                                        negate=True).then_inc(s.mla_max, 1)
                if hd in (2, 4, 6):
                    lo(23 + hd // 2)
                if hd == 5:
                    mla_out(0)
            lo(27)
            mla_out(1)
            for hd in range(RH):
                dve.wait_ge(s.ret_scores, hd + 1)
                if hd >= 2:
                    dve.wait_ge(s.ret_o_head, hd - 1)
                nc.vector.tensor_tensor(sT[:, hd % 2, :], bank[:, 4 + hd % 2, 0:3 * P], decay[:, hd, :],
                                        ALU.mult).then_inc(s.ret_masked, 1)
            oh = proj[:, :, 0:512].rearrange("p a (h c) -> p a h c", c=RD)
            mean = st[:, 48:64].rearrange("p (a h o) -> p a h o", a=2, o=1)
            var = st[:, 64:80].rearrange("p (a h o) -> p a h o", a=2, o=1)
            dve.wait_ge(s.ret_copied, 1)
            link(nc.vector.tensor_reduce(st[:, 48:64].rearrange("p (a h) -> p a h", a=2), oh, AX.X, ALU.add))
            link(nc.vector.tensor_scalar(st[:, 48:64], st[:, 48:64], -1.0 / RD, None, ALU.mult))
            for a in range(TT):
                ins = nc.vector.tensor_tensor(oh[:, a], oh[:, a], mean[:, a].to_broadcast([P, RH, RD]), ALU.add)
            ins.then_inc(s.ret_centred, 1)
            dve.wait_ge(s.ret_sq, 1)
            link(nc.vector.tensor_reduce(st[:, 64:80].rearrange("p (a h) -> p a h", a=2),
                                         xn[:, :, 0:512].rearrange("p a (h c) -> p a h c", c=RD), AX.X, ALU.add))
            mean_square(st[:, 64:80], st[:, 64:80], RD).then_inc(s.rms_ms, 1)
            dve.wait_ge(s.acc_free0, 5)
            link(nc.vector.tensor_tensor(proj[:, :, 0:512], proj[:, :, 0:512], proj[:, :, 1536:2048], ALU.mult))
            dve.wait_ge(s.rms_root, 3)
            link(nc.vector.reciprocal(st[:, 64:80], st[:, 64:80]))
            for a in range(TT):
                ins = nc.vector.tensor_tensor(oh[:, a], oh[:, a], var[:, a].to_broadcast([P, RH, RD]), ALU.mult)
            ins.then_inc(s.ret_y, 1)
            turned_lo(a_lo, a_hi, 0, KT, s.mixed_hi, 0, lambda k: mix_gain[:, k:k + 1], s.mixed_lo)

            def add_chunk(c, first, mm):
                dve.wait_ge(s.mm_done, mm)
                xc = x[:, :, 512 * (c - first):512 * (c - first) + 512]
                nc.vector.tensor_tensor(xc, pair(c), xc, ALU.add).then_inc(acc_free[c % 2], 1)

            lo(28, 29, 30, 31)
            add_chunk(C_OUT, C_OUT, 28)
            lo(32, 33, 34, 35)
            add_chunk(C_OUT + 1, C_OUT, 32)
            inverse_rms(3, 4)
            scale_x()
            turned_lo(h_lo, h_hi, 0, KT, s.h_hi_done, 4, lambda k: column("ffn_norm_w", k), s.h_lo_done)

            def tap(j, row):
                return vec[:, 2 * j + row:2 * j + row + 1] if isinstance(j, int) else vec[:, bass.ds(j * 2 + row, 1)]

            def convolve(j, e, v):
                dve.wait_ge(s.taps, j * 2 + v + 1)
                for f in range(2):
                    u, y = bank[:, 2 * e + v, f * 256:f * 256 + 256], conv[:, v, e, f * 256:f * 256 + 256]
                    ins = nc.vector.scalar_tensor_tensor(y[:, 1:256], u[:, 0:255], tap(j, CW1 + 22 * v + f), y[:, 1:256],
                                                         ALU.mult, ALU.add)
                ins.then_inc(s.tap1, 1)
                dve.wait_ge(s.tap1, j * 2 + v + 1)
                for f in range(2):
                    u, y = bank[:, 2 * e + v, f * 256:f * 256 + 256], conv[:, v, e, f * 256:f * 256 + 256]
                    ins = nc.vector.scalar_tensor_tensor(y[:, 2:256], u[:, 0:254], tap(j, CW0 + 22 * v + f), y[:, 2:256],
                                                         ALU.mult, ALU.add)
                ins.then_inc((s.gate_conv, s.val_conv)[v], 1)

            def ff1_chunk(j, e, split1, split2, split3):
                convolve(j, e, 0)
                split1()
                convolve(j, e, 1)
                split2()
                dve.wait_ge(s.gate_silu, j + 1)
                dve.wait_ge(s.val_conv, j + 1)
                nc.vector.tensor_tensor(act1[:, e, :], silu1[:, e, :], conv[:, 1, e, :], ALU.mult).then_inc(s.act_ready, 1)
                dve.wait_ge(s.act_hi_done, j + 1)
                nc.vector.tensor_tensor(flat(a_lo[:, 2 * e:2 * e + 2, :]), act1[:, e, :],
                                        flat(a_hi[:, 2 * e:2 * e + 2, :]).bitcast(F32), ALU.subtract).then_inc(
                                            s.act_lo_done, 1)
                split3()

            n1 = 2 * M_FF1
            ff1_chunk(0, 0, lambda: lo(n1 + 4, n1 + 5), lambda: lo(n1 + 6, n1 + 7), lambda: None)
            with dve.Fori(0, CH1 // 2 - 1) as i:
                for e in range(2):
                    b = n1 + 6 * e
                    ff1_chunk(i * 2 + 1 + e, 1 - e, lambda: lo(b + 8, b + 9, i=i), lambda: lo(b + 10, b + 11, i=i),
                              lambda: lo(b + 12, b + 13, i=i))
            b = n1 + 12 * (CH1 // 2 - 1)
            ff1_chunk(CH1 - 2, 1, lambda: lo(b + 8, b + 9), lambda: lo(b + 10, b + 11), lambda: lo(b + 12, b + 13))
            ff1_chunk(CH1 - 1, 0, lambda: lo(b + 14, b + 15), lambda: lo(b + 16, b + 17), lambda: lo(b + 18, b + 19))
            n2 = 2 * M_IN2
            lo(n2 + 2, n2 + 3)

            def add_down(mm):
                dve.wait_ge(s.mm_done, mm)
                for a in range(TT):
                    ins = nc.vector.tensor_tensor(x[:, a, :], flat(bank[:, 4 + 2 * a:6 + 2 * a, :]), x[:, a, :], ALU.add)
                    if a == 1 or mm == 2 * M_END:
                        ins.then_inc(s.x_added, 1)

            add_down(2 * M_IN2)
            inverse_rms(4, 5)
            dve.wait_ge(s.fw_in, 16)
            for a in range(TT):
                ins = nc.vector.scalar_tensor_tensor(x[:, a, :], x[:, a, :], st[:, 2 + a:3 + a], fw, ALU.mult, ALU.mult)
            ins.then_inc(s.x_added, 1)
            inverse_rms(5, 6)
            scale_x()
            turned_lo(h_lo, h_hi, 0, KT, s.h_hi_done, 8, lambda k: column("norm1_g_2", k), s.h_lo_done)
            lo(*range(n2 + 4, n2 + 18))
            act_q = qkg[:, 0:1]
            dve.wait_ge(s.qkg_in, 64)
            nc.vector.tensor_scalar(act_q, act_q, AD ** -0.5, None, ALU.mult).then_inc(s.qkg_scaled, 1)
            dve.wait_ge(s.gla_turned, 4)
            nc.vector.tensor_copy(gkT.rearrange("p (b h) t -> p b (h t)", b=2), bank[:, 6:8, :]).then_inc(s.gla_kT, 1)
            lo(n2 + 18, n2 + 19)
            dve.wait_ge(s.pa_turned, 1)
            nc.vector.tensor_copy(paT[0:16, :], bank[0:16, 4, 0:TOKENS]).then_inc(s.pa_T, 1)
            lo(n2 + 20, n2 + 21)
            link(nc.vector.memset(resets, 1.0))
            nc.vector.memset(resets.rearrange("p (n t) -> p n t", t=P)[:, :, 0:1], 0.0)
            dve.wait_ge(s.gla_soft, 1)
            link(nc.vector.scalar_tensor_tensor(z, z, 0.0, soft, ALU.min, ALU.subtract))
            link(nc.vector.tensor_tensor_scan(run, resets, z, 0.0, ALU.mult, ALU.add))
            nc.vector.memset(g_in, 0.0)

            def level_distance(t):
                if t == 0:
                    r, d = [v.rearrange("p (h a t) -> p h a t", a=2, t=P) for v in (run, z)]
                    nc.vector.tensor_tensor(d[:, :, 0, :], r[:, :, 0, :], r[:, :, 0, P - 1:P].to_broadcast([P, GH, P]),
                                            ALU.subtract)
                    nc.vector.tensor_copy(d[:, :, 1, :], r[:, :, 1, :]).then_inc(s.gla_diff, 1)
                    return
                b = 2 << (LEVELS - t)
                r, d = [v.rearrange("p (n t) -> p n t", t=b) for v in (run, z)]
                nc.vector.tensor_tensor(d, r, r[:, :, b // 2 - 1:b // 2].to_broadcast([P, GH * TOKENS // b, b]),
                                        ALU.subtract).then_inc(s.gla_diff, 1)

            level_distance(0)
            dve.wait_ge(s.levels_in, 16)
            for t in range(3 * AG):
                n = n2 + 18 + 4 * t
                if t <= LEVELS:
                    dve.wait_ge(s.gla_e, t + 1)
                    nc.vector.tensor_tensor(flat(qe), flat(gqT), z, ALU.mult)
                    nc.vector.tensor_tensor(flat(ke), flat(gkT), z, ALU.mult).then_inc(s.gla_qe, 1)
                if t + 1 <= LEVELS:
                    dve.wait_ge(s.gla_qe, t + 1)
                    level_distance(t + 1)
                lo(n + 4, n + 5, n + 6, n + 7)
                if t % 3 < 2:
                    nth = 2 * (t // 3) + t % 3
                    if nth >= 1:
                        dve.wait_ge(s.att_scaled, nth)
                    dve.wait_ge(s.att_squared, nth + 1)
                    v = st[:, 48:64].rearrange("p (a h) -> p a h", a=2)
                    link(nc.vector.tensor_reduce(v, asq.rearrange("p a (h c) -> p a h c", c=AD), AX.X, ALU.add))
                    mean_square(st[:, 48:64], st[:, 48:64], AD).then_inc(s.att_ms, 1)
                dve.wait_ge(s.gla_level, t + 1)
                if t == 0:
                    nc.vector.tensor_copy(flat(g_cross), bank[:, 4, :]).then_inc(s.gla_taken, 1)
                else:
                    lv = LEVELS if t == 8 else LEVELS - t
                    mask = levels[:, lv:lv + 1, :].bitcast(I32).to_broadcast([P, 8, P])
                    nc.vector.copy_predicated(g_in.rearrange("p h a t -> p (h a) t"), mask,
                                              bank[:, 4:6, :].rearrange("p b (n t) -> p (b n) t", t=P)).then_inc(
                                                  s.gla_taken, 1)
                if t % 3 < 2:
                    dve.wait_ge(s.att_root, nth + 1)
                    r = st[:, 48:64].rearrange("p (a h o) -> p a h o", a=2, o=1)
                    for a in range(TT):
                        v = a_tok[:, t % 3, a, :].rearrange("p (h c) -> p h c", c=AD)
                        ins = nc.vector.tensor_tensor(v, v, r[:, a].to_broadcast([P, AH, AD]), ALU.mult)
                    ins.then_inc(s.att_scaled, 1)
            lo(2 * M_R + 4)
            dve.wait_ge(s.gla_ssq, 1)
            mean_square(st[:, 16:24], st[:, 16:24], GV).then_inc(s.gla_ms, 1)
            dve.wait_ge(s.gla_norm, 1)
            r = st[:, 16:24].rearrange("p (a h o) -> p a h o", a=2, o=1)
            for a in range(TT):
                v = go[:, a, :].rearrange("p (h c) -> p h c", c=GV)
                ins = nc.vector.tensor_tensor(v, v, r[:, a].to_broadcast([P, GH, GV]), ALU.mult)
            link(ins)

            def att_out(a):
                dve.wait_ge(s.att_pv, AH * (a + 1))
                sums = st[:, 80 + AH * a:88 + AH * a]
                link(nc.vector.reciprocal(sums, sums))
                nc.vector.tensor_tensor(oa[:, a, :].rearrange("p (h c) -> p h c", c=AD),
                                        bank[:, 7, :].rearrange("p (h c) -> p h c", c=AD),
                                        sums.rearrange("p (h o) -> p h o", o=1).to_broadcast([P, AH, AD]),
                                        ALU.mult).then_inc(s.att_o, 1)

            dve.wait_ge(s.dil_in, 16)
            f = 1
            for u in range(2 * AH):
                a = u // AH
                keys = AG * (a + 1) * P
                dve.wait_ge(s.att_scores, u + 1)
                if u >= 2:
                    dve.wait_ge(s.att_turnedp, u - 1 if u - 2 < AH else AH + 2 * (u - 2 - AH) + 2)
                src = bank[:, 4 + u % 2, 0:keys] if a == 0 else flat(bank[:, 4:6, :])[:, 0:keys]
                nc.vector.tensor_tensor(p[:, u % 2, 0:keys], src, dil[:, 3 * P * a:3 * P * a + keys],
                                        ALU.add).then_inc(s.att_masked, 1)
                dve.wait_ge(s.att_masked, u + 1)
                nc.vector.tensor_reduce(st[:, 32 + u:33 + u], p[:, u % 2, 0:keys], AX.X, ALU.max,
                                        negate=True).then_inc(s.att_max, 1)
                for _ in range((u > 0) + (u >= AH)):
                    lo(2 * M_R + 4 + f)
                    f += 1
                if u == AH:
                    att_out(0)
                    dve.wait_ge(acc_free[C_R % 2], C_R // 2 + 1)
                    dve.wait_ge(acc_free[(C_R + 1) % 2], (C_R + 1) // 2 + 1)
                    nc.vector.tensor_tensor(go, go, silu_r, ALU.mult).then_inc(s.gla_ready, 1)
            att_out(1)
            turned_lo(a_lo, a_hi, 4, 4, s.go_hi, 0, lambda k: column("gla_out_norm_g_2", k % 2), s.go_lo)
            turned_lo(a_lo, a_hi, 0, 4, s.oa_hi, 0, lambda k: 1.0, s.oa_lo, 6)
            turned_lo(a_lo, a_hi, 8, 4, s.go_hi, 2, lambda k: column("gla_out_norm_g_2", k % 2), s.go_lo)
            n = 2 * M_BR

            def mixed(q, mm):
                c = C_BR + q
                dve.wait_ge(s.mm_done, mm)
                for br in range(2):
                    ins = nc.vector.tensor_tensor(mix[:, br, q % 2, :], flat(gates[br][:, 2 * q:2 * q + 2, :]),
                                                  bank[:, 2 * (c % 2) + br, :], ALU.mult)
                ins.then_inc(acc_free[c % 2], 1)
                dve.wait_ge(acc_free[c % 2], c // 2 + 1)
                nc.vector.tensor_tensor(mix[:, 0, q % 2, :], mix[:, 0, q % 2, :], mix[:, 1, q % 2, :],
                                        ALU.add).then_inc(s.mix_ready, 1)
                dve.wait_ge(s.mix_hi, q + 1)
                nc.vector.tensor_tensor(flat(h_lo[:, 2 * q:2 * q + 2, :]), mix[:, 0, q % 2, :],
                                        flat(h_hi[:, 2 * q:2 * q + 2, :]).bitcast(F32), ALU.subtract).then_inc(s.mix_lo, 1)

            lo(n + 4, n + 5, n + 6, n + 7)
            mixed(0, n + 4)
            lo(n + 8, n + 9)
            mixed(1, n + 6)
            lo(n + 10, n + 11, n + 12, n + 13)
            mixed(2, n + 10)
            lo(n + 14, n + 15)
            mixed(3, n + 12)
            lo(*range(n + 16, n + 20))
            add_chunk(C_OUT2, C_OUT2, 2 * M_OUT2 + 4)
            lo(*range(n + 20, n + 24))
            add_chunk(C_OUT2 + 1, C_OUT2, 2 * M_OUT2 + 8)
            inverse_rms(6, 7)
            scale_x()
            turned_lo(h_lo, h_hi, 0, KT, s.h_hi_done, 12, lambda k: column("norm2_g_2", k), s.h_lo_done)

            def ff2_chunk(j, e, split1, split2):
                dve.wait_ge(s.up_relu, j + 1)
                nc.vector.tensor_tensor(square2[:, e, :], relu2[:, e, :], relu2[:, e, :], ALU.mult).then_inc(
                    s.up_square, 1)
                split1()
                dve.wait_ge(s.up_hi, j + 1)
                nc.vector.tensor_tensor(flat(a_lo[:, 2 * e:2 * e + 2, :]), square2[:, e, :],
                                        flat(a_hi[:, 2 * e:2 * e + 2, :]).bitcast(F32), ALU.subtract).then_inc(
                                            s.up_lo, 1)
                split2()

            n3 = 2 * M_FF2
            ff2_chunk(0, 0, lambda: lo(n3 + 4, n3 + 5), lambda: None)
            with dve.Fori(0, CH2 // 3 - 1) as i:
                for e in range(3):
                    b = n3 + 4 * e
                    ff2_chunk(i * 3 + e + 1, (e + 1) % 3, lambda: lo(b + 6, b + 7, i=i), lambda: lo(b + 8, b + 9, i=i))
            for e in range(3):
                b = n3 + 12 * (CH2 // 3 - 1) + 4 * e
                ff2_chunk(CH2 - 3 + e, (e + 1) % 3, lambda: lo(b + 6, b + 7),
                          (lambda: lo(b + 8, b + 9)) if e < 2 else (lambda: None))
            add_down(2 * M_END)


def kernel(**inputs):
    import concourse.bacc as bacc
    from concourse.bass_utils import run_bass_kernel_spmd

    nc = bacc.Bacc("TRN2", target_bir_lowering=False, num_devices=1)
    arrays, aps = {}, {}
    for name in PARTS:
        a = np.ascontiguousarray(inputs[name])
        arrays[f"in_{name}"] = a
        aps[name] = nc.dram_tensor(f"in_{name}", a.shape, mybir.dt.from_np(a.dtype), kind="ExternalInput").ap()
    arrays["constants"] = constants()
    consts = nc.dram_tensor("constants", (P, C_END), F32, kind="ExternalInput").ap()
    out = nc.dram_tensor("out", (1, TOKENS, D), F32, kind="ExternalOutput").ap()
    two_blocks_kernel(nc, Parts(**aps), consts, out)
    result = run_bass_kernel_spmd(nc, [arrays], core_ids=[0])
    return result.results[0]["out"]
```

```python
from collections import namedtuple
from contextlib import ExitStack

import numpy as np

import concourse.bass as bass
from concourse import mybir

P = 128
F32 = mybir.dt.float32
F32R = mybir.dt.float32r
I32 = mybir.dt.int32
ALU = mybir.AluOpType
ACT = mybir.ActivationFunctionType
AX = mybir.AxisListType

TOKENS, D = 256, 1024
TT = TOKENS // P
KT = D // P
EPS = 1e-6
RAW, RING = 3, 4
HALF = 1024

RH, RD = 8, 64
RW = RH * RD
MH, NOPE, PE_D, MV = 8, 64, 32, 64
QK = NOPE + PE_D
QR, KVR = 256, 128
FF1 = 2816
CH1 = FF1 // 256
AH, AG, AD = 8, 3, 64
DIL = (1, 4, 16)
GH, GK, GV = 4, 128, 256
FF2 = 4096
CH2 = FF2 // 256
AQ0 = 0
AW = AG * AH * AD
GQ0 = 3 * AW
GK0, GV0 = GQ0 + 512, GQ0 + 1024
GR0 = GV0 + 1024
GA0 = GR0 + 1024
GG0 = GA0 + 16

NEG = -1e30
LEVELS = 7

VEC = {}
_r = 0
for _name, _n in (("attn_norm_w", 8), ("ffn_norm_w", 8), ("norm1_g_2", 8), ("norm2_g_2", 8),
                  ("branch_gate_bias_2", 16), ("ret_gn_w", 4), ("ones", 4), ("mla_q_norm_w", 2), ("mla_kv_norm_w", 1),
                  ("gla_gate_bias_2", 4), ("gla_out_norm_g_2", 2), ("final_norm_w", 8),
                  ("attn_q_norm_g_2", 1), ("attn_k_norm_g_2", 1), ("conv_b", 44), ("conv_w", 132)):
    VEC[_name] = (_r, _n)
    _r += _n
VCOLS = _r
CW0 = VEC["conv_w"][0]
CW1, CW2 = CW0 + 44, CW0 + 88

C_IDENT = 0
C_INVF = C_IDENT + P
C_CAUSAL = C_INVF + 48
C_DECAY = C_CAUSAL + 3 * P
C_DIL = C_DECAY + RH * 3 * P
C_LEVEL = C_DIL + 9 * P
C_END = C_LEVEL + (LEVELS + 1) * P


def constants():
    t = np.zeros((P, C_END), np.float32)
    t[:, C_IDENT:C_IDENT + P] = np.eye(P)
    t[:, C_INVF:C_INVF + 32] = 10000.0 ** (-np.arange(0, 64, 2) / 64)
    t[:, C_INVF + 32:C_INVF + 48] = 10000.0 ** (-np.arange(0, 32, 2) / 32)
    i = np.arange(P)
    late = np.where(i[None, :] <= i[:, None], 0.0, NEG)
    t[:, C_CAUSAL:C_CAUSAL + P] = late
    t[:, C_CAUSAL + 2 * P:C_CAUSAL + 3 * P] = late
    for h in range(RH):
        log_gamma = np.log1p(-(2.0 ** (-5.0 - h)))
        for n, shift in enumerate((0, P, 0)):
            d = shift + i[None, :] - i[:, None]
            at = C_DECAY + (3 * h + n) * P
            t[:, at:at + P] = np.where(d >= 0, np.exp(log_gamma * np.maximum(d, 0)), 0) * RD ** -0.5
    for a in range(TT):
        keys = (a + 1) * P
        d = a * P + i[:, None] - np.arange(keys)[None, :]
        for g, dil in enumerate(DIL):
            ok = (d >= 0) & (d % dil == 0) & (d <= P * dil)
            at = C_DIL + 3 * P * a + g * keys
            t[:, at:at + keys] = np.where(ok, 0.0, NEG)
    for lv in range(LEVELS):
        b = 2 << lv
        ok = (i[:, None] // b == i[None, :] // b) & (i[:, None] % b < b // 2) & (i[None, :] % b >= b // 2)
        t[:, C_LEVEL + lv * P:C_LEVEL + (lv + 1) * P] = ok
    t[:, C_LEVEL + LEVELS * P:C_END] = np.eye(P)
    return t


M_FF1 = 16
M_IN2 = M_FF1 + 3 * CH1
M_ATT = M_IN2 + 9
M_R = M_ATT + 6 * AG
M_GATE = M_R + 4
M_BR = M_GATE + 8
M_OUT2 = M_BR + 6
M_FF2 = M_OUT2 + 4
M_END = M_FF2 + 2 * CH2
C_OUT, C_GLA, C_ATT, C_R = 9, 11, 16, 25
C_GATE, C_BR, C_OUT2 = 27, 31, 35

PARTS = ("x", "positions", "w_in", "w_uq", "w_ukv", "w_out", "w_up", "w_down", "final_norm_w", "w_in_2",
         "gla_gate_up_2", "w_attn_branch_2", "w_gla_branch_2", "w_out_2", "w_ff_up_2", "w_ff_down_2", "vectors")
Parts = namedtuple("Parts", PARTS)

TWO_PI = (6.28125, 0.0019350051879882812, 3.0199159819e-07)
MAGIC = 1.5 * 2 ** 23
ROOT_GUESS = 0x5F3759DF


def slab_table(w):
    def rows(x, k0, k1, c0, c1):
        return x[k0 * P:k1 * P, c0:c1].rearrange("(k p) c -> p k c", p=P)

    def chunk(x, c0, c1):
        return [(rows(x, k, k + 4, c0, c1), 2 * (c1 - c0), 0) for k in (0, 4)]

    w_in, w_in_2 = w.w_in[0], w.w_in_2[0]
    one = chunk(w_in, 2048, 2464) + chunk(w_in, 0, 512)
    one += [(rows(w.w_uq[0], 0, 2, 0, 768), 768, 0), (rows(w.w_ukv[0], 0, 1, 0, 1024), 512, 0)]
    for c in (512, 1024, 1536):
        one += chunk(w_in, c, c + 512)
    for c in (0, 512):
        one += chunk(w.w_out[0], c, c + 512)
    assert len(one) == M_FF1

    two = chunk(w_in_2, GQ0, GQ0 + 512) + chunk(w_in_2, GK0, GK0 + 512)
    two += [(rows(w_in_2, 0, KT, GA0, GA0 + 16), 64, 0)]
    two += chunk(w_in_2, GV0, GV0 + 512) + chunk(w_in_2, GV0 + 512, GV0 + 1024)
    for g in range(AG):
        for part in range(3):
            two += chunk(w_in_2, part * AW + g * 512, part * AW + g * 512 + 512)
    for c in (GR0, GR0 + 512):
        two += chunk(w_in_2, c, c + 512)
    for c in range(GG0, GG0 + 2048, 256):
        two += [(rows(w_in_2, 0, KT, c, c + 256), HALF, 256)]
    for c in (0, 512):
        two += [(rows(w.w_attn_branch_2[0], 0, 4, c, c + 512), HALF, 512)]
        two += [(rows(w.w_gla_branch_2[0], 0, KT, q, q + 256), HALF, 256) for q in (c, c + 256)]
    for c in (0, 512):
        two += chunk(w.w_out_2[0], c, c + 512)
    assert len(two) == M_FF2 - M_IN2
    return {**dict(enumerate(one)), **{M_IN2 + n: t for n, t in enumerate(two)}}


def ffn_columns(m):
    if m < M_IN2:
        return 0 if m == M_IN2 - 1 or m >= M_FF1 + 2 and (m - M_FF1 - 2) % 3 == 2 else 256
    return 0 if m == M_END - 1 or (m > M_FF2 and (m - M_FF2) % 2 == 0) else 256


SEMAPHORES = (
    "x_in ident_in pos_in consts_in vecs_in fw_in gate_up_in levels_in dil_in out_stored "
    "hi_done lo_done mm_done acc_free0 acc_free1 "
    "act_chain dve_chain pool_chain "
    "ssq inverse_rms x_scaled x_turned h_hi_done h_lo_done x_added "
    "trig_arg trig latent_scaled latents_turned latents_hi latents_lo "
    "mla_q_ready mla_k_ready mla_q_turned mla_k_turned mla_qT mla_kT mla_scores mla_masked mla_max mla_exp "
    "mla_turned mla_pt mla_pv mla_o "
    "ret_roped ret_q_turned ret_k_turned ret_qT ret_kT ret_scores ret_masked ret_o_head ret_copied "
    "ret_centred ret_sq ret_y mixed_turned mixed_hi mixed_lo "
    "taps tap1 gate_conv val_conv gate_silu act_ready act_hi_done act_lo_done "
    "gla_turned gla_qT gla_kT pa_turned pa_T gla_logits gla_z  gla_soft gla_diff "
    "gla_e gla_qe gla_level gla_taken gla_o gla_go gla_ssq gla_ready gate_done "
    "go_turned go_hi go_lo "
    "att_squared att_ms root_guessed root_found att_scaled att_turned att_T "
    "att_scores att_masked att_max att_exp att_turnedp att_pt att_pv att_o oa_turned oa_hi oa_lo "
    "mix_ready mix_hi mix_lo "
    "up_relu up_square up_hi up_lo"
).split()
Semaphores = namedtuple("Semaphores", SEMAPHORES)


def two_blocks_kernel(nc, w, consts, out):
    with ExitStack() as ctx:
        def sb(name, shape, dt=F32):
            return ctx.enter_context(nc.sbuf_tensor(name, shape, dt))

        bank = ctx.enter_context(nc.psum_tensor("bank", [P, 8, 512], F32))
        raw = sb("raw", [P, RAW, 2 * HALF])
        w_hi = sb("w_hi", [P, RING, HALF], F32R)
        w_lo = sb("w_lo", [P, RING, HALF], F32R)
        h_hi = sb("h_hi", [P, KT, TOKENS], F32R)
        h_lo = sb("h_lo", [P, KT, TOKENS], F32R)
        a_hi = sb("a_hi", [P, 12, TOKENS], F32R)
        a_lo = sb("a_lo", [P, 12, TOKENS], F32R)
        x = sb("x_tok", [P, TT, D])
        ident = sb("ident", [P, P])
        vec = sb("vec", [P, VCOLS])
        newton = sb("newton", [P, 2, 16])
        heads_newton = sb("heads_newton", [P, 2, 16])
        st = sb("stats", [P, 96])
        arena = sb("arena", [P, 26016])

        s = Semaphores(*[ctx.enter_context(nc.semaphore(n)) for n in SEMAPHORES])
        raw_in = [ctx.enter_context(nc.semaphore(f"raw_in{r}")) for r in range(RAW)]
        acc_free = (s.acc_free0, s.acc_free1)
        table = slab_table(w)

        def area(at, *dims):
            n = 1
            for d in dims:
                n *= d
            v = arena[:, at:at + n]
            if len(dims) == 2:
                return v.rearrange("p (a b) -> p a b", b=dims[1])
            if len(dims) == 3:
                return v.rearrange("p (a b c) -> p a b c", b=dims[1], c=dims[2])
            if len(dims) == 4:
                return v.rearrange("p (a b c d) -> p a b c d", b=dims[1], c=dims[2], d=dims[3])
            return v

        def column(name, k=0):
            r = VEC[name][0] + k
            return vec[:, r:r + 1]

        def flat(v):
            return v.rearrange("p a b -> p (a b)")

        def raw_half(r, half, size, cols):
            if not cols:
                return raw[:, r, half * size:(half + 1) * size]
            c = cols // 2
            return raw[:, r, 0:2 * size].rearrange("p (k c) -> p k c", c=cols)[:, :, half * c:(half + 1) * c]

        def pair(c, width=512):
            return bank[:, 2 * (c % 2):2 * (c % 2) + 2, 0:width]

        xn = area(0, TT, D)
        proj = area(4096, TT, 2464)
        causal = area(9024, 3 * P)
        decay = area(9408, RH, 3 * P)
        q_tok = area(12480, TT, MH, QK)
        k_tok = area(14016, TT, MH, QK)
        kv = area(15552, TT, MH, NOPE + MV)
        mqT = area(17600, MH, TOKENS)
        mkT = area(19648, MH, TOKENS)
        rqT = area(21696, RH // 2, TOKENS)
        rkT = area(22720, RH // 2, TOKENS)
        sT = area(23744, 2, 3 * P)
        pT = area(24512, 2, 3 * P)
        rope_tmp = area(0, 2, RH * RD // 2)
        r_row = area(2048, TOKENS)
        angle = area(25280, 2, TT, 48)
        turns = area(25472, 2, TT, 48)
        pos_i = area(25664, TT)
        pos_f = area(25666, TT)
        invf = area(25668, 48)
        conv = area(0, 2, 2, 512)
        silu1 = area(2048, 2, 512)
        act1 = area(3072, 2, 512)
        fw = area(24864, D)
        gqk = area(0, 2, TT, 512)
        qe = area(0, GH, TOKENS)
        ke = area(1024, GH, TOKENS)
        soft = area(2048, GH * TOKENS)
        gv = area(3072, TT, GH * GV)
        gqT = area(5120, GH, TOKENS)
        gkT = area(6144, GH, TOKENS)
        run = area(7168, GH * TOKENS)
        z = area(8192, GH * TOKENS)
        g_in = area(9216, GH, TT, P)
        resets = area(9216, GH * TOKENS)
        g_cross = area(10240, GH, P)
        levels = area(10752, LEVELS + 1, P)
        paT = area(11776, TOKENS)
        gate_up = area(12032, GH * GK)
        ga = area(12544, TT, 16)
        a_tok = area(12576, 2, TT, 512)
        aqT = area(14624, 4 * AG, TOKENS)
        akT = area(17696, 4 * AG, TOKENS)
        av = area(20768, TT, AW)
        asq = area(23840, TT, 512)
        dil = area(24864, 9 * P)
        go = area(5120, TT, GH * GV)
        silu_r = area(0, TT, GH * GV)
        go_squares = area(3072, TT, GH * GV)
        gates = (area(3072, KT, TOKENS), area(7168, KT, TOKENS))
        p = area(9216, 2, 6 * P)
        ppT = area(10752, 2, 6 * P)
        oa = area(23840, TT, 512)
        mix = area(12576, 2, 2, 512)
        relu2 = area(3072, 3, 512)
        square2 = area(4608, 3, 512)

        def turn(dst, src, rows=P):
            return nc.tensor.transpose(dst, src, ident[0:rows, 0:rows])

        block = ctx.enter_context(nc.Block())

        @block.sync
        def _(sp):
            def load_slab(slot, m, dst, src):
                if not isinstance(m, int) or m >= RAW:
                    sp.wait_ge(s.lo_done, m * 2 - 2 * RAW + 2)
                sp.dma_start(dst, src).then_inc(raw_in[slot], 16)

            def load(m):
                src = table[m][0]
                _, k, c = src.shape
                load_slab(m % RAW, m, raw[:, m % RAW, 0:k * c].rearrange("p (k c) -> p k c", c=c), src)

            def load_ffn(m0, i, src):
                m = m0 if i is None else i * 6 + m0
                k = src.shape[1]
                load_slab(m0 % RAW, m, raw[:, m0 % RAW, :].rearrange("p (k c) -> p k c", k=k), src)

            sp.dma_start(ident[:], consts[:, C_IDENT:C_IDENT + P]).then_inc(s.ident_in, 16)
            sp.dma_start(x[:], w.x[0].rearrange("(a p) d -> p a d", p=P)).then_inc(s.x_in, 16)
            load(0)
            load(1)
            sp.dma_start(pos_i.bitcast(I32), w.positions).then_inc(s.pos_in, 16)
            sp.dma_start(invf, consts[:, C_INVF:C_INVF + 48]).then_inc(s.pos_in, 16)
            load(2)
            sp.dma_start(causal, consts[:, C_CAUSAL:C_CAUSAL + 3 * P]).then_inc(s.consts_in, 16)
            sp.dma_start(decay, consts[:, C_DECAY:C_DIL].rearrange("p (h c) -> p h c", h=RH)).then_inc(s.consts_in, 16)
            for m in range(3, M_FF1):
                load(m)

            up = w.w_up[0].rearrange("(k p) c -> p k c", p=P)
            down = w.w_down[0].rearrange("(n k p) c -> n p k c", k=2, p=P)
            load_ffn(M_FF1, None, up[:, :, 0:256])
            load_ffn(M_FF1 + 1, None, up[:, :, FF1:FF1 + 256])
            with sp.Fori(0, CH1 // 2) as i:
                for e in range(2):
                    m = M_FF1 + 2 + 3 * e
                    load_ffn(m, i, up[:, :, bass.ds(i * 512 + 256 * (e + 1), 256)])
                    load_ffn(m + 1, i, up[:, :, bass.ds(i * 512 + FF1 + 256 * (e + 1), 256)])
                    load_ffn(m + 2, i, down[bass.ds(i * 2 + e, 1)].rearrange("n p k c -> p (n k) c"))
            load_ffn(M_IN2 - 1, None, down[CH1 - 1])

            load(M_IN2)
            sp.wait_ge(s.mm_done, 2 * M_FF1)
            sp.dma_start(fw, w.final_norm_w.rearrange("(o d) -> o d", o=1).to_broadcast([P, D])).then_inc(s.fw_in, 16)
            sp.dma_start(gate_up[0:16, :], w.gla_gate_up_2[0]).then_inc(s.gate_up_in, 16)
            sp.dma_start(levels, consts[:, C_LEVEL:C_END].rearrange("p (l c) -> p l c", c=P)).then_inc(s.levels_in, 16)
            for m in range(M_IN2 + 1, M_IN2 + 5):
                load(m)
            sp.wait_ge(s.x_added, 2)
            sp.dma_start(dil, consts[:, C_DIL:C_LEVEL]).then_inc(s.dil_in, 16)
            for m in range(M_IN2 + 5, M_FF2):
                load(m)

            up = w.w_ff_up_2[0].rearrange("(k p) c -> p k c", p=P)
            down = w.w_ff_down_2[0].rearrange("(n k p) c -> n p k c", k=2, p=P)
            load_ffn(M_FF2, None, up[:, :, 0:256])
            with sp.Fori(0, CH2 // 3) as i:
                for e in range(3):
                    m = M_FF2 + 1 + 2 * e
                    load_ffn(m, i, up[:, :, bass.ds(i * 768 + 256 * (e + 1), 256)])
                    load_ffn(m + 1, i, down[bass.ds(i * 3 + e, 1)].rearrange("n p k c -> p (n k) c"))
            load_ffn(M_END - 1, None, down[CH2 - 1])

            for a in range(TT):
                sp.wait_ge(s.x_added, 3 + a)
                sp.dma_start(out[0].rearrange("(a p) d -> a p d", p=P)[a], x[:, a, :]).then_inc(s.out_stored, 16)
            sp.wait_ge(s.out_stored, 16 * TT)

        @block.gpsimd
        def _(gp):
            steps = 0

            def link(ins):
                nonlocal steps
                steps += 1
                ins.then_inc(s.pool_chain, 1)
                gp.wait_ge(s.pool_chain, steps)

            for n in range(2 * AG + 1):
                v = st[:, 48:64] if n < 2 * AG else st[:, 16:24]
                y, t = [heads_newton[:, i, 0:v.shape[1]] for i in range(2)]
                gp.wait_ge(s.root_guessed, n + 1)
                for step in range(3):
                    link(nc.gpsimd.tensor_tensor(t, y, y, ALU.mult))
                    link(nc.gpsimd.tensor_tensor(t, t, v, ALU.mult))
                    link(nc.gpsimd.tensor_scalar(t, t, -0.5, 1.5, ALU.mult, ALU.add))
                    if step < 2:
                        link(nc.gpsimd.tensor_tensor(y, y, t, ALU.mult))
                nc.gpsimd.tensor_tensor(v, y, t, ALU.mult).then_inc(s.root_found, 1)

        @block.tensor
        def _(pe):
            def passes(dst, l_hi, l_lo, r_hi, r_lo, start, stop):
                nc.tensor.matmul(dst, l_hi, r_hi, start=start, stop=False)
                nc.tensor.matmul(dst, l_hi, r_lo, start=False, stop=False)
                return nc.tensor.matmul(dst, l_lo, r_hi, start=False, stop=stop)

            def half_rows(n, width, k0, kn, lhs, accs, first, last, ready=None, i=None):
                q = n % RING
                pe.wait_ge(s.lo_done, n + 1 if i is None else i * 12 + n + 1)
                for k in range(kn):
                    if ready:
                        ready(k0 + k)
                    for a in range(TT):
                        for acc, c0, c1 in accs[a]:
                            at = k * width
                            ins = passes(acc, lhs[0][:, k0 + k, a * P:(a + 1) * P], lhs[1][:, k0 + k, a * P:(a + 1) * P],
                                         w_hi[:, q, at + c0:at + c1], w_lo[:, q, at + c0:at + c1],
                                         first and k == 0, last and k == kn - 1)
                ins.then_inc(s.mm_done, 1)

            def chunk_rows(n, c, width, lhs, ready=None, halves=(0, 1, 2, 3), kn=2):
                for e in halves:
                    if e == 0:
                        pe.wait_ge(acc_free[c % 2], c // 2)
                    half_rows(n + e, width, kn * e, kn, lhs, [[(pair(c, width)[:, a], 0, width)] for a in range(TT)],
                              e == 0, e == KT // kn - 1, ready)

            def half_columns(n, kn, c, dst, lhs, i=None):
                q = n % RING
                pe.wait_ge(s.lo_done, n + 1 if i is None else i * 12 + n + 1)
                for t in range(c):
                    for k in range(kn):
                        at = (k * c + t) * P
                        wh, wl = w_hi[:, q, at:at + P], w_lo[:, q, at:at + P]
                        ins = passes(dst[:, t * TOKENS:(t + 1) * TOKENS], wh, wl, lhs[0][:, k, :], lhs[1][:, k, :],
                                     k == 0, k == kn - 1)
                ins.then_inc(s.mm_done, 1)

            def turn_tiles(count, src, done, banks=(4, 5, 6, 7), free=None):
                for k in range(count):
                    b = banks[k // 2]
                    if k % 2 == 0 and free:
                        free(k // 2)
                    for a in range(TT):
                        at = k % 2 * TOKENS + a * P
                        ins = turn(bank[:, b, at:at + P], src(a, k))
                    if k % 2 == 1 or k == count - 1:
                        ins.then_inc(done, 1)

            h, al = (h_hi, h_lo), (a_hi, a_lo)

            def normed(norm, src=x):
                turn_tiles(KT, lambda a, k: src[:, a, k * P:(k + 1) * P], s.x_turned)
                return lambda k: pe.wait_ge(s.h_lo_done, 4 * norm + k // 2 + 1) if k % 2 == 0 else None

            pe.wait_ge(s.ident_in, 16)
            pe.wait_ge(s.x_in, 16)
            ready = normed(0)
            chunk_rows(0, 0, 416, h, ready)
            chunk_rows(4, 1, 512, h)
            pe.wait_ge(s.latent_scaled, 1)
            turn_tiles(3, lambda a, k: proj[:, a, 2048 + k * P:2176 + k * P], s.latents_turned)
            for k in range(2):
                if k == 0:
                    pe.wait_ge(s.latents_lo, 1)
                    for a in range(TT):
                        pe.wait_ge(acc_free[a], 1)
                half_rows(8 + k, 768, k, 1, al, [[(bank[:, 2 * a, :], 0, 512), (bank[:, 2 * a + 1, 0:256], 512, 768)]
                                                 for a in range(TT)], k == 0, k == 1)
            pe.wait_ge(s.latents_lo, 2)
            for e in range(2):
                for a in range(TT):
                    pe.wait_ge(acc_free[a], 2)
                half_rows(10 + e, 512, 2, 1, al, [[(bank[:, 2 * a + e, :], 0, 512)] for a in range(TT)], True, True)
            chunk_rows(12, 6, 512, h)
            pe.wait_ge(s.mla_q_ready, 1)
            for hd in range(MH):
                for a in range(TT):
                    at = hd % 2 * TOKENS + a * P
                    ins = turn(bank[0:QK, 4 + hd // 2, at:at + P], q_tok[:, a, hd, :])
                if hd % 2:
                    ins.then_inc(s.mla_q_turned, 1)
            chunk_rows(16, 7, 512, h, halves=(0, 1))
            pe.wait_ge(s.mla_k_ready, 1)
            for hd in range(MH):
                if hd % 2 == 0:
                    pe.wait_ge(s.mla_qT, hd // 2 + 1)
                for a in range(TT):
                    at = hd % 2 * TOKENS + a * P
                    ins = turn(bank[0:QK, 4 + hd // 2, at:at + P], k_tok[:, a, hd, :])
                if hd % 2:
                    ins.then_inc(s.mla_k_turned, 1)
            chunk_rows(16, 7, 512, h, halves=(2, 3))
            pe.wait_ge(s.ret_roped, 1)
            pe.wait_ge(s.mla_kT, 4)
            turn_tiles(4, lambda a, k: proj[:, a, k * P:(k + 1) * P], s.ret_q_turned, (4, 5))
            turn_tiles(4, lambda a, k: proj[:, a, 512 + k * P:640 + k * P], s.ret_k_turned, (6, 7))

            def mla_score(hd):
                if hd >= 2:
                    pe.wait_ge(s.mla_masked, hd - 1)
                b = bank[:, 4 + hd % 2, :]
                nc.tensor.matmul(b[:, 0:P], mqT[0:QK, hd, 0:P], mkT[0:QK, hd, 0:P], start=True, stop=True)
                nc.tensor.matmul(b[:, P:3 * P], mqT[0:QK, hd, P:2 * P], mkT[0:QK, hd, :], start=True,
                                 stop=True).then_inc(s.mla_scores, 1)

            pe.wait_ge(s.ret_qT, 2)
            mla_score(0)
            mla_score(1)
            pe.wait_ge(s.ret_kT, 2)
            for hd in range(MH):
                if hd % 2 == 0:
                    chunk_rows(20, 8, 512, h, halves=(hd // 2,))
                pe.wait_ge(s.mla_exp, hd + 1)
                if hd >= 1:
                    pe.wait_ge(s.mla_pt, hd)
                for n in range(3):
                    ins = turn(bank[:, 6, n * P:(n + 1) * P], sT[:, hd % 2, n * P:(n + 1) * P])
                ins.then_inc(s.mla_turned, 1)
                if hd + 2 < MH:
                    mla_score(hd + 2)
                pe.wait_ge(s.mla_pt, hd + 1)
                if hd == 4:
                    pe.wait_ge(s.mla_o, 1)
                o = bank[:, 7, hd % 4 * 128:hd % 4 * 128 + 128]
                v = [kv[:, a, hd, NOPE:NOPE + MV] for a in range(TT)]
                w_ = pT[:, hd % 2, :]
                nc.tensor.matmul(o[:, 0:64], w_[:, 0:P], v[0], start=True, stop=True)
                nc.tensor.matmul(o[:, 64:128], w_[:, P:2 * P], v[0], start=True, stop=False)
                nc.tensor.matmul(o[:, 64:128], w_[:, 2 * P:3 * P], v[1], start=False, stop=True).then_inc(s.mla_pv, 1)

            def ret_score(hd):
                if hd >= 2:
                    pe.wait_ge(s.ret_masked, hd - 1)
                r = hd % 2 * RD
                q, k = rqT[r:r + RD, hd // 2, :], rkT[r:r + RD, hd // 2, :]
                b = bank[:, 4 + hd % 2, :]
                nc.tensor.matmul(b[:, 0:2 * P], k[:, 0:P], q, start=True, stop=True)
                nc.tensor.matmul(b[:, 2 * P:3 * P], k[:, P:2 * P], q[:, P:2 * P], start=True,
                                 stop=True).then_inc(s.ret_scores, 1)

            pe.wait_ge(s.mla_masked, MH)
            ret_score(0)
            ret_score(1)
            pe.wait_ge(s.mla_pt, MH)
            pe.wait_ge(s.mla_o, 2)
            pe.wait_ge(s.acc_free1, 4)
            for hd in range(RH):
                pe.wait_ge(s.ret_masked, hd + 1)
                v = [proj[:, a, 1024 + hd * RD:1024 + (hd + 1) * RD] for a in range(TT)]
                o = [bank[:, 6 + a, hd * RD:(hd + 1) * RD] for a in range(TT)]
                w_ = sT[:, hd % 2, :]
                nc.tensor.matmul(o[0], w_[:, 0:P], v[0], start=True, stop=True)
                nc.tensor.matmul(o[1], w_[:, P:2 * P], v[0], start=True, stop=False)
                nc.tensor.matmul(o[1], w_[:, 2 * P:3 * P], v[1], start=False, stop=True).then_inc(s.ret_o_head, 1)
                if hd + 2 < RH:
                    ret_score(hd + 2)
            pe.wait_ge(s.ret_masked, RH)
            pe.wait_ge(s.ret_copied, 1)
            pe.wait_ge(s.ret_y, 1)
            turn_tiles(KT, lambda a, k: proj[:, a, k * P:(k + 1) * P], s.mixed_turned)
            for c in range(2):
                chunk_rows(24 + 4 * c, C_OUT + c, 512, al,
                           lambda k: pe.wait_ge(s.mixed_lo, k // 2 + 1) if k % 2 == 0 else None)

            pe.wait_ge(s.x_scaled, 2)
            ready = normed(1, xn)

            def ff1_up(n, e, i=None, j0=None):
                for v in range(2):
                    if i is not None or j0 >= 2:
                        pe.wait_ge((s.gate_conv, s.val_conv)[v], j0 - 1 if i is None else i * 2 + j0 - 1)
                    for f in range(2):
                        half_columns(n + 2 * v + f, KT, 1, bank[:, 2 * e + v, f * TOKENS:(f + 1) * TOKENS], h, i)

            def ff_down(n, at, first, last, act, i=None):
                act()
                for k in range(2):
                    half_rows(n + k, 1024, at + k, 1, al,
                              [[(bank[:, 4 + 2 * a + b, :], 512 * b, 512 * b + 512) for b in range(2)] for a in range(TT)],
                              first and k == 0, last and k == 1, None, i)

            n1 = 2 * M_FF1
            for k in range(KT):
                ready(k)
            pe.wait_ge(s.acc_free0, 6)
            ff1_up(n1, 0, None, 0)
            pe.wait_ge(s.acc_free1, 5)
            ff1_up(n1 + 4, 1, None, 1)
            ff_down(n1 + 8, 0, True, False, lambda: pe.wait_ge(s.act_lo_done, 1))
            ff1_up(n1 + 10, 0, None, 2)
            ff_down(n1 + 14, 2, False, False, lambda: pe.wait_ge(s.act_lo_done, 2))
            with pe.Fori(1, CH1 // 2) as i:
                ff1_up(n1 + 4, 1, i, 1)
                ff_down(n1 + 8, 0, False, False, lambda: pe.wait_ge(s.act_lo_done, i * 2 + 1), i)
                ff1_up(n1 + 10, 0, i, 2)
                ff_down(n1 + 14, 2, False, False, lambda: pe.wait_ge(s.act_lo_done, i * 2 + 2), i)
            ff_down(2 * M_IN2 - 2, 0, False, True, lambda: pe.wait_ge(s.act_lo_done, CH1))

            n2 = 2 * M_IN2
            pe.wait_ge(s.x_added, 1)
            pe.wait_ge(s.val_conv, CH1)
            ready = normed(2)
            chunk_rows(n2, C_GLA, 512, h, ready)
            chunk_rows(n2 + 4, C_GLA + 1, 512, h)
            chunk_rows(n2 + 8, C_GLA + 2, 16, h, halves=(0, 1), kn=4)
            chunk_rows(n2 + 10, C_GLA + 3, 512, h)
            pe.wait_ge(s.acc_free1, 6)
            turn_tiles(4, lambda a, k: gqk[:, 0, a, k * P:(k + 1) * P], s.gla_turned, (4, 5))
            pe.wait_ge(s.acc_free0, 7)
            turn_tiles(4, lambda a, k: gqk[:, 1, a, k * P:(k + 1) * P], s.gla_turned, (6, 7))
            chunk_rows(n2 + 14, C_GLA + 4, 512, h, halves=(0, 1))
            pe.wait_ge(s.acc_free1, 7)
            pe.wait_ge(s.gla_qT, 1)
            for a in range(TT):
                turn(bank[0:16, 4, a * P:(a + 1) * P], ga[:, a, :])
            for a in range(TT):
                ins = nc.tensor.matmul(bank[:, 4, TOKENS + a * P:TOKENS + (a + 1) * P],
                                       st[:, 8 + a:9 + a].to_broadcast([P, P]), ident[:], start=True, stop=True)
            ins.then_inc(s.pa_turned, 1)
            chunk_rows(n2 + 14, C_GLA + 4, 512, h, halves=(2, 3))
            pe.wait_ge(s.pa_T, 1)
            pe.wait_ge(s.gate_up_in, 16)
            pe.wait_ge(s.gla_kT, 1)
            for hd in range(GH):
                ins = nc.tensor.matmul(bank[:, 6 + hd // 2, hd % 2 * TOKENS:(hd % 2 + 1) * TOKENS],
                                       gate_up[0:16, hd * GK:(hd + 1) * GK], paT[0:16, :], start=True, stop=True)
            ins.then_inc(s.gla_logits, 1)

            def turn_heads(t):
                nth = t // 3 * 2 + t % 3
                pe.wait_ge(s.att_scaled, nth + 1)
                if nth == 0:
                    pe.wait_ge(s.gla_z, 1)
                else:
                    pe.wait_ge(s.att_T, nth)
                turn_tiles(4, lambda a, k: a_tok[:, t % 3, a, k * P:(k + 1) * P], s.att_turned, (6, 7))

            def level(t):
                q_, k_ = (gqT, gkT) if t == 8 else (qe, ke)
                pe.wait_ge(s.gla_qe, min(t + 1, 8))
                if t >= 1:
                    pe.wait_ge(s.gla_taken, t)
                for hd in range(GH):
                    if t == 0:
                        ins = nc.tensor.matmul(bank[:, 4, hd * P:(hd + 1) * P], k_[:, hd, 0:P], q_[:, hd, P:2 * P],
                                               start=True, stop=True)
                    else:
                        for a in range(TT):
                            at = (hd % 2 * 2 + a) * P
                            ins = nc.tensor.matmul(bank[:, 4 + hd // 2, at:at + P], k_[:, hd, a * P:(a + 1) * P],
                                                   q_[:, hd, a * P:(a + 1) * P], start=True, stop=True)
                ins.then_inc(s.gla_level, 1)

            for t in range(3 * AG + 2):
                chunk_rows(n2 + 18 + 4 * t, C_ATT + t, 512, h)
                if t >= 1 and (t - 1) % 3 < 2 and t - 1 < 3 * AG:
                    turn_heads(t - 1)
                if 1 <= t <= 9:
                    level(t - 1)
            pe.wait_ge(s.gla_taken, 9)
            pe.wait_ge(s.att_T, 2 * AG)
            for a in range(TT):
                for hd in range(GH):
                    o = bank[:, 4 + 2 * a + hd // 2, hd % 2 * GV:(hd % 2 + 1) * GV]
                    v = [gv[:, t, hd * GV:(hd + 1) * GV] for t in range(TT)]
                    if a == 1:
                        nc.tensor.matmul(o, g_cross[:, hd, :], v[0], start=True, stop=False)
                    ins = nc.tensor.matmul(o, g_in[:, hd, a, :], v[a], start=a == 0, stop=True)
                ins.then_inc(s.gla_o, 1)

            def fill(f):
                c = C_GATE + f // 4
                if f % 4 == 0:
                    pe.wait_ge(acc_free[c % 2], c // 2)
                t = f % 4
                half_columns(2 * M_GATE + f, KT, 1, bank[:, 2 * (c % 2) + t // 2, t % 2 * TOKENS:(t % 2 + 1) * TOKENS], h)

            def att_score(u):
                a, i = u // AH, u % AH
                keys = (a + 1) * P
                r = i % 2 * AD
                if u >= 1:
                    pe.wait_ge(s.att_masked, u)
                for g in range(AG):
                    k = g * 4 + i // 2
                    at = (4 + u % 2) * 512 + g * keys if a == 0 else 4 * 512 + g * keys
                    ins = nc.tensor.matmul(bank[:, at // 512, at % 512:at % 512 + keys],
                                           aqT[r:r + AD, k, a * P:(a + 1) * P], akT[r:r + AD, k, 0:keys],
                                           start=True, stop=True)
                ins.then_inc(s.att_scores, 1)

            def att_turn(u, part):
                done = u if u < AH else AH + 2 * (u - AH)
                if part == 0:
                    pe.wait_ge(s.att_exp, u + 1)
                if done + part >= 1:
                    pe.wait_ge(s.att_pt, done + part)
                for b in range(3):
                    at = (3 * part + b) * P
                    ins = turn(bank[:, 6, b * P:(b + 1) * P], p[:, u % 2, at:at + P])
                ins.then_inc(s.att_turnedp, 1)

            def att_value(u):
                a, i = u // AH, u % AH
                pe.wait_ge(s.att_pt, u + 1 if a == 0 else AH + 2 * (u - AH) + 2)
                if u == AH:
                    pe.wait_ge(s.att_o, 1)
                o = bank[:, 7, i * AD:(i + 1) * AD]
                n = AG * (a + 1)
                for b in range(n):
                    g, t = b // (a + 1), b % (a + 1)
                    ins = nc.tensor.matmul(o, ppT[:, u % 2, b * P:(b + 1) * P],
                                           av[:, t, g * 512 + i * AD:g * 512 + (i + 1) * AD], start=b == 0, stop=b == n - 1)
                ins.then_inc(s.att_pv, 1)

            fill(0)
            pe.wait_ge(s.gla_go, 2)
            att_score(0)
            for u in range(2 * AH):
                if u > 0:
                    fill(u)
                att_turn(u, 0)
                if u + 1 < 2 * AH:
                    att_score(u + 1)
                if u > 0:
                    att_value(u - 1)
                if u >= AH:
                    att_turn(u, 1)
            att_value(2 * AH - 1)

            pe.wait_ge(s.gla_ready, 1)
            pe.wait_ge(s.att_masked, 2 * AH)
            turn_tiles(4, lambda a, k: go[:, a, k * P:(k + 1) * P], s.go_turned, (4, 5))
            pe.wait_ge(s.att_o, 2)
            turn_tiles(4, lambda a, k: oa[:, a, k * P:(k + 1) * P], s.oa_turned, (6, 7))
            turn_tiles(4, lambda a, k: go[:, a, 512 + k * P:640 + k * P], s.go_turned, (4, 5),
                       lambda b: pe.wait_ge(s.go_lo, b + 1))
            b0 = 2 * M_BR
            for e in range(2):
                if e == 0:
                    pe.wait_ge(s.oa_lo, 2)
                for t in range(2):
                    c = C_BR + 2 * e + t
                    pe.wait_ge(acc_free[c % 2], c // 2)
                    half_columns(b0 + 6 * e + t, 4, 2, bank[:, 2 * (c % 2), :], (a_hi, a_lo))
                if e == 0:
                    pe.wait_ge(s.go_lo, 4)
                for t in range(2):
                    c = C_BR + 2 * e + t
                    for f in range(2):
                        half_columns(b0 + 6 * e + 2 + 2 * t + f, KT, 1,
                                     bank[:, 2 * (c % 2) + 1, f * TOKENS:(f + 1) * TOKENS],
                                     (a_hi[:, 4:12, :], a_lo[:, 4:12, :]))
            for c in range(2):
                chunk_rows(2 * M_OUT2 + 4 * c, C_OUT2 + c, 512, h,
                           lambda k: pe.wait_ge(s.mix_lo, k // 2 + 1) if k % 2 == 0 else None)

            pe.wait_ge(s.acc_free0, 19)
            pe.wait_ge(s.acc_free1, 18)
            ready = normed(3)
            for k in range(KT):
                ready(k)

            def ff2_up(n, b, j0, i=None):
                if i is not None or j0 >= 3:
                    pe.wait_ge(s.up_relu, j0 - 2 if i is None else i * 3 + j0 - 2)
                for f in range(2):
                    half_columns(n + f, KT, 1, bank[:, b, f * TOKENS:(f + 1) * TOKENS], h, i)

            n3 = 2 * M_FF2

            def ff2_step(i, first):
                for e in range(3):
                    ff2_up(n3 + 2 + 4 * e, (e + 1) % 3, e + 1, i)
                    ff_down(n3 + 4 + 4 * e, 2 * e, first and e == 0, False,
                            lambda: pe.wait_ge(s.up_lo, e + 1 if i is None else i * 3 + e + 1), i)

            ff2_up(n3, 0, 0)
            ff2_step(None, True)
            with pe.Fori(1, CH2 // 3) as i:
                ff2_step(i, False)
            ff_down(2 * M_END - 2, 0, False, True, lambda: pe.wait_ge(s.up_lo, CH2))

        @block.scalar
        def _(act):
            chain = [0]

            def link(ins):
                chain[0] += 1
                ins.then_inc(s.act_chain, 1)
                act.wait_ge(s.act_chain, chain[0])

            def split_hi(n, size, cols, i=None):
                m, half = n // 2, n % 2
                if half == 0:
                    landed = 16 * (m // RAW + 1)
                    act.wait_ge(raw_in[m % RAW], landed if i is None else i * 32 + landed)
                if i is not None or n >= RING:
                    act.wait_ge(s.mm_done, n - RING + 1 if i is None else i * 12 + n - RING + 1)
                dst = w_hi[:, n % RING, 0:size]
                if cols:
                    dst = dst.rearrange("p (k c) -> p k c", c=cols // 2)
                nc.scalar.copy(dst, raw_half(m % RAW, half, size, cols)).then_inc(s.hi_done, 1)

            def hi(*ns, i=None):
                for n in ns:
                    _, size, cols = table[n // 2] if n // 2 in table else (None, HALF, ffn_columns(n // 2))
                    split_hi(n, size, cols, i)

            def evacuate(dst, src, c, mm, func=ACT.Copy, rms=None):
                act.wait_ge(s.mm_done, mm)
                if rms is None:
                    ins = nc.scalar.activation(dst, src, func)
                else:
                    for a in range(TT):
                        ins = nc.scalar.activation(dst[:, a], src[:, a], func, scale=st[:, rms + a:rms + a + 1])
                ins.then_inc(acc_free[c % 2], 1)

            def mean_squares():
                for a in range(TT):
                    ins = nc.scalar.activation(xn[:, a, :], x[:, a, :], ACT.Square, scale=D ** -0.5,
                                               accum_out=st[:, a:a + 1])
                ins.then_inc(s.ssq, 1)

            def turned_hi(dst, at, count, turned, before, gain, done, first=4):
                for k in range(count):
                    if k % 2 == 0:
                        act.wait_ge(turned, before + k // 2 + 1)
                    ins = nc.scalar.activation(dst[:, at + k, :], bank[:, first + k // 2, k % 2 * 256:k % 2 * 256 + 256],
                                               ACT.Copy, scale=gain(k))
                    if k % 2 == 1 or k == count - 1:
                        ins.then_inc(done, 1)

            nc.scalar.dma_start(vec[:], w.vectors).then_inc(s.vecs_in, 16)
            hi(0)
            act.wait_ge(s.vecs_in, 16)
            turned_hi(h_hi, 0, KT, s.x_turned, 0, lambda k: column("attn_norm_w", k), s.h_hi_done)
            hi(1, 2, 3)
            mean_squares()
            hi(4, 5, 6, 7)
            act.wait_ge(s.inverse_rms, 1)
            evacuate(proj[:, :, 2048:2464], pair(0, 416), 0, 4, rms=2)
            act.wait_ge(s.acc_free0, 1)
            for a in range(TT):
                nc.scalar.activation(xn[:, a, 0:QR], proj[:, a, 2048:2304], ACT.Square, scale=QR ** -0.5,
                                     accum_out=st[:, 4 + a:5 + a])
            for a in range(TT):
                ins = nc.scalar.activation(xn[:, a, QR:QR + KVR], proj[:, a, 2304:2432], ACT.Square,
                                           scale=KVR ** -0.5, accum_out=st[:, 6 + a:7 + a])
            ins.then_inc(s.ssq, 1)
            act.wait_ge(s.trig_arg, 1)
            nc.scalar.activation(angle, angle, ACT.Sin).then_inc(s.trig, 1)
            hi(8, 9, 10, 11)
            turned_hi(a_hi, 0, 3, s.latents_turned, 0,
                      lambda k: column("mla_q_norm_w", k) if k < 2 else column("mla_kv_norm_w"), s.latents_hi)
            evacuate(proj[:, :, 0:512], pair(1), 1, 8, rms=2)
            hi(12, 13)
            for a in range(TT):
                evacuate(q_tok[:, a].rearrange("p h c -> p (h c)"),
                         flat(pair(2 + a))[:, 0:MH * QK], 2 + a, 10)
            hi(14, 15)
            for a in range(TT):
                evacuate(kv[:, a].rearrange("p h c -> p (h c)"), flat(pair(4 + a)), 4 + a, 12)
            hi(16, 17, 18, 19)
            evacuate(proj[:, :, 512:1024], pair(6), 6, 16, rms=2)
            for r in range(4):
                act.wait_ge(s.mla_q_turned, r + 1)
                nc.scalar.activation(flat(mqT[0:QK, 2 * r:2 * r + 2, :]), bank[0:QK, 4 + r, :], ACT.Copy,
                                     scale=QK ** -0.5).then_inc(s.mla_qT, 1)
            hi(20, 21, 22, 23)
            evacuate(proj[:, :, 1024:1536], pair(7), 7, 20, rms=2)
            for b in range(2):
                act.wait_ge(s.ret_q_turned, b + 1)
                nc.scalar.copy(flat(rqT[:, 2 * b:2 * b + 2, :]), bank[:, 4 + b, :]).then_inc(s.ret_qT, 1)
            for hd in range(MH + 1):
                if hd < MH:
                    act.wait_ge(s.mla_max, hd + 1)
                    for a in range(TT):
                        row = sT[:, hd % 2, 0:P] if a == 0 else sT[:, hd % 2, P:3 * P]
                        at = 2 * hd + a
                        ins = nc.scalar.activation(row, row, ACT.Exp, bias=st[:, 16 + at:17 + at],
                                                   accum_out=st[:, 32 + at:33 + at])
                    ins.then_inc(s.mla_exp, 1)
                if hd >= 1:
                    act.wait_ge(s.mla_turned, hd)
                    if hd >= 3:
                        act.wait_ge(s.mla_pv, hd - 2)
                    nc.scalar.copy(pT[:, (hd - 1) % 2, :], bank[:, 6, 0:3 * P]).then_inc(s.mla_pt, 1)
                if hd % 2 and hd < MH:
                    hi(24 + hd // 2)
            evacuate(proj[:, :, 1536:2048], pair(8), 8, 24, ACT.Silu, rms=2)
            act.wait_ge(s.ret_o_head, RH)
            nc.scalar.copy(proj[:, :, 0:512], bank[:, 6:8, :]).then_inc(s.ret_copied, 1)
            act.wait_ge(s.ret_centred, 1)
            nc.scalar.activation(xn[:, :, 0:512], proj[:, :, 0:512], ACT.Square,
                                 scale=RD ** -0.5).then_inc(s.ret_sq, 1)
            turned_hi(a_hi, 0, KT, s.mixed_turned, 0, lambda k: column("ret_gn_w", k), s.mixed_hi)
            hi(28, 29, 30, 31, 32, 33, 34, 35)
            act.wait_ge(s.acc_free1, 5)
            act.wait_ge(s.acc_free0, 6)
            mean_squares()
            turned_hi(h_hi, 0, KT, s.x_turned, 4, lambda k: column("ffn_norm_w", k), s.h_hi_done)

            def taps(j, e, v):
                for f in range(2):
                    t = 22 * v + f
                    bias, scale = VEC["conv_b"][0] + t, CW2 + t
                    ins = nc.scalar.activation(
                        conv[:, v, e, f * 256:f * 256 + 256], bank[:, 2 * e + v, f * 256:f * 256 + 256], ACT.Identity,
                        bias=vec[:, bass.ds(j * 2 + bias, 1)] if not isinstance(j, int) else
                        vec[:, 2 * j + bias:2 * j + bias + 1],
                        scale=vec[:, bass.ds(j * 2 + scale, 1)] if not isinstance(j, int) else
                        vec[:, 2 * j + scale:2 * j + scale + 1])
                ins.then_inc(s.taps, 1)

            def ff1_chunk(j, e, mm, split1, split2, split3):
                act.wait_ge(s.mm_done, mm)
                taps(j, e, 0)
                split1()
                act.wait_ge(s.mm_done, mm + 2)
                taps(j, e, 1)
                split2()
                act.wait_ge(s.gate_conv, j + 1)
                nc.scalar.activation(silu1[:, e, :], conv[:, 0, e, :], ACT.Silu).then_inc(s.gate_silu, 1)
                act.wait_ge(s.act_ready, j + 1)
                nc.scalar.copy(flat(a_hi[:, 2 * e:2 * e + 2, :]), act1[:, e, :]).then_inc(s.act_hi_done, 1)
                split3()

            n1 = 2 * M_FF1
            ff1_chunk(0, 0, n1 + 2, lambda: hi(n1 + 4, n1 + 5), lambda: hi(n1 + 6, n1 + 7), lambda: None)
            with act.Fori(0, CH1 // 2 - 1) as i:
                for e in range(2):
                    b = n1 + 6 * e
                    ff1_chunk(i * 2 + 1 + e, 1 - e, i * 12 + b + 6, lambda: hi(b + 8, b + 9, i=i),
                              lambda: hi(b + 10, b + 11, i=i), lambda: hi(b + 12, b + 13, i=i))
            b = n1 + 12 * (CH1 // 2 - 1)
            ff1_chunk(CH1 - 2, 1, b + 6, lambda: hi(b + 8, b + 9), lambda: hi(b + 10, b + 11), lambda: hi(b + 12, b + 13))
            ff1_chunk(CH1 - 1, 0, b + 12, lambda: hi(b + 14, b + 15), lambda: hi(b + 16, b + 17),
                      lambda: hi(b + 18, b + 19))
            n2 = 2 * M_IN2
            hi(n2 + 2, n2 + 3)

            act.wait_ge(s.x_added, 1)
            turned_hi(h_hi, 0, KT, s.x_turned, 8, lambda k: column("norm1_g_2", k), s.h_hi_done)
            mean_squares()
            act.wait_ge(s.x_added, 2)
            mean_squares()
            hi(n2 + 4, n2 + 5, n2 + 6, n2 + 7)
            act.wait_ge(s.inverse_rms, 2)
            evacuate(gqk[:, 0], pair(C_GLA), C_GLA, n2 + 4, rms=8)
            hi(n2 + 8, n2 + 9, n2 + 10, n2 + 11)
            evacuate(gqk[:, 1], pair(C_GLA + 1), C_GLA + 1, n2 + 8, rms=8)
            hi(n2 + 12, n2 + 13)
            evacuate(ga, pair(C_GLA + 2, 16), C_GLA + 2, n2 + 10, rms=8)
            hi(n2 + 14, n2 + 15, n2 + 16, n2 + 17)
            evacuate(gv[:, :, 0:512], pair(C_GLA + 3), C_GLA + 3, n2 + 14, rms=8)
            act.wait_ge(s.gla_turned, 2)
            nc.scalar.activation(gqT.rearrange("p (b h) t -> p b (h t)", b=2), bank[:, 4:6, :], ACT.Copy,
                                 scale=GK ** -0.5).then_inc(s.gla_qT, 1)
            hi(n2 + 18, n2 + 19, n2 + 20, n2 + 21)
            evacuate(gv[:, :, 512:1024], pair(C_GLA + 4), C_GLA + 4, n2 + 18, rms=8)
            act.wait_ge(s.gla_logits, 1)
            for hd in range(GH):
                ins = nc.scalar.activation(z[:, hd * TOKENS:(hd + 1) * TOKENS],
                                           bank[:, 6 + hd // 2, hd % 2 * TOKENS:(hd % 2 + 1) * TOKENS], ACT.Identity,
                                           bias=column("gla_gate_bias_2", hd))
            ins.then_inc(s.gla_z, 1)
            act.wait_ge(s.gla_z, 1)
            link(nc.scalar.activation(soft, z, ACT.Abs))
            link(nc.scalar.activation(soft, soft, ACT.Exp, scale=-1.0))
            nc.scalar.activation(soft, soft, ACT.Ln, bias=1.0).then_inc(s.gla_soft, 1)

            def level_decay(t):
                act.wait_ge(s.gla_diff, t + 1)
                link(nc.scalar.activation(z, z, ACT.Abs))
                nc.scalar.activation(z, z, ACT.Exp, scale=-1.0 / 16).then_inc(s.gla_e, 1)

            def heads_out(t):
                nth = t // 3 * 2 + t % 3
                act.wait_ge(s.att_turned, 2 * nth + 2)
                dst = (aqT, akT)[t % 3][:, t // 3 * 4:t // 3 * 4 + 4, :]
                nc.scalar.activation(dst.rearrange("p (b k) t -> p b (k t)", b=2), bank[:, 6:8, :], ACT.Copy,
                                     scale=column(("attn_q_norm_g_2", "attn_k_norm_g_2")[t % 3])).then_inc(s.att_T, 1)

            for t in range(3 * AG + 2):
                n = n2 + 18 + 4 * t
                hi(n + 4, n + 5, n + 6, n + 7)
                g, part = t // 3, t % 3
                if t >= 3 * AG:
                    at = 512 * (t - 3 * AG)
                    evacuate(silu_r[:, :, at:at + 512], pair(C_ATT + t), C_ATT + t, n + 4, ACT.Silu, rms=8)
                else:
                    dst = av[:, :, g * 512:g * 512 + 512] if part == 2 else a_tok[:, part]
                    evacuate(dst, pair(C_ATT + t), C_ATT + t, n + 4, rms=8)
                    if part < 2:
                        nth = 2 * g + part
                        c = C_ATT + t
                        act.wait_ge(acc_free[c % 2], c // 2 + 1)
                        if nth >= 1:
                            act.wait_ge(s.att_ms, nth)
                        nc.scalar.activation(asq, a_tok[:, part], ACT.Square, scale=AD ** -0.5).then_inc(
                            s.att_squared, 1)
                if 1 <= t <= 3 * AG and (t - 1) % 3 < 2:
                    heads_out(t - 1)
                if t <= LEVELS:
                    level_decay(t)
            for a in range(TT):
                act.wait_ge(s.gla_o, a + 1)
                nc.scalar.copy(go[:, a, :], flat(bank[:, 4 + 2 * a:6 + 2 * a, :])).then_inc(s.gla_go, 1)
            hi(2 * M_GATE + 4)

            def square_heads(a):
                if a == 0:
                    act.wait_ge(s.gla_go, 2)
                for hd in range(GH):
                    at = 16 + GH * a + hd
                    ins = nc.scalar.activation(go_squares[:, a, hd * GV:(hd + 1) * GV], go[:, a, hd * GV:(hd + 1) * GV],
                                               ACT.Square, scale=GV ** -0.5, accum_out=st[:, at:at + 1])
                if a == 1:
                    ins.then_inc(s.gla_ssq, 1)

            def gate(c):
                act.wait_ge(acc_free[c % 2], c // 2 + 1)
                for k in range(4 * (c - C_GATE), 4 * (c - C_GATE) + 4):
                    g = gates[k // KT][:, k % KT, :]
                    ins = nc.scalar.activation(g, g, ACT.Sigmoid, bias=column("branch_gate_bias_2", k))
                ins.then_inc(s.gate_done, 1)

            def weights_back(u, part):
                done = (u if u < AH else AH + 2 * (u - AH)) + part
                act.wait_ge(s.att_turnedp, done + 1)
                if u >= 2:
                    act.wait_ge(s.att_pv, u - 1)
                nc.scalar.copy(ppT[:, u % 2, 3 * P * part:3 * P * (part + 1)], bank[:, 6, 0:3 * P]).then_inc(s.att_pt, 1)

            for u in range(2 * AH):
                keys = AG * (u // AH + 1) * P
                act.wait_ge(s.att_max, u + 1)
                nc.scalar.activation(p[:, u % 2, 0:keys], p[:, u % 2, 0:keys], ACT.Exp, bias=st[:, 32 + u:33 + u],
                                     accum_out=st[:, 80 + u:81 + u]).then_inc(s.att_exp, 1)
                weights_back(u, 0)
                if u > 0:
                    hi(2 * M_GATE + 4 + u)
                if u < TT:
                    square_heads(u)
                if u >= AH:
                    weights_back(u, 1)
            turned_hi(a_hi, 4, 4, s.go_turned, 0, lambda k: column("gla_out_norm_g_2", k % 2), s.go_hi)
            turned_hi(a_hi, 0, 4, s.oa_turned, 0, lambda k: 1.0, s.oa_hi, 6)
            turned_hi(a_hi, 8, 4, s.go_turned, 2, lambda k: column("gla_out_norm_g_2", k % 2), s.go_hi)
            n = 2 * M_BR

            def mixed_hi(q):
                act.wait_ge(s.mix_ready, q + 1)
                nc.scalar.copy(flat(h_hi[:, 2 * q:2 * q + 2, :]), mix[:, 0, q % 2, :]).then_inc(s.mix_hi, 1)

            for c in range(C_GATE, C_GATE + 4):
                gate(c)
            hi(n + 4, n + 5, n + 6, n + 7)
            mixed_hi(0)
            hi(n + 8, n + 9)
            mixed_hi(1)
            hi(n + 10, n + 11, n + 12, n + 13)
            mixed_hi(2)
            hi(n + 14, n + 15)
            mixed_hi(3)
            hi(*range(n + 16, n + 24))
            act.wait_ge(s.acc_free1, 18)
            act.wait_ge(s.acc_free0, 19)
            turned_hi(h_hi, 0, KT, s.x_turned, 12, lambda k: column("norm2_g_2", k), s.h_hi_done)
            mean_squares()

            def ff2_chunk(j, e, mm, split1, split2):
                act.wait_ge(s.mm_done, mm)
                nc.scalar.activation(relu2[:, e, :], bank[:, e, :], ACT.Relu).then_inc(s.up_relu, 1)
                split1()
                act.wait_ge(s.up_square, j + 1)
                nc.scalar.copy(flat(a_hi[:, 2 * e:2 * e + 2, :]), square2[:, e, :]).then_inc(s.up_hi, 1)
                split2()

            n3 = 2 * M_FF2
            ff2_chunk(0, 0, n3 + 2, lambda: hi(n3 + 4, n3 + 5), lambda: None)
            with act.Fori(0, CH2 // 3 - 1) as i:
                for e in range(3):
                    b = n3 + 4 * e
                    ff2_chunk(i * 3 + e + 1, (e + 1) % 3, i * 12 + b + 4, lambda: hi(b + 6, b + 7, i=i),
                              lambda: hi(b + 8, b + 9, i=i))
            for e in range(3):
                b = n3 + 12 * (CH2 // 3 - 1) + 4 * e
                ff2_chunk(CH2 - 3 + e, (e + 1) % 3, b + 4, lambda: hi(b + 6, b + 7),
                          (lambda: hi(b + 8, b + 9)) if e < 2 else (lambda: None))

        @block.vector
        def _(dve):
            chain = [0]

            def link(ins):
                chain[0] += 1
                ins.then_inc(s.dve_chain, 1)
                dve.wait_ge(s.dve_chain, chain[0])

            def lo(*ns, i=None):
                for n in ns:
                    _, size, cols = table[n // 2] if n // 2 in table else (None, HALF, ffn_columns(n // 2))
                    dve.wait_ge(s.hi_done, n + 1 if i is None else i * 12 + n + 1)
                    dst, h = w_lo[:, n % RING, 0:size], w_hi[:, n % RING, 0:size].bitcast(F32)
                    if cols:
                        dst = dst.rearrange("p (k c) -> p k c", c=cols // 2)
                        h = h.rearrange("p (k c) -> p k c", c=cols // 2)
                    nc.vector.tensor_tensor(dst, raw_half(n // 2 % RAW, n % 2, size, cols), h, ALU.subtract).then_inc(
                        s.lo_done, 1)

            def root_guess(v, src, y, t):
                link(nc.vector.tensor_scalar(v, src, EPS, None, ALU.add))
                link(nc.vector.tensor_scalar(t.bitcast(I32), v.bitcast(I32), 1, None, ALU.arith_shift_right))
                return nc.vector.tensor_scalar(y.bitcast(I32), t.bitcast(I32), -1, ROOT_GUESS, ALU.mult, ALU.add)

            def inverse_root(v, src=None, done=None, count=None):
                n = v.shape[1]
                y, t = newton[:, 0, 0:n], newton[:, 1, 0:n]
                link(root_guess(v, v if src is None else src, y, t))
                for step in range(3):
                    link(nc.vector.scalar_tensor_tensor(t, y, -0.5, v, ALU.mult, ALU.mult))
                    link(nc.vector.tensor_tensor(t, t, y, ALU.mult))
                    ins = nc.vector.scalar_tensor_tensor(y if step < 2 else v, t, 1.5, y, ALU.add, ALU.mult)
                    if step < 2 or done is None:
                        link(ins)
                if done is not None:
                    ins.then_inc(done, 1)
                    dve.wait_ge(done, count)

            def scale_x():
                for a in range(TT):
                    nc.vector.tensor_scalar(xn[:, a, :], x[:, a, :], st[:, 2 + a:3 + a], None, ALU.mult).then_inc(
                        s.x_scaled, 1)

            def turned_lo(dst, dst_hi, at, count, hi_done, before, gain, done, first=4):
                for k in range(count):
                    if k % 2 == 0:
                        dve.wait_ge(hi_done, before + k // 2 + 1)
                    ins = nc.vector.scalar_tensor_tensor(
                        dst[:, at + k, :], bank[:, first + k // 2, k % 2 * 256:k % 2 * 256 + 256], gain(k),
                        dst_hi[:, at + k, :].bitcast(F32), ALU.mult, ALU.subtract)
                    if k % 2 == 1 or k == count - 1:
                        ins.then_inc(done, 1)

            def rotate(t, heads, width, lane):
                half = width // 2
                for a in range(TT):
                    x1, x2 = t[:, a, :, 0:half], t[:, a, :, half:width]
                    cos, sin = [angle[:, f, a, lane:lane + half].rearrange("p (o f) -> p o f", o=1).to_broadcast(
                        [P, heads, half]) for f in range(2)]
                    t1, t2 = [rope_tmp[:, f, 0:heads * half].rearrange("p (h f) -> p h f", f=half) for f in range(2)]
                    nc.vector.tensor_tensor(t1, x1, sin, ALU.mult)
                    nc.vector.tensor_tensor(t2, x2, sin, ALU.mult)
                    nc.vector.tensor_tensor(x1, x1, cos, ALU.mult)
                    link(nc.vector.tensor_tensor(x2, x2, cos, ALU.mult))
                    nc.vector.tensor_tensor(x1, x1, t2, ALU.subtract)
                    ins = nc.vector.tensor_tensor(x2, x2, t1, ALU.add)
                    if a == 0:
                        link(ins)
                return ins

            lo(0)
            dve.wait_ge(s.vecs_in, 16)
            fn, n1g = VEC["final_norm_w"][0], VEC["norm1_g_2"][0]
            nc.vector.tensor_tensor(vec[:, n1g:n1g + KT], vec[:, n1g:n1g + KT], vec[:, fn:fn + KT], ALU.mult)
            nc.vector.tensor_scalar(column("attn_q_norm_g_2"), column("attn_q_norm_g_2"), AD ** -0.5, None, ALU.mult)
            turned_lo(h_lo, h_hi, 0, KT, s.h_hi_done, 0, lambda k: column("attn_norm_w", k), s.h_lo_done)
            lo(1, 2, 3)
            dve.wait_ge(s.ssq, 1)
            inverse_root(st[:, 2:4], st[:, 0:2], s.inverse_rms, 1)
            dve.wait_ge(s.pos_in, 32)
            link(nc.vector.tensor_copy(pos_f, pos_i.bitcast(I32)))
            for a in range(TT):
                for t in range(2):
                    ins = nc.vector.tensor_scalar(angle[:, t, a, :], invf, pos_f[:, a:a + 1], None, ALU.mult)
            link(ins)
            for t, turn_ in enumerate((0.25, 0.0)):
                ins = nc.vector.tensor_scalar(turns[:, t], angle[:, t], 0.15915494309189535, turn_, ALU.mult, ALU.add)
            link(ins)
            angle_f, turns_f = area(25280, 4 * 48), area(25472, 4 * 48)
            link(nc.vector.tensor_scalar(turns_f, turns_f, MAGIC, None, ALU.add))
            link(nc.vector.tensor_scalar(turns_f, turns_f, MAGIC, None, ALU.subtract))
            for part in TWO_PI:
                link(nc.vector.scalar_tensor_tensor(angle_f, turns_f, -part, angle_f, ALU.mult, ALU.add))
            link(nc.vector.tensor_scalar(angle[:, 0], angle[:, 0], 1.5707963267948966, None, ALU.add))
            nc.vector.tensor_scalar(angle_f, angle_f, 3.1415925, -3.1415925, ALU.min, ALU.max).then_inc(s.trig_arg, 1)
            lo(4, 5, 6, 7)
            dve.wait_ge(s.ssq, 2)
            inverse_root(st[:, 4:8])
            for a in range(TT):
                nc.vector.tensor_scalar(proj[:, a, 2048:2304], proj[:, a, 2048:2304], st[:, 4 + a:5 + a], None, ALU.mult)
                ins = nc.vector.tensor_scalar(proj[:, a, 2304:2432], proj[:, a, 2304:2432], st[:, 6 + a:7 + a], None,
                                              ALU.mult)
            ins.then_inc(s.latent_scaled, 1)
            lo(8, 9, 10, 11)
            turned_lo(a_lo, a_hi, 0, 3, s.latents_hi, 0,
                      lambda k: column("mla_q_norm_w", k) if k < 2 else column("mla_kv_norm_w"), s.latents_lo)
            dve.wait_ge(s.trig, 1)
            link(rotate(proj[:, :, 2432:2464].rearrange("p a (h c) -> p a h c", h=1), 1, PE_D, 32))
            for a in range(TT):
                nc.vector.tensor_copy(k_tok[:, a, :, NOPE:QK], proj[:, a, 2432:2464].rearrange(
                    "p (o c) -> p o c", o=1).to_broadcast([P, MH, PE_D]))
            lo(12, 13)
            dve.wait_ge(s.acc_free0, 2)
            dve.wait_ge(s.acc_free1, 2)
            rotate(q_tok[:, :, :, NOPE:QK], MH, PE_D, 32).then_inc(s.mla_q_ready, 1)
            lo(14, 15)
            for a in range(TT):
                dve.wait_ge(acc_free[a], 3)
                ins = nc.vector.tensor_copy(k_tok[:, a, :, 0:NOPE], kv[:, a, :, 0:NOPE])
            ins.then_inc(s.mla_k_ready, 1)
            lo(16, 17)
            dve.wait_ge(s.mla_q_ready, 1)
            link(rotate(proj[:, :, 0:512].rearrange("p a (h c) -> p a h c", c=RD), RH, RD, 0))
            lo(18, 19)
            for r in range(4):
                dve.wait_ge(s.mla_k_turned, r + 1)
                nc.vector.tensor_copy(flat(mkT[0:QK, 2 * r:2 * r + 2, :]), bank[0:QK, 4 + r, :]).then_inc(s.mla_kT, 1)
            dve.wait_ge(s.acc_free0, 4)
            rotate(proj[:, :, 512:1024].rearrange("p a (h c) -> p a h c", c=RD), RH, RD, 0).then_inc(s.ret_roped, 1)
            lo(20, 21, 22, 23)
            for b in range(2):
                dve.wait_ge(s.ret_k_turned, b + 1)
                nc.vector.tensor_copy(flat(rkT[:, 2 * b:2 * b + 2, :]), bank[:, 6 + b, :]).then_inc(s.ret_kT, 1)

            def mla_out(r):
                dve.wait_ge(s.mla_pv, 4 * r + 4)
                at = 32 + 8 * r
                link(nc.vector.reciprocal(st[:, at:at + 8], st[:, at:at + 8]))
                o = bank[:, 7, :].rearrange("p (h a c) -> p a h c", h=4, a=2)
                inv = st[:, at:at + 8].rearrange("p (h a o) -> p a h o", a=2, o=1)
                for a in range(TT):
                    ins = nc.vector.tensor_tensor(
                        proj[:, a, 512 + 256 * r:768 + 256 * r].rearrange("p (h c) -> p h c", c=MV),
                        o[:, a], inv[:, a].to_broadcast([P, 4, MV]), ALU.mult)
                ins.then_inc(s.mla_o, 1)

            dve.wait_ge(s.consts_in, 32)
            for hd in range(MH):
                dve.wait_ge(s.mla_scores, hd + 1)
                if hd >= 2:
                    dve.wait_ge(s.mla_turned, hd - 1)
                nc.vector.tensor_tensor(sT[:, hd % 2, :], bank[:, 4 + hd % 2, 0:3 * P], causal, ALU.add).then_inc(
                    s.mla_masked, 1)
                dve.wait_ge(s.mla_masked, hd + 1)
                at = 16 + 2 * hd
                nc.vector.tensor_reduce(st[:, at:at + 1], sT[:, hd % 2, 0:P], AX.X, ALU.max, negate=True)
                nc.vector.tensor_reduce(st[:, at + 1:at + 2], sT[:, hd % 2, P:3 * P], AX.X, ALU.max,
                                        negate=True).then_inc(s.mla_max, 1)
                if hd in (2, 4, 6):
                    lo(23 + hd // 2)
                if hd == 5:
                    mla_out(0)
            lo(27)
            mla_out(1)
            for hd in range(RH):
                dve.wait_ge(s.ret_scores, hd + 1)
                if hd >= 2:
                    dve.wait_ge(s.ret_o_head, hd - 1)
                nc.vector.tensor_tensor(sT[:, hd % 2, :], bank[:, 4 + hd % 2, 0:3 * P], decay[:, hd, :],
                                        ALU.mult).then_inc(s.ret_masked, 1)
            oh = proj[:, :, 0:512].rearrange("p a (h c) -> p a h c", c=RD)
            mean = st[:, 48:64].rearrange("p (a h o) -> p a h o", a=2, o=1)
            var = st[:, 64:80].rearrange("p (a h o) -> p a h o", a=2, o=1)
            dve.wait_ge(s.ret_copied, 1)
            link(nc.vector.tensor_reduce(st[:, 48:64].rearrange("p (a h) -> p a h", a=2), oh, AX.X, ALU.add))
            link(nc.vector.tensor_scalar(st[:, 48:64], st[:, 48:64], -1.0 / RD, None, ALU.mult))
            for a in range(TT):
                ins = nc.vector.tensor_tensor(oh[:, a], oh[:, a], mean[:, a].to_broadcast([P, RH, RD]), ALU.add)
            ins.then_inc(s.ret_centred, 1)
            dve.wait_ge(s.ret_sq, 1)
            link(nc.vector.tensor_reduce(st[:, 64:80].rearrange("p (a h) -> p a h", a=2),
                                         xn[:, :, 0:512].rearrange("p a (h c) -> p a h c", c=RD), AX.X, ALU.add))
            inverse_root(st[:, 64:80])
            dve.wait_ge(s.acc_free0, 5)
            link(nc.vector.tensor_tensor(proj[:, :, 0:512], proj[:, :, 0:512], proj[:, :, 1536:2048], ALU.mult))
            for a in range(TT):
                ins = nc.vector.tensor_tensor(oh[:, a], oh[:, a], var[:, a].to_broadcast([P, RH, RD]), ALU.mult)
            ins.then_inc(s.ret_y, 1)
            turned_lo(a_lo, a_hi, 0, KT, s.mixed_hi, 0, lambda k: column("ret_gn_w", k), s.mixed_lo)

            def add_chunk(c, first, mm):
                dve.wait_ge(s.mm_done, mm)
                xc = x[:, :, 512 * (c - first):512 * (c - first) + 512]
                nc.vector.tensor_tensor(xc, pair(c), xc, ALU.add).then_inc(acc_free[c % 2], 1)

            lo(28, 29, 30, 31)
            add_chunk(C_OUT, C_OUT, 28)
            lo(32, 33, 34, 35)
            add_chunk(C_OUT + 1, C_OUT, 32)
            dve.wait_ge(s.ssq, 3)
            inverse_root(st[:, 2:4], st[:, 0:2])
            scale_x()
            turned_lo(h_lo, h_hi, 0, KT, s.h_hi_done, 4, lambda k: column("ffn_norm_w", k), s.h_lo_done)

            def tap(j, row):
                return vec[:, 2 * j + row:2 * j + row + 1] if isinstance(j, int) else vec[:, bass.ds(j * 2 + row, 1)]

            def convolve(j, e, v):
                dve.wait_ge(s.taps, j * 2 + v + 1)
                for f in range(2):
                    u, y = bank[:, 2 * e + v, f * 256:f * 256 + 256], conv[:, v, e, f * 256:f * 256 + 256]
                    ins = nc.vector.scalar_tensor_tensor(y[:, 1:256], u[:, 0:255], tap(j, CW1 + 22 * v + f), y[:, 1:256],
                                                         ALU.mult, ALU.add)
                ins.then_inc(s.tap1, 1)
                dve.wait_ge(s.tap1, j * 2 + v + 1)
                for f in range(2):
                    u, y = bank[:, 2 * e + v, f * 256:f * 256 + 256], conv[:, v, e, f * 256:f * 256 + 256]
                    ins = nc.vector.scalar_tensor_tensor(y[:, 2:256], u[:, 0:254], tap(j, CW0 + 22 * v + f), y[:, 2:256],
                                                         ALU.mult, ALU.add)
                ins.then_inc((s.gate_conv, s.val_conv)[v], 1)

            def ff1_chunk(j, e, split1, split2, split3):
                convolve(j, e, 0)
                split1()
                convolve(j, e, 1)
                split2()
                dve.wait_ge(s.gate_silu, j + 1)
                dve.wait_ge(s.val_conv, j + 1)
                nc.vector.tensor_tensor(act1[:, e, :], silu1[:, e, :], conv[:, 1, e, :], ALU.mult).then_inc(s.act_ready, 1)
                dve.wait_ge(s.act_hi_done, j + 1)
                nc.vector.tensor_tensor(flat(a_lo[:, 2 * e:2 * e + 2, :]), act1[:, e, :],
                                        flat(a_hi[:, 2 * e:2 * e + 2, :]).bitcast(F32), ALU.subtract).then_inc(
                                            s.act_lo_done, 1)
                split3()

            n1 = 2 * M_FF1
            ff1_chunk(0, 0, lambda: lo(n1 + 4, n1 + 5), lambda: lo(n1 + 6, n1 + 7), lambda: None)
            with dve.Fori(0, CH1 // 2 - 1) as i:
                for e in range(2):
                    b = n1 + 6 * e
                    ff1_chunk(i * 2 + 1 + e, 1 - e, lambda: lo(b + 8, b + 9, i=i), lambda: lo(b + 10, b + 11, i=i),
                              lambda: lo(b + 12, b + 13, i=i))
            b = n1 + 12 * (CH1 // 2 - 1)
            ff1_chunk(CH1 - 2, 1, lambda: lo(b + 8, b + 9), lambda: lo(b + 10, b + 11), lambda: lo(b + 12, b + 13))
            ff1_chunk(CH1 - 1, 0, lambda: lo(b + 14, b + 15), lambda: lo(b + 16, b + 17), lambda: lo(b + 18, b + 19))
            n2 = 2 * M_IN2
            lo(n2 + 2, n2 + 3)

            def add_down(mm, inverse_ms=None):
                dve.wait_ge(s.mm_done, mm)
                for a in range(TT):
                    y = flat(bank[:, 4 + 2 * a:6 + 2 * a, :])
                    if inverse_ms is None:
                        ins = nc.vector.tensor_tensor(x[:, a, :], y, x[:, a, :], ALU.add)
                    else:
                        ins = nc.vector.scalar_tensor_tensor(x[:, a, :], y, inverse_ms[a], x[:, a, :], ALU.mult, ALU.add)
                        ins.then_inc(s.x_added, 1)
                return ins

            add_down(2 * M_IN2).then_inc(s.x_added, 1)
            turned_lo(h_lo, h_hi, 0, KT, s.h_hi_done, 8, lambda k: column("norm1_g_2", k), s.h_lo_done)
            dve.wait_ge(s.ssq, 4)
            inverse_root(st[:, 2:4], st[:, 0:2])
            dve.wait_ge(s.fw_in, 16)
            dve.wait_ge(s.x_turned, 12)
            for a in range(TT):
                ins = nc.vector.scalar_tensor_tensor(x[:, a, :], x[:, a, :], st[:, 2 + a:3 + a], fw, ALU.mult, ALU.mult)
            ins.then_inc(s.x_added, 1)
            lo(n2 + 4, n2 + 5)
            dve.wait_ge(s.ssq, 5)
            inverse_root(st[:, 8:10], st[:, 0:2])
            nc.vector.tensor_tensor(st[:, 8:10], st[:, 8:10], st[:, 2:4], ALU.mult).then_inc(s.inverse_rms, 1)
            lo(*range(n2 + 6, n2 + 18))
            dve.wait_ge(s.gla_turned, 4)
            nc.vector.tensor_copy(gkT.rearrange("p (b h) t -> p b (h t)", b=2), bank[:, 6:8, :]).then_inc(s.gla_kT, 1)
            lo(n2 + 18, n2 + 19)
            dve.wait_ge(s.pa_turned, 1)
            nc.vector.tensor_copy(paT[0:16, :], bank[0:16, 4, 0:TOKENS]).then_inc(s.pa_T, 1)
            lo(n2 + 20, n2 + 21)
            link(nc.vector.memset(resets, 1.0))
            nc.vector.memset(resets.rearrange("p (n t) -> p n t", t=P)[:, :, 0:1], 0.0)
            dve.wait_ge(s.gla_soft, 1)
            link(nc.vector.scalar_tensor_tensor(z, z, 0.0, soft, ALU.min, ALU.subtract))
            link(nc.vector.tensor_tensor_scan(run, resets, z, 0.0, ALU.mult, ALU.add))
            nc.vector.memset(g_in, 0.0)
            nc.vector.tensor_copy(r_row, bank[:, 4, TOKENS:2 * TOKENS])

            def level_distance(t):
                if t == 0:
                    r, d = [v.rearrange("p (h a t) -> p h a t", a=2, t=P) for v in (run, z)]
                    nc.vector.tensor_tensor(d[:, :, 0, :], r[:, :, 0, :], r[:, :, 0, P - 1:P].to_broadcast([P, GH, P]),
                                            ALU.subtract)
                    nc.vector.tensor_copy(d[:, :, 1, :], r[:, :, 1, :]).then_inc(s.gla_diff, 1)
                    return
                b = 2 << (LEVELS - t)
                r, d = [v.rearrange("p (n t) -> p n t", t=b) for v in (run, z)]
                nc.vector.tensor_tensor(d, r, r[:, :, b // 2 - 1:b // 2].to_broadcast([P, GH * TOKENS // b, b]),
                                        ALU.subtract).then_inc(s.gla_diff, 1)

            def over_rms(t):
                dve.wait_ge(s.root_found, 2 * (t // 3) + t % 3 + 1)
                r = st[:, 48:64].rearrange("p (a h o) -> p a h o", a=2, o=1)
                for a in range(TT):
                    v = a_tok[:, t % 3, a, :].rearrange("p (h c) -> p h c", c=AD)
                    ins = nc.vector.tensor_tensor(v, v, r[:, a].to_broadcast([P, AH, AD]), ALU.mult)
                ins.then_inc(s.att_scaled, 1)

            dve.wait_ge(s.levels_in, 16)
            for t in range(3 * AG + 2):
                n = n2 + 18 + 4 * t
                lo(n + 4, n + 5)
                if 1 <= t <= LEVELS + 1:
                    dve.wait_ge(s.gla_e, t)
                    nc.vector.tensor_tensor(flat(qe), flat(gqT), z, ALU.mult)
                    nc.vector.tensor_tensor(flat(ke), flat(gkT), z, ALU.mult).then_inc(s.gla_qe, 1)
                if 1 <= t <= 3 * AG and (t - 1) % 3 < 2:
                    over_rms(t - 1)
                if t <= LEVELS:
                    if t >= 1:
                        dve.wait_ge(s.gla_qe, t)
                    level_distance(t)
                lo(n + 6, n + 7)
                heads = t < 3 * AG and t % 3 < 2
                if heads:
                    nth = 2 * (t // 3) + t % 3
                    if nth >= 1:
                        dve.wait_ge(s.att_scaled, nth)
                    dve.wait_ge(s.att_squared, nth + 1)
                    v = st[:, 48:64].rearrange("p (a h) -> p a h", a=2)
                    nc.vector.tensor_reduce(v, asq.rearrange("p a (h c) -> p a h c", c=AD), AX.X,
                                            ALU.add).then_inc(s.att_ms, 1)
                    dve.wait_ge(s.att_ms, nth + 1)
                    v = st[:, 48:64]
                    root_guess(v, v, heads_newton[:, 0], heads_newton[:, 1]).then_inc(s.root_guessed, 1)
                if 1 <= t <= 9:
                    dve.wait_ge(s.gla_level, t)
                if t == 1:
                    nc.vector.tensor_copy(flat(g_cross), bank[:, 4, :]).then_inc(s.gla_taken, 1)
                elif 2 <= t <= 9:
                    lv = LEVELS if t == 9 else LEVELS - t + 1
                    mask = levels[:, lv:lv + 1, :].bitcast(I32).to_broadcast([P, 8, P])
                    nc.vector.copy_predicated(g_in.rearrange("p h a t -> p (h a) t"), mask,
                                              bank[:, 4:6, :].rearrange("p b (n t) -> p (b n) t", t=P)).then_inc(
                                                  s.gla_taken, 1)
            lo(2 * M_GATE + 4)
            def att_out(a):
                dve.wait_ge(s.att_pv, AH * (a + 1))
                sums = st[:, 80 + AH * a:88 + AH * a]
                link(nc.vector.reciprocal(sums, sums))
                nc.vector.tensor_tensor(oa[:, a, :].rearrange("p (h c) -> p h c", c=AD),
                                        bank[:, 7, :].rearrange("p (h c) -> p h c", c=AD),
                                        sums.rearrange("p (h o) -> p h o", o=1).to_broadcast([P, AH, AD]),
                                        ALU.mult).then_inc(s.att_o, 1)

            def gates_over_rms(f):
                g = f // 4
                c = C_GATE + g
                dve.wait_ge(s.mm_done, 2 * M_GATE + f + 1)
                nc.vector.tensor_tensor(gates[g // 2][:, g % 2 * 4:g % 2 * 4 + 4, :],
                                        pair(c).rearrange("p b (k t) -> p (b k) t", k=2),
                                        r_row.rearrange("p (o t) -> p o t", o=1).to_broadcast([P, 4, TOKENS]),
                                        ALU.mult).then_inc(acc_free[c % 2], 1)

            dve.wait_ge(s.dil_in, 16)
            for u in range(2 * AH):
                a = u // AH
                keys = AG * (a + 1) * P
                dve.wait_ge(s.att_scores, u + 1)
                if u >= 2:
                    dve.wait_ge(s.att_turnedp, u - 1 if u - 2 < AH else AH + 2 * (u - 2 - AH) + 2)
                src = bank[:, 4 + u % 2, 0:keys] if a == 0 else flat(bank[:, 4:6, :])[:, 0:keys]
                nc.vector.tensor_tensor(p[:, u % 2, 0:keys], src, dil[:, 3 * P * a:3 * P * a + keys],
                                        ALU.add).then_inc(s.att_masked, 1)
                dve.wait_ge(s.att_masked, u + 1)
                nc.vector.tensor_reduce(st[:, 32 + u:33 + u], p[:, u % 2, 0:keys], AX.X, ALU.max,
                                        negate=True).then_inc(s.att_max, 1)
                if u > 0:
                    lo(2 * M_GATE + 4 + u)
                if u == 2:
                    dve.wait_ge(s.gla_ssq, 1)
                    root_guess(st[:, 16:24], st[:, 16:24], heads_newton[:, 0, 0:8], heads_newton[:, 1, 0:8]).then_inc(
                        s.root_guessed, 1)
                if u == 4:
                    dve.wait_ge(s.root_found, 2 * AG + 1)
                    for c in (C_R, C_R + 1):
                        dve.wait_ge(acc_free[c % 2], c // 2 + 1)
                if 4 <= u < 8:
                    for at in (2 * u - 8, 2 * u - 7):
                        a, cols = at // GH, slice(at % GH * GV, at % GH * GV + GV)
                        ins = nc.vector.scalar_tensor_tensor(go[:, a, cols], go[:, a, cols], st[:, 16 + at:17 + at],
                                                             silu_r[:, a, cols], ALU.mult, ALU.mult)
                    if u == 7:
                        ins.then_inc(s.gla_ready, 1)
                if u % 4 == 3:
                    gates_over_rms(u)
                if u == AH:
                    att_out(0)
            att_out(1)
            turned_lo(a_lo, a_hi, 4, 4, s.go_hi, 0, lambda k: column("gla_out_norm_g_2", k % 2), s.go_lo)
            turned_lo(a_lo, a_hi, 0, 4, s.oa_hi, 0, lambda k: 1.0, s.oa_lo, 6)
            turned_lo(a_lo, a_hi, 8, 4, s.go_hi, 2, lambda k: column("gla_out_norm_g_2", k % 2), s.go_lo)
            n = 2 * M_BR

            def mixed(q, mm):
                c = C_BR + q
                dve.wait_ge(s.mm_done, mm)
                for br in range(2):
                    ins = nc.vector.tensor_tensor(mix[:, br, q % 2, :], flat(gates[br][:, 2 * q:2 * q + 2, :]),
                                                  bank[:, 2 * (c % 2) + br, :], ALU.mult)
                ins.then_inc(acc_free[c % 2], 1)
                dve.wait_ge(acc_free[c % 2], c // 2 + 1)
                nc.vector.tensor_tensor(mix[:, 0, q % 2, :], mix[:, 0, q % 2, :], mix[:, 1, q % 2, :],
                                        ALU.add).then_inc(s.mix_ready, 1)
                dve.wait_ge(s.mix_hi, q + 1)
                nc.vector.tensor_tensor(flat(h_lo[:, 2 * q:2 * q + 2, :]), mix[:, 0, q % 2, :],
                                        flat(h_hi[:, 2 * q:2 * q + 2, :]).bitcast(F32), ALU.subtract).then_inc(s.mix_lo, 1)

            lo(n + 4, n + 5, n + 6, n + 7)
            dve.wait_ge(s.gate_done, 4)
            mixed(0, n + 4)
            lo(n + 8, n + 9)
            mixed(1, n + 6)
            lo(n + 10, n + 11, n + 12, n + 13)
            mixed(2, n + 10)
            lo(n + 14, n + 15)
            mixed(3, n + 12)
            lo(*range(n + 16, n + 20))
            add_chunk(C_OUT2, C_OUT2, 2 * M_OUT2 + 4)
            lo(*range(n + 20, n + 24))
            add_chunk(C_OUT2 + 1, C_OUT2, 2 * M_OUT2 + 8)
            turned_lo(h_lo, h_hi, 0, KT, s.h_hi_done, 12, lambda k: column("norm2_g_2", k), s.h_lo_done)
            dve.wait_ge(s.ssq, 6)
            link(nc.vector.tensor_scalar(st[:, 2:4], st[:, 0:2], EPS, None, ALU.add))
            nc.vector.reciprocal(st[:, 2:4], st[:, 2:4])

            def ff2_chunk(j, e, split1, split2):
                dve.wait_ge(s.up_relu, j + 1)
                nc.vector.tensor_tensor(square2[:, e, :], relu2[:, e, :], relu2[:, e, :], ALU.mult).then_inc(
                    s.up_square, 1)
                split1()
                dve.wait_ge(s.up_hi, j + 1)
                nc.vector.tensor_tensor(flat(a_lo[:, 2 * e:2 * e + 2, :]), square2[:, e, :],
                                        flat(a_hi[:, 2 * e:2 * e + 2, :]).bitcast(F32), ALU.subtract).then_inc(
                                            s.up_lo, 1)
                split2()

            n3 = 2 * M_FF2
            ff2_chunk(0, 0, lambda: lo(n3 + 4, n3 + 5), lambda: None)
            with dve.Fori(0, CH2 // 3 - 1) as i:
                for e in range(3):
                    b = n3 + 4 * e
                    ff2_chunk(i * 3 + e + 1, (e + 1) % 3, lambda: lo(b + 6, b + 7, i=i), lambda: lo(b + 8, b + 9, i=i))
            for e in range(3):
                b = n3 + 12 * (CH2 // 3 - 1) + 4 * e
                ff2_chunk(CH2 - 3 + e, (e + 1) % 3, lambda: lo(b + 6, b + 7),
                          (lambda: lo(b + 8, b + 9)) if e < 2 else (lambda: None))
            add_down(2 * M_END, [st[:, 2 + a:3 + a] for a in range(TT)])


def kernel(**inputs):
    import concourse.bacc as bacc
    from concourse.bass_utils import run_bass_kernel_spmd

    nc = bacc.Bacc("TRN2", target_bir_lowering=False, num_devices=1)
    arrays, aps = {}, {}
    vectors = {name: np.asarray(inputs[name]).reshape(-1) for name in VEC if name != "ones"}
    vectors["ones"] = np.ones(4 * P, np.float32)
    for name in ("attn_q_norm_g_2", "attn_k_norm_g_2"):
        vectors[name] = np.tile(vectors[name], 2)
    laid_out = {"positions": np.asarray(inputs["positions"]).reshape(TT, P).T,
                "vectors": np.concatenate([vectors[name].reshape(-1, P) for name in VEC]).T}
    for name in PARTS:
        a = np.ascontiguousarray(laid_out.get(name, inputs.get(name)))
        arrays[f"in_{name}"] = a
        aps[name] = nc.dram_tensor(f"in_{name}", a.shape, mybir.dt.from_np(a.dtype), kind="ExternalInput").ap()
    arrays["constants"] = constants()
    consts = nc.dram_tensor("constants", (P, C_END), F32, kind="ExternalInput").ap()
    out = nc.dram_tensor("out", (1, TOKENS, D), F32, kind="ExternalOutput").ap()
    two_blocks_kernel(nc, Parts(**aps), consts, out)
    result = run_bass_kernel_spmd(nc, [arrays], core_ids=[0])
    return result.results[0]["out"]
```

```python
from collections import namedtuple
from contextlib import ExitStack

import numpy as np

import concourse.bass as bass
from concourse import mybir

P = 128
F32 = mybir.dt.float32
F32R = mybir.dt.float32r
I32 = mybir.dt.int32
ALU = mybir.AluOpType
ACT = mybir.ActivationFunctionType
AX = mybir.AxisListType

TOKENS, D = 256, 1024
TT = TOKENS // P
KT = D // P
EPS = 1e-6
RAW, RING = 3, 4
HALF = 1024

RH, RD = 8, 64
MH, NOPE, PE_D, MV = 8, 64, 32, 64
QK = NOPE + PE_D
QR, KVR = 256, 128
FF1 = 2816
CH1 = FF1 // 256
AH, AG, AD = 8, 3, 64
DIL = (1, 4, 16)
GH, GK, GV = 4, 128, 256
FF2 = 4096
CH2 = FF2 // 256
AW = AG * AH * AD
GQ0 = 3 * AW
GK0, GV0 = GQ0 + 512, GQ0 + 1024
GR0 = GV0 + 1024
GA0 = GR0 + 1024
GG0 = GA0 + 16

NEG = -1e30
LEVELS = 7

VEC = {}
_r = 0
for _name, _n in (("attn_norm_w", 8), ("ffn_norm_w", 8), ("norm1_g_2", 8), ("norm2_g_2", 8),
                  ("branch_gate_bias_2", 16), ("ret_gn_w", 4), ("ones", 4), ("mla_q_norm_w", 2), ("mla_kv_norm_w", 1),
                  ("gla_gate_bias_2", 4), ("gla_out_norm_g_2", 2), ("final_norm_w", 8),
                  ("attn_q_norm_g_2", 1), ("attn_k_norm_g_2", 1), ("conv_b", 44), ("conv_w", 132)):
    VEC[_name] = (_r, _n)
    _r += _n
VCOLS = _r
CW0 = VEC["conv_w"][0]
CW1, CW2 = CW0 + 44, CW0 + 88

C_IDENT = 0
C_INVF = C_IDENT + P
C_CAUSAL = C_INVF + 48
C_DECAY = C_CAUSAL + 3 * P
C_DIL = C_DECAY + RH * 3 * P
C_LEVEL = C_DIL + 9 * P
C_END = C_LEVEL + (LEVELS + 1) * P


def constants():
    t = np.zeros((P, C_END), np.float32)
    t[:, C_IDENT:C_IDENT + P] = np.eye(P)
    t[:, C_INVF:C_INVF + 32] = 10000.0 ** (-np.arange(0, 64, 2) / 64)
    t[:, C_INVF + 32:C_INVF + 48] = 10000.0 ** (-np.arange(0, 32, 2) / 32)
    i = np.arange(P)
    late = np.where(i[None, :] <= i[:, None], 0.0, NEG)
    t[:, C_CAUSAL:C_CAUSAL + P] = late
    t[:, C_CAUSAL + 2 * P:C_CAUSAL + 3 * P] = late
    for h in range(RH):
        log_gamma = np.log1p(-(2.0 ** (-5.0 - h)))
        for n, shift in enumerate((0, P, 0)):
            d = shift + i[None, :] - i[:, None]
            at = C_DECAY + (3 * h + n) * P
            t[:, at:at + P] = np.where(d >= 0, np.exp(log_gamma * np.maximum(d, 0)), 0) * RD ** -0.5
    for a in range(TT):
        keys = (a + 1) * P
        d = a * P + i[:, None] - np.arange(keys)[None, :]
        for g, dil in enumerate(DIL):
            ok = (d >= 0) & (d % dil == 0) & (d <= P * dil)
            at = C_DIL + 3 * P * a + g * keys
            t[:, at:at + keys] = np.where(ok, 0.0, NEG)
    for lv in range(LEVELS):
        b = 2 << lv
        ok = (i[:, None] // b == i[None, :] // b) & (i[:, None] % b < b // 2) & (i[None, :] % b >= b // 2)
        t[:, C_LEVEL + lv * P:C_LEVEL + (lv + 1) * P] = ok
    t[:, C_LEVEL + LEVELS * P:C_END] = np.eye(P)
    return t


M_FF1 = 16
M_IN2 = M_FF1 + 3 * CH1
M_ATT = M_IN2 + 9
M_R = M_ATT + 6 * AG
M_GATE = M_R + 4
M_BR = M_GATE + 8
M_OUT2 = M_BR + 6
M_FF2 = M_OUT2 + 4
M_END = M_FF2 + 2 * CH2
C_OUT, C_GLA, C_ATT, C_R = 9, 11, 16, 25
C_GATE, C_BR, C_OUT2 = 27, 31, 35

PARTS = ("x", "positions", "w_in", "w_uq", "w_ukv", "w_out", "w_up", "w_down", "final_norm_w", "w_in_2",
         "gla_gate_up_2", "w_attn_branch_2", "w_gla_branch_2", "w_out_2", "w_ff_up_2", "w_ff_down_2", "vectors")
Parts = namedtuple("Parts", PARTS)

TWO_PI = (6.28125, 0.0019350051879882812, 3.0199159819e-07)
MAGIC = 1.5 * 2 ** 23
ROOT_GUESS = 0x5F3759DF


def slab_table(w):
    def rows(x, k0, k1, c0, c1):
        return x[k0 * P:k1 * P, c0:c1].rearrange("(k p) c -> p k c", p=P)

    def chunk(x, c0, c1):
        return [(rows(x, k, k + 4, c0, c1), 2 * (c1 - c0), 0) for k in (0, 4)]

    w_in, w_in_2 = w.w_in[0], w.w_in_2[0]
    one = chunk(w_in, 2048, 2464) + chunk(w_in, 0, 512) + chunk(w_in, 512, 1024)
    one += [(rows(w.w_uq[0], 0, 2, 0, 768), 768, 0), (rows(w.w_ukv[0], 0, 1, 0, 1024), 512, 0)]
    one += chunk(w_in, 1024, 1536) + chunk(w_in, 1536, 2048)
    mixer = chunk(w.w_out[0], 0, 512) + chunk(w.w_out[0], 512, 1024)
    one += [mixer[n] for n in (0, 2, 1, 3)]
    assert len(one) == M_FF1

    two = chunk(w_in_2, GQ0, GQ0 + 512) + chunk(w_in_2, GK0, GK0 + 512)
    two += [(rows(w_in_2, 0, KT, GA0, GA0 + 16), 64, 0)]
    two += chunk(w_in_2, GV0, GV0 + 512) + chunk(w_in_2, GV0 + 512, GV0 + 1024)
    for g in range(AG):
        for part in range(3):
            two += chunk(w_in_2, part * AW + g * 512, part * AW + g * 512 + 512)
    for c in (GR0, GR0 + 512):
        two += chunk(w_in_2, c, c + 512)
    for c in range(GG0, GG0 + 2048, 256):
        two += [(rows(w_in_2, 0, KT, c, c + 256), HALF, 256)]
    for c in (0, 512):
        two += [(rows(w.w_attn_branch_2[0], 0, 4, c, c + 512), HALF, 512)]
        two += [(rows(w.w_gla_branch_2[0], 0, KT, q, q + 256), HALF, 256) for q in (c, c + 256)]
    for c in (0, 512):
        two += chunk(w.w_out_2[0], c, c + 512)
    assert len(two) == M_FF2 - M_IN2
    return {**dict(enumerate(one)), **{M_IN2 + n: t for n, t in enumerate(two)}}


def ffn_columns(m):
    if m < M_IN2:
        return 0 if m == M_IN2 - 1 or m >= M_FF1 + 2 and (m - M_FF1 - 2) % 3 == 2 else 256
    return 0 if m == M_END - 1 or (m > M_FF2 and (m - M_FF2) % 2 == 0) else 256


SEMAPHORES = (
    "x_in ident_in pos_in consts_in vecs_in fw_in gate_up_in levels_in dil_in out_stored "
    "hi_done lo_done mm_done acc_free0 acc_free1 "
    "act_chain dve_chain pool_chain "
    "ssq inverse_rms x_scaled x_turned h_hi_done h_lo_done x_added x_tiles tile_done "
    "trig_arg trig latent_scaled latents_turned latents_hi latents_lo "
    "mla_q_ready mla_k_ready mla_q_turned mla_k_turned mla_qT mla_kT mla_scores mla_masked mla_max mla_exp "
    "mla_turned mla_pt mla_pv mla_o "
    "ret_roped ret_q_turned ret_k_turned ret_qT ret_kT ret_scores ret_masked ret_o_head ret_copied "
    "ret_centred ret_sq ret_y mixed_turned mixed_hi mixed_lo "
    "taps tap1 gate_conv val_conv gate_silu act_ready act_hi_done act_lo_done "
    "gla_turned gla_qT gla_kT pa_turned pa_T gla_logits gla_z gla_soft gla_diff "
    "gla_e gla_qe gla_level gla_taken gla_o gla_go gla_ssq gla_ready gate_done "
    "go_turned go_hi go_lo "
    "att_squared att_ms root_guessed root_found att_scaled att_turned att_T "
    "att_scores att_masked att_max att_exp att_turnedp att_pt att_pv att_o oa_turned oa_hi oa_lo "
    "mix_ready mix_hi mix_lo "
    "up_relu up_square up_hi up_lo"
).split()
Semaphores = namedtuple("Semaphores", SEMAPHORES)


def two_blocks_kernel(nc, w, consts, out):
    with ExitStack() as ctx:
        def sb(name, shape, dt=F32):
            return ctx.enter_context(nc.sbuf_tensor(name, shape, dt))

        bank = ctx.enter_context(nc.psum_tensor("bank", [P, 8, 512], F32))
        raw = sb("raw", [P, RAW, 2 * HALF])
        w_hi = sb("w_hi", [P, RING, HALF], F32R)
        w_lo = sb("w_lo", [P, RING, HALF], F32R)
        h_hi = sb("h_hi", [P, KT, TOKENS], F32R)
        h_lo = sb("h_lo", [P, KT, TOKENS], F32R)
        a_hi = sb("a_hi", [P, 12, TOKENS], F32R)
        a_lo = sb("a_lo", [P, 12, TOKENS], F32R)
        x = sb("x_tok", [P, TT, D])
        ident = sb("ident", [P, P])
        vec = sb("vec", [P, VCOLS])
        newton = sb("newton", [P, 2, 16])
        heads_newton = sb("heads_newton", [P, 2, 16])
        st = sb("stats", [P, 96])
        arena = sb("arena", [P, 26016])

        s = Semaphores(*[ctx.enter_context(nc.semaphore(n)) for n in SEMAPHORES])
        raw_in = [ctx.enter_context(nc.semaphore(f"raw_in{r}")) for r in range(RAW)]
        acc_free = (s.acc_free0, s.acc_free1)
        table = slab_table(w)
        IN2_BANKS = (0, 1, 4, 5)

        def area(at, *dims):
            n = 1
            for d in dims:
                n *= d
            v = arena[:, at:at + n]
            if len(dims) == 2:
                return v.rearrange("p (a b) -> p a b", b=dims[1])
            if len(dims) == 3:
                return v.rearrange("p (a b c) -> p a b c", b=dims[1], c=dims[2])
            if len(dims) == 4:
                return v.rearrange("p (a b c d) -> p a b c d", b=dims[1], c=dims[2], d=dims[3])
            return v

        def column(name, k=0):
            r = VEC[name][0] + k
            return vec[:, r:r + 1]

        def flat(v):
            return v.rearrange("p a b -> p (a b)")

        def raw_half(r, half, size, cols):
            if not cols:
                return raw[:, r, half * size:(half + 1) * size]
            c = cols // 2
            return raw[:, r, 0:2 * size].rearrange("p (k c) -> p k c", c=cols)[:, :, half * c:(half + 1) * c]

        def pair(c, width=512):
            return bank[:, 2 * (c % 2):2 * (c % 2) + 2, 0:width]

        xn = area(0, TT, D)
        proj = area(4096, TT, 2464)
        causal = area(9024, 3 * P)
        decay = area(9408, RH, 3 * P)
        q_tok = area(12480, TT, MH, QK)
        k_tok = area(14016, TT, MH, QK)
        kv = area(15552, TT, MH, NOPE + MV)
        mqT = area(17600, MH, TOKENS)
        mkT = area(19648, MH, TOKENS)
        rqT = area(21696, RH // 2, TOKENS)
        rkT = area(22720, RH // 2, TOKENS)
        sT = area(23744, 2, 3 * P)
        pT = area(24512, 2, 3 * P)
        rope_tmp = area(0, 2, RH * RD // 2)
        r_row = area(2048, TOKENS)
        angle = area(25280, 2, TT, 48)
        turns = area(25472, 2, TT, 48)
        pos_i = area(25664, TT)
        pos_f = area(25666, TT)
        invf = area(25668, 48)
        conv = area(0, 2, 2, 512)
        silu1 = area(2048, 2, 512)
        act1 = area(3072, 2, 512)
        fw = area(24864, D)
        gqk = area(0, 2, TT, 512)
        qe = area(0, GH, TOKENS)
        ke = area(1024, GH, TOKENS)
        soft = area(2048, GH * TOKENS)
        gv = area(3072, TT, GH * GV)
        gqT = area(5120, GH, TOKENS)
        gkT = area(6144, GH, TOKENS)
        run = area(7168, GH * TOKENS)
        z = area(8192, GH * TOKENS)
        g_in = area(9216, GH, TT, P)
        resets = area(9216, GH * TOKENS)
        g_cross = area(10240, GH, P)
        levels = area(10752, LEVELS + 1, P)
        paT = area(11776, TOKENS)
        gate_up = area(12032, GH * GK)
        ga = area(12544, TT, 16)
        a_tok = area(12576, 2, TT, 512)
        aqT = area(14624, 4 * AG, TOKENS)
        akT = area(17696, 4 * AG, TOKENS)
        av = area(20768, TT, AW)
        asq = area(23840, TT, 512)
        dil = area(24864, 9 * P)
        go = area(5120, TT, GH * GV)
        silu_r = area(0, TT, GH * GV)
        go_squares = area(3072, TT, GH * GV)
        gates = (area(3072, KT, TOKENS), area(7168, KT, TOKENS))
        p = area(9216, 2, 6 * P)
        ppT = area(10752, 2, 6 * P)
        oa = area(23840, TT, 512)
        mix = area(12576, 2, 2, 512)
        relu2 = area(3072, 3, 512)
        square2 = area(4608, 3, 512)

        def turn(dst, src, rows=P):
            return nc.tensor.transpose(dst, src, ident[0:rows, 0:rows])

        block = ctx.enter_context(nc.Block())

        @block.sync
        def _(sp):
            def load_slab(slot, m, dst, src):
                if not isinstance(m, int) or m >= RAW:
                    sp.wait_ge(s.lo_done, m * 2 - 2 * RAW + 2)
                sp.dma_start(dst, src).then_inc(raw_in[slot], 16)

            def load(m):
                src = table[m][0]
                _, k, c = src.shape
                load_slab(m % RAW, m, raw[:, m % RAW, 0:k * c].rearrange("p (k c) -> p k c", c=c), src)

            def load_ffn(m0, i, src):
                m = m0 if i is None else i * 6 + m0
                k = src.shape[1]
                load_slab(m0 % RAW, m, raw[:, m0 % RAW, :].rearrange("p (k c) -> p k c", k=k), src)

            sp.dma_start(ident[:], consts[:, C_IDENT:C_IDENT + P]).then_inc(s.ident_in, 16)
            sp.dma_start(x[:], w.x[0].rearrange("(a p) d -> p a d", p=P)).then_inc(s.x_in, 16)
            load(0)
            load(1)
            sp.dma_start(pos_i.bitcast(I32), w.positions).then_inc(s.pos_in, 16)
            sp.dma_start(invf, consts[:, C_INVF:C_INVF + 48]).then_inc(s.pos_in, 16)
            load(2)
            sp.dma_start(causal, consts[:, C_CAUSAL:C_CAUSAL + 3 * P]).then_inc(s.consts_in, 16)
            sp.dma_start(decay, consts[:, C_DECAY:C_DIL].rearrange("p (h c) -> p h c", h=RH)).then_inc(s.consts_in, 16)
            for m in range(3, M_FF1):
                load(m)

            up = w.w_up[0].rearrange("(k p) c -> p k c", p=P)
            down = w.w_down[0].rearrange("(n k p) c -> n p k c", k=2, p=P)
            load_ffn(M_FF1, None, up[:, :, 0:256])
            load_ffn(M_FF1 + 1, None, up[:, :, FF1:FF1 + 256])
            with sp.Fori(0, CH1 // 2) as i:
                for e in range(2):
                    m = M_FF1 + 2 + 3 * e
                    load_ffn(m, i, up[:, :, bass.ds(i * 512 + 256 * (e + 1), 256)])
                    load_ffn(m + 1, i, up[:, :, bass.ds(i * 512 + FF1 + 256 * (e + 1), 256)])
                    load_ffn(m + 2, i, down[bass.ds(i * 2 + e, 1)].rearrange("n p k c -> p (n k) c"))
            load_ffn(M_IN2 - 1, None, down[CH1 - 1])

            load(M_IN2)
            sp.wait_ge(s.mm_done, 2 * M_FF1)
            sp.dma_start(fw, w.final_norm_w.rearrange("(o d) -> o d", o=1).to_broadcast([P, D])).then_inc(s.fw_in, 16)
            sp.dma_start(gate_up[0:16, :], w.gla_gate_up_2[0]).then_inc(s.gate_up_in, 16)
            sp.dma_start(levels, consts[:, C_LEVEL:C_END].rearrange("p (l c) -> p l c", c=P)).then_inc(s.levels_in, 16)
            for m in range(M_IN2 + 1, M_IN2 + 5):
                load(m)
            sp.wait_ge(s.x_added, 1)
            sp.dma_start(dil, consts[:, C_DIL:C_LEVEL]).then_inc(s.dil_in, 16)
            for m in range(M_IN2 + 5, M_FF2):
                load(m)

            up = w.w_ff_up_2[0].rearrange("(k p) c -> p k c", p=P)
            down = w.w_ff_down_2[0].rearrange("(n k p) c -> n p k c", k=2, p=P)
            load_ffn(M_FF2, None, up[:, :, 0:256])
            with sp.Fori(0, CH2 // 3) as i:
                for e in range(3):
                    m = M_FF2 + 1 + 2 * e
                    load_ffn(m, i, up[:, :, bass.ds(i * 768 + 256 * (e + 1), 256)])
                    load_ffn(m + 1, i, down[bass.ds(i * 3 + e, 1)].rearrange("n p k c -> p (n k) c"))
            load_ffn(M_END - 1, None, down[CH2 - 1])

            for a in range(TT):
                sp.wait_ge(s.x_added, 2 + a)
                sp.dma_start(out[0].rearrange("(a p) d -> a p d", p=P)[a], x[:, a, :]).then_inc(s.out_stored, 16)
            sp.wait_ge(s.out_stored, 16 * TT)

        @block.gpsimd
        def _(gp):
            steps = 0

            def link(ins):
                nonlocal steps
                steps += 1
                ins.then_inc(s.pool_chain, 1)
                gp.wait_ge(s.pool_chain, steps)

            for n in range(2 * AG + 2):
                v = st[:, 64:80] if n == 0 else st[:, 48:64] if n <= 2 * AG else st[:, 16:24]
                y, t = [heads_newton[:, i, 0:v.shape[1]] for i in range(2)]
                gp.wait_ge(s.root_guessed, n + 1)
                for step in range(3):
                    link(nc.gpsimd.tensor_tensor(t, y, y, ALU.mult))
                    link(nc.gpsimd.tensor_tensor(t, t, v, ALU.mult))
                    link(nc.gpsimd.tensor_scalar(t, t, -0.5, 1.5, ALU.mult, ALU.add))
                    if step < 2:
                        link(nc.gpsimd.tensor_tensor(y, y, t, ALU.mult))
                nc.gpsimd.tensor_tensor(v, y, t, ALU.mult).then_inc(s.root_found, 1)

        @block.tensor
        def _(pe):
            def passes(dst, l_hi, l_lo, r_hi, r_lo, start, stop):
                nc.tensor.matmul(dst, l_hi, r_hi, start=start, stop=False)
                nc.tensor.matmul(dst, l_hi, r_lo, start=False, stop=False)
                return nc.tensor.matmul(dst, l_lo, r_hi, start=False, stop=stop)

            LAST = "last"

            def half_rows(n, width, k0, kn, lhs, accs, first, last, ready=None, i=None):
                q = n % RING
                pe.wait_ge(s.lo_done, n + 1 if i is None else i * 12 + n + 1)
                for k in range(kn):
                    if ready:
                        ready(k0 + k)
                    for a in range(TT):
                        for acc, c0, c1 in accs[a]:
                            at = k * width
                            ins = passes(acc, lhs[0][:, k0 + k, a * P:(a + 1) * P], lhs[1][:, k0 + k, a * P:(a + 1) * P],
                                         w_hi[:, q, at + c0:at + c1], w_lo[:, q, at + c0:at + c1],
                                         first and k == 0, last and k == kn - 1)
                ins.then_inc(s.mm_done, 1)

            def last_halves(n, width, ks, kn, lhs, accs, ready=None):
                pe.wait_ge(s.lo_done, n + 2)
                for a in range(TT):
                    for e in range(2):
                        q = (n + e) % RING
                        for k in range(kn):
                            if ready and a == 0:
                                ready(ks[e] + k)
                            l_hi, l_lo = [lhs[i][:, ks[e] + k, a * P:(a + 1) * P] for i in range(2)]
                            for acc, c0, c1 in accs[a]:
                                at = k * width
                                ins = passes(acc, l_hi, l_lo, w_hi[:, q, at + c0:at + c1], w_lo[:, q, at + c0:at + c1],
                                             False, e == 1 and k == kn - 1)
                    ins.then_inc((s.tile_done, s.mm_done)[a], a + 1)

            def chunk_rows(n, c, width, lhs, ready=None, halves=(0, 1, 2, 3), kn=2):
                if halves == LAST:
                    last_halves(n + 2, width, (4, 6), kn, lhs, [[(pair(c, width)[:, a], 0, width)] for a in range(TT)],
                                ready)
                    return
                for e in halves:
                    if e == 0:
                        pe.wait_ge(acc_free[c % 2], c // 2)
                    half_rows(n + e, width, kn * e, kn, lhs, [[(pair(c, width)[:, a], 0, width)] for a in range(TT)],
                              e == 0, e == KT // kn - 1, ready)

            def half_columns(n, kn, c, dst, lhs, i=None, ready=None):
                q = n % RING
                pe.wait_ge(s.lo_done, n + 1 if i is None else i * 12 + n + 1)
                for t in range(c):
                    for k in range(kn):
                        if ready:
                            ready(k)
                        at = (k * c + t) * P
                        wh, wl = w_hi[:, q, at:at + P], w_lo[:, q, at:at + P]
                        ins = passes(dst[:, t * TOKENS:(t + 1) * TOKENS], wh, wl, lhs[0][:, k, :], lhs[1][:, k, :],
                                     k == 0, k == kn - 1)
                ins.then_inc(s.mm_done, 1)

            def turn_x(src, added, banks=(4, 5, 6, 7)):
                for a in range(TT):
                    added(a)
                    for k in range(KT):
                        ins = turn(bank[:, banks[k // 2], k % 2 * TOKENS + a * P:k % 2 * TOKENS + (a + 1) * P],
                                   src[:, a, k * P:(k + 1) * P])
                        if a == 1 and k % 2 == 1:
                            ins.then_inc(s.x_turned, 1)

            def turn_tiles(count, src, done, banks=(4, 5, 6, 7), free=None):
                for k in range(count):
                    b = banks[k // 2]
                    if k % 2 == 0 and free:
                        free(k // 2)
                    for a in range(TT):
                        at = k % 2 * TOKENS + a * P
                        ins = turn(bank[:, b, at:at + P], src(a, k))
                    if k % 2 == 1 or k == count - 1:
                        ins.then_inc(done, 1)

            h, al = (h_hi, h_lo), (a_hi, a_lo)

            def h_ready(norm):
                return lambda k: pe.wait_ge(s.h_lo_done, 4 * norm + k // 2 + 1) if k % 2 == 0 else None

            pe.wait_ge(s.ident_in, 16)
            turn_x(x, lambda a: pe.wait_ge(s.x_in, 16))
            ready = h_ready(0)
            chunk_rows(0, 0, 416, h, ready)
            chunk_rows(4, 1, 512, h)
            pe.wait_ge(s.latent_scaled, 1)
            turn_tiles(3, lambda a, k: proj[:, a, 2048 + k * P:2176 + k * P], s.latents_turned)
            chunk_rows(8, 2, 512, h)
            pe.wait_ge(s.latents_lo, 1)
            pe.wait_ge(s.acc_free1, 1)
            pe.wait_ge(s.acc_free0, 2)
            for k in range(2):
                half_rows(12 + k, 768, k, 1, al, [[(pair(3 + a)[:, 0], 0, 512), (pair(3 + a, 256)[:, 1], 512, 768)]
                                                  for a in range(TT)], k == 0, k == 1)
            pe.wait_ge(s.latents_lo, 2)
            for e in range(2):
                half_rows(14 + e, 512, 2, 1, al, [[(bank[:, 4 + 2 * a + e, :], 0, 512)] for a in range(TT)], True, True)
            chunk_rows(16, 7, 512, h, halves=(0, 1))
            pe.wait_ge(s.acc_free1, 3)
            pe.wait_ge(s.acc_free0, 4)
            pe.wait_ge(s.ret_roped, 1)
            turn_tiles(4, lambda a, k: proj[:, a, k * P:(k + 1) * P], s.ret_q_turned, (4, 5))
            turn_tiles(4, lambda a, k: proj[:, a, 512 + k * P:640 + k * P], s.ret_k_turned, (6, 7))
            chunk_rows(16, 7, 512, h, halves=(2, 3))
            pe.wait_ge(s.mla_q_ready, 1)
            pe.wait_ge(s.ret_qT, 2)
            pe.wait_ge(s.ret_kT, 2)
            for hd in range(MH):
                for a in range(TT):
                    at = hd % 2 * TOKENS + a * P
                    ins = turn(bank[0:QK, 4 + hd // 2, at:at + P], q_tok[:, a, hd, :])
                if hd % 2:
                    ins.then_inc(s.mla_q_turned, 1)
            chunk_rows(20, 8, 512, h, halves=(0,))
            pe.wait_ge(s.mla_k_ready, 1)
            for hd in range(MH):
                if hd % 2 == 0:
                    pe.wait_ge(s.mla_qT, hd // 2 + 1)
                for a in range(TT):
                    at = hd % 2 * TOKENS + a * P
                    ins = turn(bank[0:QK, 4 + hd // 2, at:at + P], k_tok[:, a, hd, :])
                if hd % 2:
                    ins.then_inc(s.mla_k_turned, 1)
            chunk_rows(20, 8, 512, h, halves=(1,))

            def ret_score(hd):
                if hd >= 2:
                    pe.wait_ge(s.ret_masked, hd - 1)
                r = hd % 2 * RD
                q, k = rqT[r:r + RD, hd // 2, :], rkT[r:r + RD, hd // 2, :]
                b = bank[:, 4 + hd % 2, :]
                nc.tensor.matmul(b[:, 0:2 * P], k[:, 0:P], q, start=True, stop=True)
                nc.tensor.matmul(b[:, 2 * P:3 * P], k[:, P:2 * P], q[:, P:2 * P], start=True,
                                 stop=True).then_inc(s.ret_scores, 1)

            pe.wait_ge(s.mla_kT, 4)
            ret_score(0)
            ret_score(1)
            pe.wait_ge(s.acc_free1, 4)
            for hd in range(RH):
                if hd in (1, 3):
                    chunk_rows(20, 8, 512, h, halves=((hd + 3) // 2,))
                pe.wait_ge(s.ret_masked, hd + 1)
                v = [proj[:, a, 1024 + hd * RD:1024 + (hd + 1) * RD] for a in range(TT)]
                o = [bank[:, 6 + a, hd * RD:(hd + 1) * RD] for a in range(TT)]
                w_ = sT[:, hd % 2, :]
                nc.tensor.matmul(o[0], w_[:, 0:P], v[0], start=True, stop=True)
                nc.tensor.matmul(o[1], w_[:, P:2 * P], v[0], start=True, stop=False)
                nc.tensor.matmul(o[1], w_[:, 2 * P:3 * P], v[1], start=False, stop=True).then_inc(s.ret_o_head, 1)
                if hd + 2 < RH:
                    ret_score(hd + 2)

            def mla_score(hd):
                if hd >= 2:
                    pe.wait_ge(s.mla_masked, hd - 1)
                b = bank[:, 4 + hd % 2, :]
                nc.tensor.matmul(b[:, 0:P], mqT[0:QK, hd, 0:P], mkT[0:QK, hd, 0:P], start=True, stop=True)
                nc.tensor.matmul(b[:, P:3 * P], mqT[0:QK, hd, P:2 * P], mkT[0:QK, hd, :], start=True,
                                 stop=True).then_inc(s.mla_scores, 1)

            def mla_value(hd):
                pe.wait_ge(s.mla_pt, hd + 1)
                if hd == 4:
                    pe.wait_ge(s.mla_o, 1)
                o = bank[:, 7, hd % 4 * 128:hd % 4 * 128 + 128]
                v = [kv[:, a, hd, NOPE:NOPE + MV] for a in range(TT)]
                w_ = pT[:, hd % 2, :]
                nc.tensor.matmul(o[:, 0:64], w_[:, 0:P], v[0], start=True, stop=True)
                nc.tensor.matmul(o[:, 64:128], w_[:, P:2 * P], v[0], start=True, stop=False)
                nc.tensor.matmul(o[:, 64:128], w_[:, 2 * P:3 * P], v[1], start=False, stop=True).then_inc(s.mla_pv, 1)

            pe.wait_ge(s.ret_masked, RH)
            mla_score(0)
            mla_score(1)
            for hd in range(MH):
                if hd == 4:
                    pe.wait_ge(s.ret_y, 1)
                    turn_tiles(4, lambda a, k: proj[:, a, k * P:(k + 1) * P], s.mixed_turned, (2, 3))
                if hd == 5:
                    pe.wait_ge(s.mixed_lo, 2)
                    chunk_rows(24, C_OUT, 512, al, halves=(0,))
                if hd == 6:
                    chunk_rows(24, C_OUT, 512, al, halves=(1,))
                pe.wait_ge(s.mla_exp, hd + 1)
                if hd == 0:
                    pe.wait_ge(s.ret_copied, 1)
                else:
                    pe.wait_ge(s.mla_pt, hd)
                for n in range(3):
                    ins = turn(bank[:, 6, n * P:(n + 1) * P], sT[:, hd % 2, n * P:(n + 1) * P])
                ins.then_inc(s.mla_turned, 1)
                if hd + 2 < MH:
                    mla_score(hd + 2)
                if hd >= 1:
                    mla_value(hd - 1)
            mla_value(MH - 1)
            chunk_rows(26, C_OUT + 1, 512, al, halves=(0,))
            pe.wait_ge(s.mla_masked, MH)
            pe.wait_ge(s.mla_o, 2)
            turn_tiles(4, lambda a, k: proj[:, a, 512 + k * P:640 + k * P], s.mixed_turned, (4, 5))
            chunk_rows(26, C_OUT + 1, 512, al, halves=(1,))
            for c in range(2):
                chunk_rows(26 + 2 * c, C_OUT + c, 512, al,
                           lambda k: pe.wait_ge(s.mixed_lo, k // 2 + 1) if k % 2 == 0 else None,
                           halves=(2, 3) if c == 0 else LAST)

            turn_x(xn, lambda a: pe.wait_ge(s.x_scaled, a + 1))
            ready = h_ready(1)

            def ff1_up(n, e, i=None, j0=None, ready=None):
                for v in range(2):
                    if i is not None or j0 >= 2:
                        pe.wait_ge((s.gate_conv, s.val_conv)[v], j0 - 1 if i is None else i * 2 + j0 - 1)
                    for f in range(2):
                        half_columns(n + 2 * v + f, KT, 1, bank[:, 2 * e + v, f * TOKENS:(f + 1) * TOKENS], h, i,
                                     ready if v == f == 0 else None)

            down_banks = [[(bank[:, 4 + 2 * a + b, :], 512 * b, 512 * b + 512) for b in range(2)] for a in range(TT)]

            def ff_down(n, at, first, last, act, i=None):
                act()
                for k in range(2):
                    half_rows(n + k, 1024, at + k, 1, al, down_banks, first and k == 0, last and k == 1, None, i)

            n1 = 2 * M_FF1
            pe.wait_ge(s.acc_free0, 6)
            ff1_up(n1, 0, None, 0, ready)
            pe.wait_ge(s.acc_free1, 5)
            ff1_up(n1 + 4, 1, None, 1)
            ff_down(n1 + 8, 0, True, False, lambda: pe.wait_ge(s.act_lo_done, 1))
            ff1_up(n1 + 10, 0, None, 2)
            ff_down(n1 + 14, 2, False, False, lambda: pe.wait_ge(s.act_lo_done, 2))
            with pe.Fori(1, CH1 // 2) as i:
                ff1_up(n1 + 4, 1, i, 1)
                ff_down(n1 + 8, 0, False, False, lambda: pe.wait_ge(s.act_lo_done, i * 2 + 1), i)
                ff1_up(n1 + 10, 0, i, 2)
                ff_down(n1 + 14, 2, False, False, lambda: pe.wait_ge(s.act_lo_done, i * 2 + 2), i)
            pe.wait_ge(s.act_lo_done, CH1)
            last_halves(2 * M_IN2 - 2, 1024, (0, 1), 1, al, down_banks)

            n2 = 2 * M_IN2
            pe.wait_ge(s.val_conv, CH1)
            turn_x(x, lambda a: pe.wait_ge(s.x_tiles, 2 + a), IN2_BANKS)
            ready = h_ready(2)
            chunk_rows(n2, C_GLA, 512, h, ready)
            chunk_rows(n2 + 4, C_GLA + 1, 512, h)
            chunk_rows(n2 + 8, C_GLA + 2, 16, h, halves=(0, 1), kn=4)
            chunk_rows(n2 + 10, C_GLA + 3, 512, h)
            pe.wait_ge(s.acc_free1, 6)
            turn_tiles(4, lambda a, k: gqk[:, 0, a, k * P:(k + 1) * P], s.gla_turned, (4, 5))
            pe.wait_ge(s.acc_free0, 7)
            turn_tiles(4, lambda a, k: gqk[:, 1, a, k * P:(k + 1) * P], s.gla_turned, (6, 7))
            chunk_rows(n2 + 14, C_GLA + 4, 512, h, halves=(0, 1))
            pe.wait_ge(s.acc_free1, 7)
            pe.wait_ge(s.gla_qT, 1)
            for a in range(TT):
                turn(bank[0:16, 4, a * P:(a + 1) * P], ga[:, a, :])
            for a in range(TT):
                ins = nc.tensor.matmul(bank[:, 4, TOKENS + a * P:TOKENS + (a + 1) * P],
                                       st[:, 8 + a:9 + a].to_broadcast([P, P]), ident[:], start=True, stop=True)
            ins.then_inc(s.pa_turned, 1)
            chunk_rows(n2 + 14, C_GLA + 4, 512, h, halves=(2, 3))
            pe.wait_ge(s.pa_T, 1)
            pe.wait_ge(s.gate_up_in, 16)
            pe.wait_ge(s.gla_kT, 1)
            for hd in range(GH):
                ins = nc.tensor.matmul(bank[:, 6 + hd // 2, hd % 2 * TOKENS:(hd % 2 + 1) * TOKENS],
                                       gate_up[0:16, hd * GK:(hd + 1) * GK], paT[0:16, :], start=True, stop=True)
            ins.then_inc(s.gla_logits, 1)

            def turn_heads(t):
                nth = t // 3 * 2 + t % 3
                pe.wait_ge(s.att_scaled, nth + 1)
                if nth == 0:
                    pe.wait_ge(s.gla_z, 1)
                else:
                    pe.wait_ge(s.att_T, nth)
                turn_tiles(4, lambda a, k: a_tok[:, t % 3, a, k * P:(k + 1) * P], s.att_turned, (6, 7))

            def level(t):
                q_, k_ = (gqT, gkT) if t == 8 else (qe, ke)
                pe.wait_ge(s.gla_qe, min(t + 1, 8))
                if t >= 1:
                    pe.wait_ge(s.gla_taken, t)
                for hd in range(GH):
                    if t == 0:
                        ins = nc.tensor.matmul(bank[:, 4, hd * P:(hd + 1) * P], k_[:, hd, 0:P], q_[:, hd, P:2 * P],
                                               start=True, stop=True)
                    else:
                        for a in range(TT):
                            at = (hd % 2 * 2 + a) * P
                            ins = nc.tensor.matmul(bank[:, 4 + hd // 2, at:at + P], k_[:, hd, a * P:(a + 1) * P],
                                                   q_[:, hd, a * P:(a + 1) * P], start=True, stop=True)
                ins.then_inc(s.gla_level, 1)

            for t in range(3 * AG + 2):
                chunk_rows(n2 + 18 + 4 * t, C_ATT + t, 512, h)
                if t >= 1 and (t - 1) % 3 < 2 and t - 1 < 3 * AG:
                    turn_heads(t - 1)
                if 1 <= t <= 9:
                    level(t - 1)
            pe.wait_ge(s.gla_taken, 9)
            pe.wait_ge(s.att_T, 2 * AG)
            for a in range(TT):
                for hd in range(GH):
                    o = bank[:, 4 + 2 * a + hd // 2, hd % 2 * GV:(hd % 2 + 1) * GV]
                    v = [gv[:, t, hd * GV:(hd + 1) * GV] for t in range(TT)]
                    if a == 1:
                        nc.tensor.matmul(o, g_cross[:, hd, :], v[0], start=True, stop=False)
                    ins = nc.tensor.matmul(o, g_in[:, hd, a, :], v[a], start=a == 0, stop=True)
                ins.then_inc(s.gla_o, 1)

            def fill(f):
                c = C_GATE + f // 4
                if f % 4 == 0:
                    pe.wait_ge(acc_free[c % 2], c // 2)
                t = f % 4
                half_columns(2 * M_GATE + f, KT, 1, bank[:, 2 * (c % 2) + t // 2, t % 2 * TOKENS:(t % 2 + 1) * TOKENS], h)

            def att_score(u):
                a, i = u // AH, u % AH
                keys = (a + 1) * P
                r = i % 2 * AD
                if u >= 1:
                    pe.wait_ge(s.att_masked, u)
                for g in range(AG):
                    k = g * 4 + i // 2
                    at = (4 + u % 2) * 512 + g * keys if a == 0 else 4 * 512 + g * keys
                    ins = nc.tensor.matmul(bank[:, at // 512, at % 512:at % 512 + keys],
                                           aqT[r:r + AD, k, a * P:(a + 1) * P], akT[r:r + AD, k, 0:keys],
                                           start=True, stop=True)
                ins.then_inc(s.att_scores, 1)

            def att_turn(u, part):
                done = u if u < AH else AH + 2 * (u - AH)
                if part == 0:
                    pe.wait_ge(s.att_exp, u + 1)
                if done + part >= 1:
                    pe.wait_ge(s.att_pt, done + part)
                for b in range(3):
                    at = (3 * part + b) * P
                    ins = turn(bank[:, 6, b * P:(b + 1) * P], p[:, u % 2, at:at + P])
                ins.then_inc(s.att_turnedp, 1)

            def att_value(u):
                a, i = u // AH, u % AH
                pe.wait_ge(s.att_pt, u + 1 if a == 0 else AH + 2 * (u - AH) + 2)
                if u == AH:
                    pe.wait_ge(s.att_o, 1)
                o = bank[:, 7, i * AD:(i + 1) * AD]
                n = AG * (a + 1)
                for b in range(n):
                    g, t = b // (a + 1), b % (a + 1)
                    ins = nc.tensor.matmul(o, ppT[:, u % 2, b * P:(b + 1) * P],
                                           av[:, t, g * 512 + i * AD:g * 512 + (i + 1) * AD], start=b == 0, stop=b == n - 1)
                ins.then_inc(s.att_pv, 1)

            fill(0)
            pe.wait_ge(s.gla_go, 2)
            att_score(0)
            fill(1)
            for u in range(2 * AH):
                if 0 < u < 2 * AH - 1:
                    fill(u + 1)
                att_turn(u, 0)
                if u + 1 < 2 * AH:
                    att_score(u + 1)
                if u > 0:
                    att_value(u - 1)
                if u >= AH:
                    att_turn(u, 1)
            att_value(2 * AH - 1)

            pe.wait_ge(s.gla_ready, 1)
            pe.wait_ge(s.att_masked, 2 * AH)
            turn_tiles(4, lambda a, k: go[:, a, k * P:(k + 1) * P], s.go_turned, (4, 5))
            pe.wait_ge(s.att_o, 2)
            turn_tiles(4, lambda a, k: oa[:, a, k * P:(k + 1) * P], s.oa_turned, (6, 7))
            turn_tiles(4, lambda a, k: go[:, a, 512 + k * P:640 + k * P], s.go_turned, (4, 5),
                       lambda b: pe.wait_ge(s.go_lo, b + 1))
            b0 = 2 * M_BR
            for e in range(2):
                if e == 0:
                    pe.wait_ge(s.oa_lo, 2)
                for t in range(2):
                    c = C_BR + 2 * e + t
                    pe.wait_ge(acc_free[c % 2], c // 2)
                    half_columns(b0 + 6 * e + t, 4, 2, bank[:, 2 * (c % 2), :], (a_hi, a_lo))
                if e == 0:
                    pe.wait_ge(s.go_lo, 4)
                for t in range(2):
                    c = C_BR + 2 * e + t
                    for f in range(2):
                        half_columns(b0 + 6 * e + 2 + 2 * t + f, KT, 1,
                                     bank[:, 2 * (c % 2) + 1, f * TOKENS:(f + 1) * TOKENS],
                                     (a_hi[:, 4:12, :], a_lo[:, 4:12, :]))
            for c in range(2):
                chunk_rows(2 * M_OUT2 + 4 * c, C_OUT2 + c, 512, h,
                           lambda k: pe.wait_ge(s.mix_lo, k // 2 + 1) if k % 2 == 0 else None,
                           (0, 1, 2, 3) if c == 0 else (0, 1))
            chunk_rows(2 * M_OUT2 + 4, C_OUT2 + 1, 512, h, None, LAST)

            turn_x(x, lambda a: pe.wait_ge(s.x_tiles, 4) if a == 0 else pe.wait_ge(s.acc_free0, 19))
            ready = h_ready(3)

            def ff2_up(n, b, j0, i=None, ready=None):
                if i is not None or j0 >= 3:
                    pe.wait_ge(s.up_relu, j0 - 2 if i is None else i * 3 + j0 - 2)
                for f in range(2):
                    half_columns(n + f, KT, 1, bank[:, b, f * TOKENS:(f + 1) * TOKENS], h, i, ready if f == 0 else None)

            n3 = 2 * M_FF2

            def ff2_step(i, first):
                for e in range(3):
                    ff2_up(n3 + 2 + 4 * e, (e + 1) % 3, e + 1, i)
                    ff_down(n3 + 4 + 4 * e, 2 * e, first and e == 0, False,
                            lambda: pe.wait_ge(s.up_lo, e + 1 if i is None else i * 3 + e + 1), i)

            ff2_up(n3, 0, 0, None, ready)
            ff2_step(None, True)
            with pe.Fori(1, CH2 // 3) as i:
                ff2_step(i, False)
            pe.wait_ge(s.up_lo, CH2)
            last_halves(2 * M_END - 2, 1024, (0, 1), 1, al, down_banks)

        @block.scalar
        def _(act):
            chain = [0]

            def link(ins):
                chain[0] += 1
                ins.then_inc(s.act_chain, 1)
                act.wait_ge(s.act_chain, chain[0])

            def split_hi(n, size, cols, i=None):
                m, half = n // 2, n % 2
                if half == 0:
                    landed = 16 * (m // RAW + 1)
                    act.wait_ge(raw_in[m % RAW], landed if i is None else i * 32 + landed)
                if i is not None or n >= RING:
                    act.wait_ge(s.mm_done, n - RING + 1 if i is None else i * 12 + n - RING + 1)
                dst = w_hi[:, n % RING, 0:size]
                if cols:
                    dst = dst.rearrange("p (k c) -> p k c", c=cols // 2)
                nc.scalar.copy(dst, raw_half(m % RAW, half, size, cols)).then_inc(s.hi_done, 1)

            def hi(*ns, i=None):
                for n in ns:
                    _, size, cols = table[n // 2] if n // 2 in table else (None, HALF, ffn_columns(n // 2))
                    split_hi(n, size, cols, i)

            def evacuate(dst, src, c, mm, func=ACT.Copy, rms=None):
                act.wait_ge(s.mm_done, mm)
                if rms is None:
                    ins = nc.scalar.activation(dst, src, func)
                else:
                    for a in range(TT):
                        ins = nc.scalar.activation(dst[:, a], src[:, a], func, scale=st[:, rms + a:rms + a + 1])
                ins.then_inc(acc_free[c % 2], 1)

            def mean_squares():
                for a in range(TT):
                    ins = nc.scalar.activation(xn[:, a, :], x[:, a, :], ACT.Square, scale=D ** -0.5,
                                               accum_out=st[:, a:a + 1])
                ins.then_inc(s.ssq, 1)

            def turned_hi(dst, at, count, turned, before, gain, done, banks=(4, 5, 6, 7)):
                for k in range(count):
                    if k % 2 == 0:
                        act.wait_ge(turned, before + k // 2 + 1)
                    ins = nc.scalar.activation(dst[:, at + k, :], bank[:, banks[k // 2], k % 2 * 256:k % 2 * 256 + 256],
                                               ACT.Copy, scale=gain(k))
                    if k % 2 == 1 or k == count - 1:
                        ins.then_inc(done, 1)

            nc.scalar.dma_start(vec[:], w.vectors).then_inc(s.vecs_in, 16)
            hi(0)
            act.wait_ge(s.vecs_in, 16)
            turned_hi(h_hi, 0, KT, s.x_turned, 0, lambda k: column("attn_norm_w", k), s.h_hi_done)
            hi(1, 2, 3)
            mean_squares()
            hi(4, 5, 6, 7)
            act.wait_ge(s.inverse_rms, 1)
            evacuate(proj[:, :, 2048:2464], pair(0, 416), 0, 4, rms=2)
            act.wait_ge(s.acc_free0, 1)
            for a in range(TT):
                nc.scalar.activation(xn[:, a, 0:QR], proj[:, a, 2048:2304], ACT.Square, scale=QR ** -0.5,
                                     accum_out=st[:, 4 + a:5 + a])
            for a in range(TT):
                ins = nc.scalar.activation(xn[:, a, QR:QR + KVR], proj[:, a, 2304:2432], ACT.Square,
                                           scale=KVR ** -0.5, accum_out=st[:, 6 + a:7 + a])
            ins.then_inc(s.ssq, 1)
            hi(8, 9, 10, 11)
            turned_hi(a_hi, 0, 3, s.latents_turned, 0,
                      lambda k: column("mla_q_norm_w", k) if k < 2 else column("mla_kv_norm_w"), s.latents_hi)
            evacuate(proj[:, :, 0:512], pair(1), 1, 8, rms=2)
            act.wait_ge(s.trig_arg, 1)
            nc.scalar.activation(angle, angle, ACT.Sin).then_inc(s.trig, 1)
            hi(12, 13, 14, 15)
            evacuate(proj[:, :, 512:1024], pair(2), 2, 12, rms=2)
            hi(16, 17)
            for a in range(TT):
                evacuate(q_tok[:, a].rearrange("p h c -> p (h c)"),
                         flat(pair(3 + a))[:, 0:MH * QK], 3 + a, 14)
            hi(18)
            for a in range(TT):
                evacuate(kv[:, a].rearrange("p h c -> p (h c)"), flat(bank[:, 4 + 2 * a:6 + 2 * a, :]), 5 + a, 16)
            hi(19, 20, 21)
            for b in range(2):
                act.wait_ge(s.ret_q_turned, b + 1)
                nc.scalar.copy(flat(rqT[:, 2 * b:2 * b + 2, :]), bank[:, 4 + b, :]).then_inc(s.ret_qT, 1)
            hi(22, 23)
            evacuate(proj[:, :, 1024:1536], pair(7), 7, 20, rms=2)
            for r in range(4):
                act.wait_ge(s.mla_q_turned, r + 1)
                nc.scalar.activation(flat(mqT[0:QK, 2 * r:2 * r + 2, :]), bank[0:QK, 4 + r, :], ACT.Copy,
                                     scale=QK ** -0.5).then_inc(s.mla_qT, 1)
            hi(24, 25, 26, 27)
            evacuate(proj[:, :, 1536:2048], pair(8), 8, 24, ACT.Silu, rms=2)
            act.wait_ge(s.ret_o_head, RH)
            nc.scalar.copy(proj[:, :, 0:512], bank[:, 6:8, :]).then_inc(s.ret_copied, 1)
            for hd in range(MH + 1):
                if hd == 2:
                    act.wait_ge(s.ret_centred, 1)
                    nc.scalar.activation(xn[:, :, 0:512], proj[:, :, 0:512], ACT.Square,
                                         scale=RD ** -0.5).then_inc(s.ret_sq, 1)
                if hd == 5:
                    turned_hi(a_hi, 0, 4, s.mixed_turned, 0, lambda k: column("ret_gn_w", k), s.mixed_hi, (2, 3))
                if hd < MH:
                    act.wait_ge(s.mla_max, hd + 1)
                    for a in range(TT):
                        row = sT[:, hd % 2, 0:P] if a == 0 else sT[:, hd % 2, P:3 * P]
                        at = 2 * hd + a
                        ins = nc.scalar.activation(row, row, ACT.Exp, bias=st[:, 16 + at:17 + at],
                                                   accum_out=st[:, 32 + at:33 + at])
                    ins.then_inc(s.mla_exp, 1)
                if hd >= 1:
                    act.wait_ge(s.mla_turned, hd)
                    if hd >= 3:
                        act.wait_ge(s.mla_pv, hd - 2)
                    nc.scalar.copy(pT[:, (hd - 1) % 2, :], bank[:, 6, 0:3 * P]).then_inc(s.mla_pt, 1)
                if hd >= 6:
                    hi(22 + hd)
            turned_hi(a_hi, 4, 4, s.mixed_turned, 2, lambda k: column("ones", k), s.mixed_hi)
            hi(31)
            hi(32, 33)
            act.wait_ge(s.acc_free1, 5)
            for half in range(2):
                for a in range(TT):
                    if half == 1:
                        act.wait_ge((s.x_tiles, s.acc_free0)[a], (1, 6)[a])
                    cols = slice(half * 512, half * 512 + 512)
                    at = a + 10 * half
                    ins = nc.scalar.activation(xn[:, a, cols], x[:, a, cols], ACT.Square, scale=D ** -0.5,
                                               accum_out=st[:, at:at + 1])
            ins.then_inc(s.ssq, 1)
            hi(34, 35)
            turned_hi(h_hi, 0, KT, s.x_turned, 4, lambda k: column("ffn_norm_w", k), s.h_hi_done)

            def taps(j, e, v):
                for f in range(2):
                    t = 22 * v + f
                    bias, scale = VEC["conv_b"][0] + t, CW2 + t
                    ins = nc.scalar.activation(
                        conv[:, v, e, f * 256:f * 256 + 256], bank[:, 2 * e + v, f * 256:f * 256 + 256], ACT.Identity,
                        bias=vec[:, bass.ds(j * 2 + bias, 1)] if not isinstance(j, int) else
                        vec[:, 2 * j + bias:2 * j + bias + 1],
                        scale=vec[:, bass.ds(j * 2 + scale, 1)] if not isinstance(j, int) else
                        vec[:, 2 * j + scale:2 * j + scale + 1])
                ins.then_inc(s.taps, 1)

            def ff1_chunk(j, e, mm, split1, split2, split3):
                act.wait_ge(s.mm_done, mm)
                taps(j, e, 0)
                split1()
                act.wait_ge(s.mm_done, mm + 2)
                taps(j, e, 1)
                split2()
                act.wait_ge(s.gate_conv, j + 1)
                nc.scalar.activation(silu1[:, e, :], conv[:, 0, e, :], ACT.Silu).then_inc(s.gate_silu, 1)
                act.wait_ge(s.act_ready, j + 1)
                nc.scalar.copy(flat(a_hi[:, 2 * e:2 * e + 2, :]), act1[:, e, :]).then_inc(s.act_hi_done, 1)
                split3()

            n1 = 2 * M_FF1
            ff1_chunk(0, 0, n1 + 2, lambda: hi(n1 + 4, n1 + 5), lambda: hi(n1 + 6, n1 + 7), lambda: None)
            with act.Fori(0, CH1 // 2 - 1) as i:
                for e in range(2):
                    b = n1 + 6 * e
                    ff1_chunk(i * 2 + 1 + e, 1 - e, i * 12 + b + 6, lambda: hi(b + 8, b + 9, i=i),
                              lambda: hi(b + 10, b + 11, i=i), lambda: hi(b + 12, b + 13, i=i))
            b = n1 + 12 * (CH1 // 2 - 1)
            ff1_chunk(CH1 - 2, 1, b + 6, lambda: hi(b + 8, b + 9), lambda: hi(b + 10, b + 11), lambda: hi(b + 12, b + 13))
            ff1_chunk(CH1 - 1, 0, b + 12, lambda: hi(b + 14, b + 15), lambda: hi(b + 16, b + 17),
                      lambda: hi(b + 18, b + 19))
            n2 = 2 * M_IN2
            hi(n2 + 2, n2 + 3)

            turned_hi(h_hi, 0, KT, s.x_turned, 8, lambda k: column("norm1_g_2", k), s.h_hi_done, IN2_BANKS)
            mean_squares()
            hi(n2 + 4, n2 + 5)
            act.wait_ge(s.x_added, 1)
            mean_squares()
            hi(n2 + 6, n2 + 7)
            act.wait_ge(s.inverse_rms, 2)
            evacuate(gqk[:, 0], pair(C_GLA), C_GLA, n2 + 4, rms=8)
            hi(n2 + 8, n2 + 9, n2 + 10, n2 + 11)
            evacuate(gqk[:, 1], pair(C_GLA + 1), C_GLA + 1, n2 + 8, rms=8)
            hi(n2 + 12, n2 + 13)
            evacuate(ga, pair(C_GLA + 2, 16), C_GLA + 2, n2 + 10, rms=8)
            hi(n2 + 14, n2 + 15, n2 + 16, n2 + 17)
            evacuate(gv[:, :, 0:512], pair(C_GLA + 3), C_GLA + 3, n2 + 14, rms=8)
            act.wait_ge(s.gla_turned, 2)
            nc.scalar.activation(gqT.rearrange("p (b h) t -> p b (h t)", b=2), bank[:, 4:6, :], ACT.Copy,
                                 scale=GK ** -0.5).then_inc(s.gla_qT, 1)
            hi(n2 + 18, n2 + 19, n2 + 20, n2 + 21)
            evacuate(gv[:, :, 512:1024], pair(C_GLA + 4), C_GLA + 4, n2 + 18, rms=8)
            act.wait_ge(s.gla_logits, 1)
            for hd in range(GH):
                ins = nc.scalar.activation(z[:, hd * TOKENS:(hd + 1) * TOKENS],
                                           bank[:, 6 + hd // 2, hd % 2 * TOKENS:(hd % 2 + 1) * TOKENS], ACT.Identity,
                                           bias=column("gla_gate_bias_2", hd))
            ins.then_inc(s.gla_z, 1)
            act.wait_ge(s.gla_z, 1)
            link(nc.scalar.activation(soft, z, ACT.Abs))
            link(nc.scalar.activation(soft, soft, ACT.Exp, scale=-1.0))
            nc.scalar.activation(soft, soft, ACT.Ln, bias=1.0).then_inc(s.gla_soft, 1)

            def level_decay(t):
                act.wait_ge(s.gla_diff, t + 1)
                link(nc.scalar.activation(z, z, ACT.Abs))
                nc.scalar.activation(z, z, ACT.Exp, scale=-1.0 / 16).then_inc(s.gla_e, 1)

            def heads_out(t):
                nth = t // 3 * 2 + t % 3
                act.wait_ge(s.att_turned, 2 * nth + 2)
                dst = (aqT, akT)[t % 3][:, t // 3 * 4:t // 3 * 4 + 4, :]
                nc.scalar.activation(dst.rearrange("p (b k) t -> p b (k t)", b=2), bank[:, 6:8, :], ACT.Copy,
                                     scale=column(("attn_q_norm_g_2", "attn_k_norm_g_2")[t % 3])).then_inc(s.att_T, 1)

            for t in range(3 * AG + 2):
                n = n2 + 18 + 4 * t
                hi(n + 4, n + 5, n + 6, n + 7)
                g, part = t // 3, t % 3
                if t >= 3 * AG:
                    at = 512 * (t - 3 * AG)
                    evacuate(silu_r[:, :, at:at + 512], pair(C_ATT + t), C_ATT + t, n + 4, ACT.Silu, rms=8)
                else:
                    dst = av[:, :, g * 512:g * 512 + 512] if part == 2 else a_tok[:, part]
                    evacuate(dst, pair(C_ATT + t), C_ATT + t, n + 4, rms=8)
                    if part < 2:
                        nth = 2 * g + part
                        c = C_ATT + t
                        act.wait_ge(acc_free[c % 2], c // 2 + 1)
                        if nth >= 1:
                            act.wait_ge(s.att_ms, nth)
                        nc.scalar.activation(asq, a_tok[:, part], ACT.Square, scale=AD ** -0.5).then_inc(
                            s.att_squared, 1)
                if 1 <= t <= 3 * AG and (t - 1) % 3 < 2:
                    heads_out(t - 1)
                if t <= LEVELS:
                    level_decay(t)
            for a in range(TT):
                act.wait_ge(s.gla_o, a + 1)
                nc.scalar.copy(go[:, a, :], flat(bank[:, 4 + 2 * a:6 + 2 * a, :])).then_inc(s.gla_go, 1)
            hi(2 * M_GATE + 4)

            def square_heads(a):
                if a == 0:
                    act.wait_ge(s.gla_go, 2)
                for hd in range(GH):
                    at = 16 + GH * a + hd
                    ins = nc.scalar.activation(go_squares[:, a, hd * GV:(hd + 1) * GV], go[:, a, hd * GV:(hd + 1) * GV],
                                               ACT.Square, scale=GV ** -0.5, accum_out=st[:, at:at + 1])
                if a == 1:
                    ins.then_inc(s.gla_ssq, 1)

            def gate(c):
                act.wait_ge(acc_free[c % 2], c // 2 + 1)
                for k in range(4 * (c - C_GATE), 4 * (c - C_GATE) + 4):
                    g = gates[k // KT][:, k % KT, :]
                    ins = nc.scalar.activation(g, g, ACT.Sigmoid, bias=column("branch_gate_bias_2", k))
                ins.then_inc(s.gate_done, 1)

            def weights_back(u, part):
                done = (u if u < AH else AH + 2 * (u - AH)) + part
                act.wait_ge(s.att_turnedp, done + 1)
                if u >= 2:
                    act.wait_ge(s.att_pv, u - 1)
                nc.scalar.copy(ppT[:, u % 2, 3 * P * part:3 * P * (part + 1)], bank[:, 6, 0:3 * P]).then_inc(s.att_pt, 1)

            for u in range(2 * AH):
                keys = AG * (u // AH + 1) * P
                act.wait_ge(s.att_max, u + 1)
                nc.scalar.activation(p[:, u % 2, 0:keys], p[:, u % 2, 0:keys], ACT.Exp, bias=st[:, 32 + u:33 + u],
                                     accum_out=st[:, 80 + u:81 + u]).then_inc(s.att_exp, 1)
                weights_back(u, 0)
                if u > 0:
                    hi(2 * M_GATE + 4 + u)
                if u < TT:
                    square_heads(u)
                if u >= AH:
                    weights_back(u, 1)
            turned_hi(a_hi, 4, 4, s.go_turned, 0, lambda k: column("gla_out_norm_g_2", k % 2), s.go_hi)
            turned_hi(a_hi, 0, 4, s.oa_turned, 0, lambda k: 1.0, s.oa_hi, (6, 7))
            turned_hi(a_hi, 8, 4, s.go_turned, 2, lambda k: column("gla_out_norm_g_2", k % 2), s.go_hi)
            n = 2 * M_BR

            def mixed_hi(q):
                act.wait_ge(s.mix_ready, q + 1)
                nc.scalar.copy(flat(h_hi[:, 2 * q:2 * q + 2, :]), mix[:, 0, q % 2, :]).then_inc(s.mix_hi, 1)

            for c in range(C_GATE, C_GATE + 4):
                gate(c)
            hi(n + 4, n + 5, n + 6, n + 7)
            mixed_hi(0)
            hi(n + 8, n + 9)
            mixed_hi(1)
            hi(n + 10, n + 11, n + 12, n + 13)
            mixed_hi(2)
            hi(n + 14, n + 15)
            mixed_hi(3)
            hi(*range(n + 16, n + 24))
            turned_hi(h_hi, 0, KT, s.x_turned, 12, lambda k: column("norm2_g_2", k), s.h_hi_done)
            mean_squares()

            def ff2_chunk(j, e, mm, split1, split2):
                act.wait_ge(s.mm_done, mm)
                nc.scalar.activation(relu2[:, e, :], bank[:, e, :], ACT.Relu).then_inc(s.up_relu, 1)
                split1()
                act.wait_ge(s.up_square, j + 1)
                nc.scalar.copy(flat(a_hi[:, 2 * e:2 * e + 2, :]), square2[:, e, :]).then_inc(s.up_hi, 1)
                split2()

            n3 = 2 * M_FF2
            ff2_chunk(0, 0, n3 + 2, lambda: hi(n3 + 4, n3 + 5), lambda: None)
            with act.Fori(0, CH2 // 3 - 1) as i:
                for e in range(3):
                    b = n3 + 4 * e
                    ff2_chunk(i * 3 + e + 1, (e + 1) % 3, i * 12 + b + 4, lambda: hi(b + 6, b + 7, i=i),
                              lambda: hi(b + 8, b + 9, i=i))
            for e in range(3):
                b = n3 + 12 * (CH2 // 3 - 1) + 4 * e
                ff2_chunk(CH2 - 3 + e, (e + 1) % 3, b + 4, lambda: hi(b + 6, b + 7),
                          (lambda: hi(b + 8, b + 9)) if e < 2 else (lambda: None))

        @block.vector
        def _(dve):
            chain = [0]

            def link(ins):
                chain[0] += 1
                ins.then_inc(s.dve_chain, 1)
                dve.wait_ge(s.dve_chain, chain[0])

            def lo(*ns, i=None):
                for n in ns:
                    _, size, cols = table[n // 2] if n // 2 in table else (None, HALF, ffn_columns(n // 2))
                    dve.wait_ge(s.hi_done, n + 1 if i is None else i * 12 + n + 1)
                    dst, h = w_lo[:, n % RING, 0:size], w_hi[:, n % RING, 0:size].bitcast(F32)
                    if cols:
                        dst = dst.rearrange("p (k c) -> p k c", c=cols // 2)
                        h = h.rearrange("p (k c) -> p k c", c=cols // 2)
                    nc.vector.tensor_tensor(dst, raw_half(n // 2 % RAW, n % 2, size, cols), h, ALU.subtract).then_inc(
                        s.lo_done, 1)

            def root_guess(v, src, y, t):
                link(nc.vector.tensor_scalar(v, src, EPS, None, ALU.add))
                link(nc.vector.tensor_scalar(t.bitcast(I32), v.bitcast(I32), 1, None, ALU.arith_shift_right))
                return nc.vector.tensor_scalar(y.bitcast(I32), t.bitcast(I32), -1, ROOT_GUESS, ALU.mult, ALU.add)

            def inverse_root(v, src=None, done=None, count=None):
                n = v.shape[1]
                y, t = newton[:, 0, 0:n], newton[:, 1, 0:n]
                link(root_guess(v, v if src is None else src, y, t))
                for step in range(3):
                    link(nc.vector.scalar_tensor_tensor(t, y, -0.5, v, ALU.mult, ALU.mult))
                    link(nc.vector.tensor_tensor(t, t, y, ALU.mult))
                    ins = nc.vector.scalar_tensor_tensor(y if step < 2 else v, t, 1.5, y, ALU.add, ALU.mult)
                    if step < 2 or done is None:
                        link(ins)
                if done is not None:
                    ins.then_inc(done, 1)
                    dve.wait_ge(done, count)

            def scale_x(a):
                nc.vector.tensor_scalar(xn[:, a, :], x[:, a, :], st[:, 2 + a:3 + a], None, ALU.mult).then_inc(
                    s.x_scaled, 1)

            def turned_lo(dst, dst_hi, at, count, hi_done, before, gain, done, banks=(4, 5, 6, 7)):
                for k in range(count):
                    if k % 2 == 0:
                        dve.wait_ge(hi_done, before + k // 2 + 1)
                    ins = nc.vector.scalar_tensor_tensor(
                        dst[:, at + k, :], bank[:, banks[k // 2], k % 2 * 256:k % 2 * 256 + 256], gain(k),
                        dst_hi[:, at + k, :].bitcast(F32), ALU.mult, ALU.subtract)
                    if k % 2 == 1 or k == count - 1:
                        ins.then_inc(done, 1)

            def rotate(t, heads, width, lane):
                half = width // 2
                for a in range(TT):
                    x1, x2 = t[:, a, :, 0:half], t[:, a, :, half:width]
                    cos, sin = [angle[:, f, a, lane:lane + half].rearrange("p (o f) -> p o f", o=1).to_broadcast(
                        [P, heads, half]) for f in range(2)]
                    t1, t2 = [rope_tmp[:, f, 0:heads * half].rearrange("p (h f) -> p h f", f=half) for f in range(2)]
                    nc.vector.tensor_tensor(t1, x1, sin, ALU.mult)
                    nc.vector.tensor_tensor(t2, x2, sin, ALU.mult)
                    nc.vector.tensor_tensor(x1, x1, cos, ALU.mult)
                    link(nc.vector.tensor_tensor(x2, x2, cos, ALU.mult))
                    nc.vector.tensor_tensor(x1, x1, t2, ALU.subtract)
                    ins = nc.vector.tensor_tensor(x2, x2, t1, ALU.add)
                    if a == 0:
                        link(ins)
                return ins

            lo(0)
            dve.wait_ge(s.vecs_in, 16)
            fn, n1g = VEC["final_norm_w"][0], VEC["norm1_g_2"][0]
            nc.vector.tensor_tensor(vec[:, n1g:n1g + KT], vec[:, n1g:n1g + KT], vec[:, fn:fn + KT], ALU.mult)
            nc.vector.tensor_scalar(column("attn_q_norm_g_2"), column("attn_q_norm_g_2"), AD ** -0.5, None, ALU.mult)
            turned_lo(h_lo, h_hi, 0, KT, s.h_hi_done, 0, lambda k: column("attn_norm_w", k), s.h_lo_done)
            lo(1, 2, 3)
            dve.wait_ge(s.ssq, 1)
            inverse_root(st[:, 2:4], st[:, 0:2], s.inverse_rms, 1)
            lo(4, 5, 6, 7)
            dve.wait_ge(s.ssq, 2)
            inverse_root(st[:, 4:8])
            for a in range(TT):
                nc.vector.tensor_scalar(proj[:, a, 2048:2304], proj[:, a, 2048:2304], st[:, 4 + a:5 + a], None, ALU.mult)
                ins = nc.vector.tensor_scalar(proj[:, a, 2304:2432], proj[:, a, 2304:2432], st[:, 6 + a:7 + a], None,
                                              ALU.mult)
            ins.then_inc(s.latent_scaled, 1)
            lo(8, 9)
            dve.wait_ge(s.pos_in, 32)
            link(nc.vector.tensor_copy(pos_f, pos_i.bitcast(I32)))
            for a in range(TT):
                for t in range(2):
                    ins = nc.vector.tensor_scalar(angle[:, t, a, :], invf, pos_f[:, a:a + 1], None, ALU.mult)
            link(ins)
            for t, turn_ in enumerate((0.25, 0.0)):
                ins = nc.vector.tensor_scalar(turns[:, t], angle[:, t], 0.15915494309189535, turn_, ALU.mult, ALU.add)
            link(ins)
            angle_f, turns_f = area(25280, 4 * 48), area(25472, 4 * 48)
            link(nc.vector.tensor_scalar(turns_f, turns_f, MAGIC, None, ALU.add))
            link(nc.vector.tensor_scalar(turns_f, turns_f, MAGIC, None, ALU.subtract))
            for part in TWO_PI:
                link(nc.vector.scalar_tensor_tensor(angle_f, turns_f, -part, angle_f, ALU.mult, ALU.add))
            link(nc.vector.tensor_scalar(angle[:, 0], angle[:, 0], 1.5707963267948966, None, ALU.add))
            nc.vector.tensor_scalar(angle_f, angle_f, 3.1415925, -3.1415925, ALU.min, ALU.max).then_inc(s.trig_arg, 1)
            lo(10, 11)
            turned_lo(a_lo, a_hi, 0, 3, s.latents_hi, 0,
                      lambda k: column("mla_q_norm_w", k) if k < 2 else column("mla_kv_norm_w"), s.latents_lo)
            lo(12, 13)
            dve.wait_ge(s.trig, 1)
            link(rotate(proj[:, :, 2432:2464].rearrange("p a (h c) -> p a h c", h=1), 1, PE_D, 32))
            for a in range(TT):
                nc.vector.tensor_copy(k_tok[:, a, :, NOPE:QK], proj[:, a, 2432:2464].rearrange(
                    "p (o c) -> p o c", o=1).to_broadcast([P, MH, PE_D]))
            lo(14, 15)
            dve.wait_ge(s.acc_free1, 1)
            link(rotate(proj[:, :, 0:512].rearrange("p a (h c) -> p a h c", c=RD), RH, RD, 0))
            lo(16, 17)
            dve.wait_ge(s.acc_free0, 2)
            rotate(proj[:, :, 512:1024].rearrange("p a (h c) -> p a h c", c=RD), RH, RD, 0).then_inc(s.ret_roped, 1)
            dve.wait_ge(s.acc_free1, 2)
            dve.wait_ge(s.acc_free0, 3)
            dve.wait_ge(s.ret_roped, 1)
            rotate(q_tok[:, :, :, NOPE:QK], MH, PE_D, 32).then_inc(s.mla_q_ready, 1)
            lo(18, 19)
            dve.wait_ge(s.acc_free1, 3)
            dve.wait_ge(s.acc_free0, 4)
            for a in range(TT):
                ins = nc.vector.tensor_copy(k_tok[:, a, :, 0:NOPE], kv[:, a, :, 0:NOPE])
            ins.then_inc(s.mla_k_ready, 1)
            lo(20, 21)
            for b in range(2):
                dve.wait_ge(s.ret_k_turned, b + 1)
                nc.vector.tensor_copy(flat(rkT[:, 2 * b:2 * b + 2, :]), bank[:, 6 + b, :]).then_inc(s.ret_kT, 1)
            lo(22, 23, 24)
            for r in range(4):
                dve.wait_ge(s.mla_k_turned, r + 1)
                nc.vector.tensor_copy(flat(mkT[0:QK, 2 * r:2 * r + 2, :]), bank[0:QK, 4 + r, :]).then_inc(s.mla_kT, 1)

            dve.wait_ge(s.consts_in, 32)
            for hd in range(RH):
                dve.wait_ge(s.ret_scores, hd + 1)
                if hd >= 2:
                    dve.wait_ge(s.ret_o_head, hd - 1)
                nc.vector.tensor_tensor(sT[:, hd % 2, :], bank[:, 4 + hd % 2, 0:3 * P], decay[:, hd, :],
                                        ALU.mult).then_inc(s.ret_masked, 1)
                if hd in (0, 2, 4):
                    lo(25 + hd // 2)

            oh = proj[:, :, 0:512].rearrange("p a (h c) -> p a h c", c=RD)
            mean = st[:, 48:64].rearrange("p (a h o) -> p a h o", a=2, o=1)
            var = st[:, 64:80].rearrange("p (a h o) -> p a h o", a=2, o=1)

            def ret_mean():
                dve.wait_ge(s.ret_copied, 1)
                link(nc.vector.tensor_reduce(st[:, 48:64].rearrange("p (a h) -> p a h", a=2), oh, AX.X, ALU.add))
                link(nc.vector.tensor_scalar(st[:, 48:64], st[:, 48:64], -1.0 / RD, None, ALU.mult))
                for a in range(TT):
                    ins = nc.vector.tensor_tensor(oh[:, a], oh[:, a], mean[:, a].to_broadcast([P, RH, RD]), ALU.add)
                ins.then_inc(s.ret_centred, 1)

            def ret_variance():
                dve.wait_ge(s.ret_sq, 1)
                link(nc.vector.tensor_reduce(st[:, 64:80].rearrange("p (a h) -> p a h", a=2),
                                             xn[:, :, 0:512].rearrange("p a (h c) -> p a h c", c=RD), AX.X, ALU.add))
                v = st[:, 64:80]
                root_guess(v, v, heads_newton[:, 0], heads_newton[:, 1]).then_inc(s.root_guessed, 1)
                dve.wait_ge(s.acc_free0, 5)
                link(nc.vector.tensor_tensor(proj[:, :, 0:512], proj[:, :, 0:512], proj[:, :, 1536:2048], ALU.mult))

            def ret_scaled():
                dve.wait_ge(s.root_found, 1)
                for a in range(TT):
                    ins = nc.vector.tensor_tensor(oh[:, a], oh[:, a], var[:, a].to_broadcast([P, RH, RD]), ALU.mult)
                ins.then_inc(s.ret_y, 1)

            def mla_out(r):
                dve.wait_ge(s.mla_pv, 4 * r + 4)
                at = 32 + 8 * r
                link(nc.vector.reciprocal(st[:, at:at + 8], st[:, at:at + 8]))
                o = bank[:, 7, :].rearrange("p (h a c) -> p a h c", h=4, a=2)
                inv = st[:, at:at + 8].rearrange("p (h a o) -> p a h o", a=2, o=1)
                for a in range(TT):
                    ins = nc.vector.tensor_tensor(
                        proj[:, a, 512 + 256 * r:768 + 256 * r].rearrange("p (h c) -> p h c", c=MV),
                        o[:, a], inv[:, a].to_broadcast([P, 4, MV]), ALU.mult)
                ins.then_inc(s.mla_o, 1)

            for hd in range(MH):
                dve.wait_ge(s.mla_scores, hd + 1)
                if hd >= 2:
                    dve.wait_ge(s.mla_turned, hd - 1)
                else:
                    dve.wait_ge(s.ret_o_head, RH - 1 + hd)
                nc.vector.tensor_tensor(sT[:, hd % 2, :], bank[:, 4 + hd % 2, 0:3 * P], causal, ALU.add).then_inc(
                    s.mla_masked, 1)
                dve.wait_ge(s.mla_masked, hd + 1)
                at = 16 + 2 * hd
                nc.vector.tensor_reduce(st[:, at:at + 1], sT[:, hd % 2, 0:P], AX.X, ALU.max, negate=True)
                nc.vector.tensor_reduce(st[:, at + 1:at + 2], sT[:, hd % 2, P:3 * P], AX.X, ALU.max,
                                        negate=True).then_inc(s.mla_max, 1)
                if hd == 1:
                    ret_mean()
                if hd == 2:
                    ret_variance()
                if hd == 3:
                    ret_scaled()
                if hd == 4:
                    turned_lo(a_lo, a_hi, 0, 4, s.mixed_hi, 0, lambda k: column("ret_gn_w", k), s.mixed_lo, (2, 3))
                if hd == 5:
                    mla_out(0)
            lo(28, 29)
            mla_out(1)
            lo(30)
            turned_lo(a_lo, a_hi, 4, 4, s.mixed_hi, 2, lambda k: column("ones", k), s.mixed_lo)
            lo(31)

            def add_chunk(c, first, mm):
                dve.wait_ge(s.mm_done, mm)
                xc = x[:, :, 512 * (c - first):512 * (c - first) + 512]
                nc.vector.tensor_tensor(xc, pair(c), xc, ALU.add).then_inc(acc_free[c % 2], 1)

            lo(32, 33)
            add_chunk(C_OUT, C_OUT, 30)

            def add_tile(c, first, a, count, done):
                dve.wait_ge((s.tile_done, s.mm_done)[a], count)
                xc = x[:, a, 512 * (c - first):512 * (c - first) + 512]
                nc.vector.tensor_tensor(xc, pair(c)[:, a], xc, ALU.add).then_inc(done, 1)

            add_tile(C_OUT + 1, C_OUT, 0, 1, s.x_tiles)
            add_tile(C_OUT + 1, C_OUT, 1, 32, s.acc_free0)
            dve.wait_ge(s.ssq, 3)
            link(nc.vector.tensor_tensor(st[:, 2:4], st[:, 0:2], st[:, 10:12], ALU.add))
            inverse_root(st[:, 2:4])
            scale_x(0)
            scale_x(1)
            turned_lo(h_lo, h_hi, 0, KT, s.h_hi_done, 4, lambda k: column("ffn_norm_w", k), s.h_lo_done)
            lo(34, 35)

            def tap(j, row):
                return vec[:, 2 * j + row:2 * j + row + 1] if isinstance(j, int) else vec[:, bass.ds(j * 2 + row, 1)]

            def convolve(j, e, v):
                dve.wait_ge(s.taps, j * 2 + v + 1)
                for f in range(2):
                    u, y = bank[:, 2 * e + v, f * 256:f * 256 + 256], conv[:, v, e, f * 256:f * 256 + 256]
                    ins = nc.vector.scalar_tensor_tensor(y[:, 1:256], u[:, 0:255], tap(j, CW1 + 22 * v + f), y[:, 1:256],
                                                         ALU.mult, ALU.add)
                ins.then_inc(s.tap1, 1)
                dve.wait_ge(s.tap1, j * 2 + v + 1)
                for f in range(2):
                    u, y = bank[:, 2 * e + v, f * 256:f * 256 + 256], conv[:, v, e, f * 256:f * 256 + 256]
                    ins = nc.vector.scalar_tensor_tensor(y[:, 2:256], u[:, 0:254], tap(j, CW0 + 22 * v + f), y[:, 2:256],
                                                         ALU.mult, ALU.add)
                ins.then_inc((s.gate_conv, s.val_conv)[v], 1)

            def ff1_chunk(j, e, split1, split2, split3):
                convolve(j, e, 0)
                split1()
                convolve(j, e, 1)
                split2()
                dve.wait_ge(s.gate_silu, j + 1)
                dve.wait_ge(s.val_conv, j + 1)
                nc.vector.tensor_tensor(act1[:, e, :], silu1[:, e, :], conv[:, 1, e, :], ALU.mult).then_inc(s.act_ready, 1)
                dve.wait_ge(s.act_hi_done, j + 1)
                nc.vector.tensor_tensor(flat(a_lo[:, 2 * e:2 * e + 2, :]), act1[:, e, :],
                                        flat(a_hi[:, 2 * e:2 * e + 2, :]).bitcast(F32), ALU.subtract).then_inc(
                                            s.act_lo_done, 1)
                split3()

            n1 = 2 * M_FF1
            ff1_chunk(0, 0, lambda: lo(n1 + 4, n1 + 5), lambda: lo(n1 + 6, n1 + 7), lambda: None)
            with dve.Fori(0, CH1 // 2 - 1) as i:
                for e in range(2):
                    b = n1 + 6 * e
                    ff1_chunk(i * 2 + 1 + e, 1 - e, lambda: lo(b + 8, b + 9, i=i), lambda: lo(b + 10, b + 11, i=i),
                              lambda: lo(b + 12, b + 13, i=i))
            b = n1 + 12 * (CH1 // 2 - 1)
            ff1_chunk(CH1 - 2, 1, lambda: lo(b + 8, b + 9), lambda: lo(b + 10, b + 11), lambda: lo(b + 12, b + 13))
            ff1_chunk(CH1 - 1, 0, lambda: lo(b + 14, b + 15), lambda: lo(b + 16, b + 17), lambda: lo(b + 18, b + 19))
            n2 = 2 * M_IN2

            def add_down(nth, mm, done, inverse_ms=None):
                for a in range(TT):
                    dve.wait_ge((s.tile_done, s.mm_done)[a], (nth, mm)[a])
                    y = flat(bank[:, 4 + 2 * a:6 + 2 * a, :])
                    if inverse_ms is None:
                        ins = nc.vector.tensor_tensor(x[:, a, :], y, x[:, a, :], ALU.add)
                    else:
                        ins = nc.vector.scalar_tensor_tensor(x[:, a, :], y, inverse_ms[a], x[:, a, :], ALU.mult, ALU.add)
                    ins.then_inc(done, 1)

            add_down(2, 2 * M_IN2, s.x_tiles)
            turned_lo(h_lo, h_hi, 0, KT, s.h_hi_done, 8, lambda k: column("norm1_g_2", k), s.h_lo_done, IN2_BANKS)
            lo(n2 + 2, n2 + 3)
            dve.wait_ge(s.ssq, 4)
            inverse_root(st[:, 2:4], st[:, 0:2])
            dve.wait_ge(s.fw_in, 16)
            dve.wait_ge(s.x_turned, 12)
            for a in range(TT):
                ins = nc.vector.scalar_tensor_tensor(x[:, a, :], x[:, a, :], st[:, 2 + a:3 + a], fw, ALU.mult, ALU.mult)
            ins.then_inc(s.x_added, 1)
            lo(n2 + 4, n2 + 5)
            dve.wait_ge(s.ssq, 5)
            inverse_root(st[:, 8:10], st[:, 0:2])
            nc.vector.tensor_tensor(st[:, 8:10], st[:, 8:10], st[:, 2:4], ALU.mult).then_inc(s.inverse_rms, 1)
            lo(*range(n2 + 6, n2 + 18))
            dve.wait_ge(s.gla_turned, 4)
            nc.vector.tensor_copy(gkT.rearrange("p (b h) t -> p b (h t)", b=2), bank[:, 6:8, :]).then_inc(s.gla_kT, 1)
            lo(n2 + 18, n2 + 19)
            dve.wait_ge(s.pa_turned, 1)
            nc.vector.tensor_copy(paT[0:16, :], bank[0:16, 4, 0:TOKENS]).then_inc(s.pa_T, 1)
            lo(n2 + 20, n2 + 21)
            link(nc.vector.memset(resets, 1.0))
            nc.vector.memset(resets.rearrange("p (n t) -> p n t", t=P)[:, :, 0:1], 0.0)
            dve.wait_ge(s.gla_soft, 1)
            link(nc.vector.scalar_tensor_tensor(z, z, 0.0, soft, ALU.min, ALU.subtract))
            link(nc.vector.tensor_tensor_scan(run, resets, z, 0.0, ALU.mult, ALU.add))
            nc.vector.memset(g_in, 0.0)
            nc.vector.tensor_copy(r_row, bank[:, 4, TOKENS:2 * TOKENS])

            def level_distance(t):
                if t == 0:
                    r, d = [v.rearrange("p (h a t) -> p h a t", a=2, t=P) for v in (run, z)]
                    nc.vector.tensor_tensor(d[:, :, 0, :], r[:, :, 0, :], r[:, :, 0, P - 1:P].to_broadcast([P, GH, P]),
                                            ALU.subtract)
                    nc.vector.tensor_copy(d[:, :, 1, :], r[:, :, 1, :]).then_inc(s.gla_diff, 1)
                    return
                b = 2 << (LEVELS - t)
                r, d = [v.rearrange("p (n t) -> p n t", t=b) for v in (run, z)]
                nc.vector.tensor_tensor(d, r, r[:, :, b // 2 - 1:b // 2].to_broadcast([P, GH * TOKENS // b, b]),
                                        ALU.subtract).then_inc(s.gla_diff, 1)

            def over_rms(t):
                dve.wait_ge(s.root_found, 2 * (t // 3) + t % 3 + 2)
                r = st[:, 48:64].rearrange("p (a h o) -> p a h o", a=2, o=1)
                for a in range(TT):
                    v = a_tok[:, t % 3, a, :].rearrange("p (h c) -> p h c", c=AD)
                    ins = nc.vector.tensor_tensor(v, v, r[:, a].to_broadcast([P, AH, AD]), ALU.mult)
                ins.then_inc(s.att_scaled, 1)

            dve.wait_ge(s.levels_in, 16)
            for t in range(3 * AG + 2):
                n = n2 + 18 + 4 * t
                lo(n + 4, n + 5)
                if 1 <= t <= LEVELS + 1:
                    dve.wait_ge(s.gla_e, t)
                    nc.vector.tensor_tensor(flat(qe), flat(gqT), z, ALU.mult)
                    nc.vector.tensor_tensor(flat(ke), flat(gkT), z, ALU.mult).then_inc(s.gla_qe, 1)
                if 1 <= t <= 3 * AG and (t - 1) % 3 < 2:
                    over_rms(t - 1)
                if t <= LEVELS:
                    if t >= 1:
                        dve.wait_ge(s.gla_qe, t)
                    level_distance(t)
                lo(n + 6, n + 7)
                heads = t < 3 * AG and t % 3 < 2
                if heads:
                    nth = 2 * (t // 3) + t % 3
                    if nth >= 1:
                        dve.wait_ge(s.att_scaled, nth)
                    dve.wait_ge(s.att_squared, nth + 1)
                    v = st[:, 48:64].rearrange("p (a h) -> p a h", a=2)
                    nc.vector.tensor_reduce(v, asq.rearrange("p a (h c) -> p a h c", c=AD), AX.X,
                                            ALU.add).then_inc(s.att_ms, 1)
                    dve.wait_ge(s.att_ms, nth + 1)
                    v = st[:, 48:64]
                    root_guess(v, v, heads_newton[:, 0], heads_newton[:, 1]).then_inc(s.root_guessed, 1)
                if 1 <= t <= 9:
                    dve.wait_ge(s.gla_level, t)
                if t == 1:
                    nc.vector.tensor_copy(flat(g_cross), bank[:, 4, :]).then_inc(s.gla_taken, 1)
                elif 2 <= t <= 9:
                    lv = LEVELS if t == 9 else LEVELS - t + 1
                    mask = levels[:, lv:lv + 1, :].bitcast(I32).to_broadcast([P, 8, P])
                    nc.vector.copy_predicated(g_in.rearrange("p h a t -> p (h a) t"), mask,
                                              bank[:, 4:6, :].rearrange("p b (n t) -> p (b n) t", t=P)).then_inc(
                                                  s.gla_taken, 1)
            def att_out(a):
                dve.wait_ge(s.att_pv, AH * (a + 1))
                sums = st[:, 80 + AH * a:88 + AH * a]
                link(nc.vector.reciprocal(sums, sums))
                nc.vector.tensor_tensor(oa[:, a, :].rearrange("p (h c) -> p h c", c=AD),
                                        bank[:, 7, :].rearrange("p (h c) -> p h c", c=AD),
                                        sums.rearrange("p (h o) -> p h o", o=1).to_broadcast([P, AH, AD]),
                                        ALU.mult).then_inc(s.att_o, 1)

            def gate_half(f):
                lo(2 * M_GATE + 4 + f)
                if f % 4 == 3:
                    g = f // 4
                    c = C_GATE + g
                    dve.wait_ge(s.mm_done, 2 * M_GATE + f + 1)
                    nc.vector.tensor_tensor(gates[g // 2][:, g % 2 * 4:g % 2 * 4 + 4, :],
                                            pair(c).rearrange("p b (k t) -> p (b k) t", k=2),
                                            r_row.rearrange("p (o t) -> p o t", o=1).to_broadcast([P, 4, TOKENS]),
                                            ALU.mult).then_inc(acc_free[c % 2], 1)

            dve.wait_ge(s.dil_in, 16)
            for u in range(2 * AH):
                a = u // AH
                keys = AG * (a + 1) * P
                dve.wait_ge(s.att_scores, u + 1)
                if u >= 2:
                    dve.wait_ge(s.att_turnedp, u - 1 if u - 2 < AH else AH + 2 * (u - 2 - AH) + 2)
                src = bank[:, 4 + u % 2, 0:keys] if a == 0 else flat(bank[:, 4:6, :])[:, 0:keys]
                nc.vector.tensor_tensor(p[:, u % 2, 0:keys], src, dil[:, 3 * P * a:3 * P * a + keys],
                                        ALU.add).then_inc(s.att_masked, 1)
                dve.wait_ge(s.att_masked, u + 1)
                nc.vector.tensor_reduce(st[:, 32 + u:33 + u], p[:, u % 2, 0:keys], AX.X, ALU.max,
                                        negate=True).then_inc(s.att_max, 1)
                if u > 0:
                    gate_half(u - 1)
                if u == 2:
                    dve.wait_ge(s.gla_ssq, 1)
                    root_guess(st[:, 16:24], st[:, 16:24], heads_newton[:, 0, 0:8], heads_newton[:, 1, 0:8]).then_inc(
                        s.root_guessed, 1)
                if u == 9:
                    dve.wait_ge(s.root_found, 2 * AG + 2)
                    for c in (C_R, C_R + 1):
                        dve.wait_ge(acc_free[c % 2], c // 2 + 1)
                if 9 <= u < 13:
                    for at in (2 * u - 18, 2 * u - 17):
                        a, cols = at // GH, slice(at % GH * GV, at % GH * GV + GV)
                        ins = nc.vector.scalar_tensor_tensor(go[:, a, cols], go[:, a, cols], st[:, 16 + at:17 + at],
                                                             silu_r[:, a, cols], ALU.mult, ALU.mult)
                    if u == 12:
                        ins.then_inc(s.gla_ready, 1)
                if u == AH + 1:
                    att_out(0)
            gate_half(2 * AH - 1)
            att_out(1)
            turned_lo(a_lo, a_hi, 4, 4, s.go_hi, 0, lambda k: column("gla_out_norm_g_2", k % 2), s.go_lo)
            turned_lo(a_lo, a_hi, 0, 4, s.oa_hi, 0, lambda k: 1.0, s.oa_lo, (6, 7))
            turned_lo(a_lo, a_hi, 8, 4, s.go_hi, 2, lambda k: column("gla_out_norm_g_2", k % 2), s.go_lo)
            n = 2 * M_BR

            def mixed(q, mm):
                c = C_BR + q
                dve.wait_ge(s.mm_done, mm)
                for br in range(2):
                    ins = nc.vector.tensor_tensor(mix[:, br, q % 2, :], flat(gates[br][:, 2 * q:2 * q + 2, :]),
                                                  bank[:, 2 * (c % 2) + br, :], ALU.mult)
                ins.then_inc(acc_free[c % 2], 1)
                dve.wait_ge(acc_free[c % 2], c // 2 + 1)
                nc.vector.tensor_tensor(mix[:, 0, q % 2, :], mix[:, 0, q % 2, :], mix[:, 1, q % 2, :],
                                        ALU.add).then_inc(s.mix_ready, 1)
                dve.wait_ge(s.mix_hi, q + 1)
                nc.vector.tensor_tensor(flat(h_lo[:, 2 * q:2 * q + 2, :]), mix[:, 0, q % 2, :],
                                        flat(h_hi[:, 2 * q:2 * q + 2, :]).bitcast(F32), ALU.subtract).then_inc(s.mix_lo, 1)

            lo(n + 4, n + 5, n + 6, n + 7)
            dve.wait_ge(s.gate_done, 4)
            mixed(0, n + 4)
            lo(n + 8, n + 9)
            mixed(1, n + 6)
            lo(n + 10, n + 11, n + 12, n + 13)
            mixed(2, n + 10)
            lo(n + 14, n + 15)
            mixed(3, n + 12)
            lo(*range(n + 16, n + 20))
            add_chunk(C_OUT2, C_OUT2, 2 * M_OUT2 + 4)
            lo(n + 20, n + 21)
            add_tile(C_OUT2 + 1, C_OUT2, 0, 3, s.x_tiles)
            add_tile(C_OUT2 + 1, C_OUT2, 1, 2 * M_OUT2 + 8, s.acc_free0)
            turned_lo(h_lo, h_hi, 0, KT, s.h_hi_done, 12, lambda k: column("norm2_g_2", k), s.h_lo_done)
            lo(n + 22, n + 23)
            dve.wait_ge(s.ssq, 6)
            link(nc.vector.tensor_scalar(st[:, 2:4], st[:, 0:2], EPS, None, ALU.add))
            nc.vector.reciprocal(st[:, 2:4], st[:, 2:4])

            def ff2_chunk(j, e, split1, split2):
                dve.wait_ge(s.up_relu, j + 1)
                nc.vector.tensor_tensor(square2[:, e, :], relu2[:, e, :], relu2[:, e, :], ALU.mult).then_inc(
                    s.up_square, 1)
                split1()
                dve.wait_ge(s.up_hi, j + 1)
                nc.vector.tensor_tensor(flat(a_lo[:, 2 * e:2 * e + 2, :]), square2[:, e, :],
                                        flat(a_hi[:, 2 * e:2 * e + 2, :]).bitcast(F32), ALU.subtract).then_inc(
                                            s.up_lo, 1)
                split2()

            n3 = 2 * M_FF2
            ff2_chunk(0, 0, lambda: lo(n3 + 4, n3 + 5), lambda: None)
            with dve.Fori(0, CH2 // 3 - 1) as i:
                for e in range(3):
                    b = n3 + 4 * e
                    ff2_chunk(i * 3 + e + 1, (e + 1) % 3, lambda: lo(b + 6, b + 7, i=i), lambda: lo(b + 8, b + 9, i=i))
            for e in range(3):
                b = n3 + 12 * (CH2 // 3 - 1) + 4 * e
                ff2_chunk(CH2 - 3 + e, (e + 1) % 3, lambda: lo(b + 6, b + 7),
                          (lambda: lo(b + 8, b + 9)) if e < 2 else (lambda: None))
            add_down(4, 2 * M_END, s.x_added, [st[:, 2 + a:3 + a] for a in range(TT)])


def kernel(**inputs):
    import concourse.bacc as bacc
    from concourse.bass_utils import run_bass_kernel_spmd

    nc = bacc.Bacc("TRN2", target_bir_lowering=False, num_devices=1)
    arrays, aps = {}, {}
    vectors = {name: np.asarray(inputs[name]).reshape(-1) for name in VEC if name != "ones"}
    vectors["ones"] = np.ones(4 * P, np.float32)
    for name in ("attn_q_norm_g_2", "attn_k_norm_g_2"):
        vectors[name] = np.tile(vectors[name], 2)
    laid_out = {"positions": np.asarray(inputs["positions"]).reshape(TT, P).T,
                "vectors": np.concatenate([vectors[name].reshape(-1, P) for name in VEC]).T}
    for name in PARTS:
        a = np.ascontiguousarray(laid_out.get(name, inputs.get(name)))
        arrays[f"in_{name}"] = a
        aps[name] = nc.dram_tensor(f"in_{name}", a.shape, mybir.dt.from_np(a.dtype), kind="ExternalInput").ap()
    arrays["constants"] = constants()
    consts = nc.dram_tensor("constants", (P, C_END), F32, kind="ExternalInput").ap()
    out = nc.dram_tensor("out", (1, TOKENS, D), F32, kind="ExternalOutput").ap()
    two_blocks_kernel(nc, Parts(**aps), consts, out)
    result = run_bass_kernel_spmd(nc, [arrays], core_ids=[0])
    return result.results[0]["out"]
```
